# Optimizing a Trainium2 kernel written in Bass

```python
import math
import jax, jax.numpy as jnp
from jax import lax
import numpy as np

D_MODEL = 1024
BATCH = 1
SEQ = 2048
DEPTH = 1
DEC_BATCH = 1
DEC_SEQ = 256
PAST_LEN = 128

CONV_WIDTH = 512
CONV_GROUPS = 8
CONV_K = 3
DN_HEADS = 4
DN_DK = 128
DN_DV = 128
DN_QK = DN_HEADS * DN_DK
DN_V = DN_HEADS * DN_DV
DN_CONV_K = 3
DN_CHUNK = 64
MIX_WIDTH = CONV_WIDTH + DN_V
PROJ_WIDTH = 3 * CONV_WIDTH + 2 * DN_QK + DN_V + DN_V + 4 * DN_HEADS
N_GROUPS = 4
EXPERTS_PER_GROUP = 8
N_EXPERTS = N_GROUPS * EXPERTS_PER_GROUP
TOP_K = 2
EXPERT_FF = 512
MOE_BLOCK = 128
EPS = 1e-6

kernel_name = 'hymba_conv_gdn_hmoe_encoder'

def rmsnorm(x, g):
    xf = x.astype(jnp.float32)
    y = xf * lax.rsqrt(jnp.mean(xf * xf, axis=-1, keepdims=True) + EPS)
    return (y * g.astype(jnp.float32)).astype(x.dtype)

def l2norm(x):
    return x * lax.rsqrt(jnp.sum(x * x, axis=-1, keepdims=True) + EPS)

def depthwise_conv_centred(u, w):
    k, c = w.shape
    return lax.conv_general_dilated(
        u, w[:, None, :].astype(u.dtype), window_strides=(1,),
        padding=[((k - 1) // 2, k // 2)],
        dimension_numbers=('NWC', 'WIO', 'NWC'), feature_group_count=c)

def conv_mixer(bch, conv_w, norm_g):
    b_gate, c_gate, h = jnp.split(bch, 3, axis=-1)
    y = b_gate * depthwise_conv_centred(c_gate * h, conv_w)
    bn, t, _ = y.shape
    y = rmsnorm(y.reshape(bn, t, CONV_GROUPS, CONV_WIDTH // CONV_GROUPS),
                norm_g.reshape(CONV_GROUPS, CONV_WIDTH // CONV_GROUPS))
    return y.reshape(bn, t, CONV_WIDTH)

def chunk_gated_delta(q, k, v, g, beta):
    bn, t, h, dk = q.shape
    dv = v.shape[-1]
    c = DN_CHUNK
    n = t // c

    def chunks(a):
        a = a.reshape((bn, n, c, h) + a.shape[3:])
        return jnp.moveaxis(a, 3, 1)

    q, k, v, g, beta = chunks(q), chunks(k), chunks(v), chunks(g), chunks(beta)
    gc = jnp.cumsum(g, axis=-1)
    incl = jnp.tril(jnp.ones((c, c), dtype=bool))
    strict = jnp.tril(jnp.ones((c, c), dtype=bool), -1)
    decay = jnp.exp(jnp.where(incl, gc[..., :, None] - gc[..., None, :], -jnp.inf))
    kb = k * beta[..., None]
    lmat = jnp.where(strict, jnp.einsum('bhnid,bhnjd->bhnij', kb, k) * decay, 0.0)
    eye = jnp.eye(c, dtype=lmat.dtype)
    tinv = lax.linalg.triangular_solve(lmat + eye, jnp.broadcast_to(eye, lmat.shape),
                                       left_side=True, lower=True, unit_diagonal=True)
    w = jnp.einsum('bhnij,bhnjd->bhnid', tinv, kb * jnp.exp(gc)[..., None])
    u = jnp.einsum('bhnij,bhnjd->bhnid', tinv, v * beta[..., None])
    qk = jnp.einsum('bhnid,bhnjd->bhnij', q, k) * decay
    glast = gc[..., -1]
    q_dec = q * jnp.exp(gc)[..., None]
    k_dec = k * jnp.exp(glast[..., None] - gc)[..., None]

    def step(s, xs):
        qd, kd, wn, un, qkn, gl = xs
        v_new = un - jnp.einsum('bhid,bhde->bhie', wn, s)
        o = jnp.einsum('bhid,bhde->bhie', qd, s) + jnp.einsum('bhij,bhje->bhie', qkn, v_new)
        s = s * jnp.exp(gl)[..., None, None] + jnp.einsum('bhid,bhie->bhde', kd, v_new)
        return s, o

    xs = tuple(jnp.moveaxis(a, 2, 0) for a in (q_dec, k_dec, w, u, qk, glast))
    s0 = jnp.zeros((bn, h, dk, dv), jnp.float32)
    _, o = lax.scan(step, s0, xs)
    return jnp.transpose(o, (1, 0, 3, 2, 4)).reshape(bn, t, h, dv)

def deltanet_mixer(qkv, z, ab, conv_w, a_log, dt_bias, norm_g):
    bn, t, _ = qkv.shape
    out_dtype = qkv.dtype
    qkv = jax.nn.silu(depthwise_conv_centred(qkv, conv_w)).astype(jnp.float32)
    q, k, v = jnp.split(qkv, [DN_QK, 2 * DN_QK], axis=-1)
    q = l2norm(q.reshape(bn, t, DN_HEADS, DN_DK)) * (DN_DK ** -0.5)
    k = l2norm(k.reshape(bn, t, DN_HEADS, DN_DK))
    v = v.reshape(bn, t, DN_HEADS, DN_DV)
    ab = ab.astype(jnp.float32).reshape(bn, t, 4, DN_HEADS)
    a_log = a_log.astype(jnp.float32)
    dt_bias = dt_bias.astype(jnp.float32)
    g_f = -jnp.exp(a_log[0]) * jax.nn.softplus(ab[:, :, 0] + dt_bias[0])
    g_b = -jnp.exp(a_log[1]) * jax.nn.softplus(ab[:, :, 1] + dt_bias[1])
    beta_f = jax.nn.sigmoid(ab[:, :, 2])
    beta_b = jax.nn.sigmoid(ab[:, :, 3])
    o_f = chunk_gated_delta(q, k, v, g_f, beta_f)
    rev = lambda a: jnp.flip(a, axis=1)
    o_b = rev(chunk_gated_delta(rev(q), rev(k), rev(v), rev(g_b), rev(beta_b)))
    o = o_f + o_b
    o = o * lax.rsqrt(jnp.mean(o * o, axis=-1, keepdims=True) + EPS) * norm_g.astype(jnp.float32)
    o = o * jax.nn.silu(z.astype(jnp.float32).reshape(bn, t, DN_HEADS, DN_DV))
    return o.reshape(bn, t, DN_V).astype(out_dtype)

def hier_moe(x, rg_w, rg_b, re_w, re_b, w1, w3, w2):
    bn, t, d = x.shape
    xt = x.reshape(-1, d)
    n_tok = xt.shape[0]
    g_logits = (xt @ rg_w).astype(jnp.float32) + rg_b.astype(jnp.float32)
    g_prob = jax.nn.softmax(g_logits, axis=-1)
    g_w, g_idx = lax.top_k(g_prob, 1)
    e_logits = ((xt @ re_w).astype(jnp.float32) + re_b.astype(jnp.float32)).reshape(
        n_tok, N_GROUPS, EXPERTS_PER_GROUP)
    e_sel = jnp.take_along_axis(e_logits, g_idx[:, :, None], axis=1)[:, 0]
    e_prob = jax.nn.softmax(e_sel, axis=-1)
    top_p, top_i = lax.top_k(e_prob, TOP_K)
    gate = g_w * top_p / jnp.sum(top_p, axis=-1, keepdims=True)
    expert = (g_idx * EXPERTS_PER_GROUP + top_i).astype(jnp.int32)

    n_assign = n_tok * TOP_K
    flat_e = expert.reshape(-1)
    flat_tok = jnp.repeat(jnp.arange(n_tok, dtype=jnp.int32), TOP_K)
    flat_w = gate.reshape(-1)
    order = jnp.argsort(flat_e)
    se, stok, sw = flat_e[order], flat_tok[order], flat_w[order]
    counts = jnp.bincount(flat_e, length=N_EXPERTS).astype(jnp.int32)
    starts = jnp.cumsum(counts) - counts
    pcounts = (counts + (MOE_BLOCK - 1)) // MOE_BLOCK * MOE_BLOCK
    pends = jnp.cumsum(pcounts)
    pstarts = pends - pcounts
    dest = pstarts[se] + (jnp.arange(n_assign, dtype=jnp.int32) - starts[se])
    n_blk = (n_assign + N_EXPERTS * (MOE_BLOCK - 1) + MOE_BLOCK - 1) // MOE_BLOCK
    rows = n_blk * MOE_BLOCK
    xbuf = jnp.zeros((rows, d), x.dtype).at[dest].set(xt[stok])
    blk_start = jnp.arange(n_blk, dtype=jnp.int32) * MOE_BLOCK
    blk_e = jnp.minimum(jnp.searchsorted(pends, blk_start, side='right'), N_EXPERTS - 1)

    def expert_block(args):
        xb, e = args
        hdn = jax.nn.silu(xb @ w1[e]) * (xb @ w3[e])
        return hdn @ w2[e]

    ybuf = lax.map(expert_block, (xbuf.reshape(n_blk, MOE_BLOCK, d), blk_e)).reshape(rows, d)
    y_assign = ybuf[dest] * sw[:, None].astype(ybuf.dtype)
    y = jax.ops.segment_sum(y_assign, stok, num_segments=n_tok)
    return y.reshape(bn, t, d).astype(x.dtype)

def encoder_layer(x, norm1_g, w_in, conv_a_w, conv_a_norm_g, dn_conv_w, dn_a_log, dn_dt_bias,
                  dn_norm_g, w_o, norm2_g, rg_w, rg_b, re_w, re_b, w1, w3, w2):
    h = rmsnorm(x, norm1_g)
    proj = h @ w_in
    c0 = 3 * CONV_WIDTH
    c1 = c0 + 2 * DN_QK + DN_V
    c2 = c1 + DN_V
    bch, qkv, z, ab = proj[..., :c0], proj[..., c0:c1], proj[..., c1:c2], proj[..., c2:]
    y_a = conv_mixer(bch, conv_a_w, conv_a_norm_g)
    y_b = deltanet_mixer(qkv, z, ab, dn_conv_w, dn_a_log, dn_dt_bias, dn_norm_g)
    x = x + jnp.concatenate([y_a, y_b], axis=-1) @ w_o
    x = x + hier_moe(rmsnorm(x, norm2_g), rg_w, rg_b, re_w, re_b, w1, w3, w2)
    return x

def setup_inputs(seed: int = 0) -> dict:
    key = jax.random.key(seed)
    ks = jax.random.split(key, 24)
    f32 = jnp.float32
    nrm = lambda k, shape, scale: jax.random.normal(k, shape, f32) * scale
    gain = lambda k, shape: 1.0 + 0.02 * jax.random.normal(k, shape, f32)
    dt = jnp.exp(jax.random.uniform(ks[8], (DEPTH, 2, DN_HEADS), f32,
                                    math.log(1e-3), math.log(0.1)))
    return {
        'x_prompt': jax.random.normal(ks[0], (BATCH, SEQ, D_MODEL), f32),
        'x_sample': jax.random.normal(ks[1], (DEC_BATCH, DEC_SEQ, D_MODEL), f32),
        'norm1_g': gain(ks[2], (DEPTH, D_MODEL)),
        'w_in': nrm(ks[3], (DEPTH, D_MODEL, PROJ_WIDTH), D_MODEL ** -0.5),
        'conv_a_w': nrm(ks[4], (DEPTH, CONV_K, CONV_WIDTH), CONV_K ** -0.5),
        'conv_a_norm_g': gain(ks[5], (DEPTH, CONV_WIDTH)),
        'dn_conv_w': nrm(ks[6], (DEPTH, DN_CONV_K, 2 * DN_QK + DN_V), DN_CONV_K ** -0.5),
        'dn_a_log': jnp.log(jax.random.uniform(ks[7], (DEPTH, 2, DN_HEADS), f32, 1.0, 16.0)),
        'dn_dt_bias': dt + jnp.log(-jnp.expm1(-dt)),
        'dn_norm_g': gain(ks[9], (DEPTH, DN_DV)),
        'w_o': nrm(ks[10], (DEPTH, MIX_WIDTH, D_MODEL), MIX_WIDTH ** -0.5),
        'norm2_g': gain(ks[11], (DEPTH, D_MODEL)),
        'router_group_w': nrm(ks[12], (DEPTH, D_MODEL, N_GROUPS), D_MODEL ** -0.5),
        'router_group_b': nrm(ks[13], (DEPTH, N_GROUPS), 0.01),
        'router_expert_w': nrm(ks[14], (DEPTH, D_MODEL, N_EXPERTS), D_MODEL ** -0.5),
        'router_expert_b': nrm(ks[15], (DEPTH, N_EXPERTS), 0.01),
        'w1': nrm(ks[16], (DEPTH, N_EXPERTS, D_MODEL, EXPERT_FF), D_MODEL ** -0.5),
        'w3': nrm(ks[17], (DEPTH, N_EXPERTS, D_MODEL, EXPERT_FF), D_MODEL ** -0.5),
        'w2': nrm(ks[18], (DEPTH, N_EXPERTS, EXPERT_FF, D_MODEL), EXPERT_FF ** -0.5),
        'final_norm_g': gain(ks[19], (D_MODEL,)),
    }

def reference(x_prompt, x_sample, norm1_g, w_in, conv_a_w, conv_a_norm_g, dn_conv_w, dn_a_log,
              dn_dt_bias, dn_norm_g, w_o, norm2_g, router_group_w, router_group_b,
              router_expert_w, router_expert_b, w1, w3, w2, final_norm_g):
    def trunk(x):
        for l in range(DEPTH):
            x = encoder_layer(x, norm1_g[l], w_in[l], conv_a_w[l], conv_a_norm_g[l], dn_conv_w[l],
                              dn_a_log[l], dn_dt_bias[l], dn_norm_g[l], w_o[l], norm2_g[l],
                              router_group_w[l], router_group_b[l], router_expert_w[l],
                              router_expert_b[l], w1[l], w3[l], w2[l])
        return rmsnorm(x, final_norm_g)

    y_prompt = trunk(x_prompt)
    y_sample = trunk(x_sample)
    return (y_prompt, y_sample)


_drawn_inputs = setup_inputs


def setup_inputs(seed=0):
    import zlib

    import numpy as np

    out = dict(_drawn_inputs(seed))
    spreads = {}
    factors = {'dn_norm_g': 3.724,
     'router_group_b': 15.959,
     'router_expert_b': 18.223,
     'final_norm_g': 8.059,
     'conv_a_norm_g': 4.562,
     'norm2_g': 3.559}
    for name, (base, spread) in spreads.items():
        noise = np.random.default_rng([zlib.crc32(name.encode()), seed]).standard_normal(out[name].shape)
        drawn = base * np.exp(spread * noise) if base else spread * noise
        out[name] = __import__('jax').numpy.asarray(drawn.astype(out[name].dtype))
    for name, factor in factors.items():
        out[name] = (out[name] * factor).astype(out[name].dtype)
    return out
```

```python
from contextlib import ExitStack

import numpy as np

import concourse.bass as bass
from concourse import mybir

F32 = mybir.dt.float32
I32 = mybir.dt.int32
ALU = mybir.AluOpType
ACT = mybir.ActivationFunctionType
AX = mybir.AxisListType

P = 128
LONG, SHORT = 2048, 256
T = LONG + SHORT
NT = T // P
LT_TILES = LONG // P
D = 1024
KD = D // P
HEADS = 4
CONV_TILES = 4
EPS = 1e-6
PADW = T + 3
SEG = ((0, 1, LONG), (LONG, LONG + 2, SHORT))
NCH = 6
CH = T // NCH
JOBS = "chbqzkv"
NG, EPG, NE, FF = 4, 8, 32, 512
MAXB = (2 * T + NE * (P - 1)) // P
MAXB += MAXB % 2
SLOTS = MAXB * P
LEVELS = 7


def bcast(ap, n, axis):
    v = ap.unsqueeze(axis)
    shape = list(v.shape)
    shape[axis] = n
    return v.broadcast_to(shape)


class Bufs:

    def __init__(self, nc, ctx, phase=""):
        self.nc, self.ctx, self.phase = nc, ctx, phase

    def sb(self, name, shape, dt=F32):
        return self.ctx.enter_context(self.nc.sbuf_tensor(self.phase + name, shape, dt))

    def ps(self, name, shape):
        return self.ctx.enter_context(self.nc.psum_tensor(self.phase + name, shape, F32))

    def sem(self, name):
        return self.nc.alloc_semaphore(name=self.phase + name)


def pieces(c):
    out = []
    for t0, p0, n in SEG:
        a, b = max(c * CH, t0), min((c + 1) * CH, t0 + n)
        if a < b:
            out.append((a - c * CH, p0 + a - t0, b - a))
    return out


def constants(nc, k, dram):
    with ExitStack() as ctx:
        b = Bufs(nc, ctx, "constants_")
        set0, sel = b.sem("const_set"), b.sem("const_selected")
        small = b.sem("const_loaded")
        block = ctx.enter_context(nc.Block())

        @block.sync
        def _(sp):
            n = 0
            for dst, src in (
                (k["g1"][:, :], dram["norm1_g"].partition_broadcast(P)),
                (k["cw_mix"][:, :, :], dram["conv_a_w"]),
                (k["cg_mix"][:, :], dram["conv_a_norm_g"]),
                (k["cw_qkv"][:, :, :], dram["dn_conv_w"]),
                (k["alog"][:, :], dram["dn_a_log"].partition_broadcast(P)),
                (k["dtb"][:, :], dram["dn_dt_bias"].partition_broadcast(P)),
            ):
                sp.dma_start(dst, src).then_inc(small, 16)
                n += 16
            sp.wait_ge(small, n)

        @block.vector
        def _(dve):
            dve.memset(k["eps"][:, :], EPS)
            dve.memset(k["eps128"][:, :], EPS * P)
            dve.memset(k["one"][:, :], 1.0)

        @block.gpsimd
        def _(pool):
            fills = [(k["ident"], 0.0), (k["ones"], 1.0), (k["tri"], 1.0), (k["neg"], 0.0), (k["lower"], 1.0)]
            for buf, v in fills:
                pool.memset(buf[:], v).then_inc(set0, 1)
            n = len(fills)
            pool.memset(k["group"][:, :], 1.0).then_inc(set0, 1)
            pool.memset(k["lvl"][:, :, :, :], 0.0).then_inc(set0, 1)
            pool.wait_ge(set0, n + 2)
            halves = k["group"][:, :].rearrange("p (b r) -> p b r", b=2)
            pool.affine_select(out=halves, in_=halves, compare_op=ALU.is_ge, fill=0.0, base=0,
                               pattern=[[-64, 2], [0, 64]], channel_multiplier=1).then_inc(sel, 1)
            pool.wait_ge(sel, 1)
            pool.affine_select(out=halves, in_=halves, compare_op=ALU.is_ge, fill=0.0, base=63,
                               pattern=[[64, 2], [0, 64]], channel_multiplier=-1)
            m = 0
            for l in range(LEVELS):
                s = 1 << l
                for d in range(2):
                    v = k["lvl"][:, d, l, :].rearrange("p (b h r) -> p b h r", h=2, r=s)[:, :, 1 - d, :]
                    pool.memset(v, 1.0).then_inc(set0, 1)
                    m += 1
            pool.wait_ge(set0, n + 2 + m)
            for l in range(LEVELS):
                s = 1 << l
                for d in range(2):
                    v = k["lvl"][:, d, l, :].rearrange("p (b h r) -> p b h r", h=2, r=s)[:, :, 1 - d, :]
                    pool.affine_select(out=v, in_=v, compare_op=ALU.is_ge, fill=0.0, base=-s * d,
                                       pattern=[[-2 * s, P // (2 * s)], [0, s]], channel_multiplier=1).then_inc(sel, 1)
            pool.wait_ge(sel, 2 * LEVELS + 1)
            for l in range(LEVELS):
                s = 1 << l
                for d in range(2):
                    v = k["lvl"][:, d, l, :].rearrange("p (b h r) -> p b h r", h=2, r=s)[:, :, 1 - d, :]
                    pool.affine_select(out=v, in_=v, compare_op=ALU.is_ge, fill=0.0, base=s * d + s - 1,
                                       pattern=[[2 * s, P // (2 * s)], [0, s]], channel_multiplier=-1)
            pool.affine_select(out=k["ident"][:, :], in_=k["ident"][:, :], compare_op=ALU.not_equal, fill=1.0,
                               base=0, pattern=[[-1, P]], channel_multiplier=1)
            for buf, fill in ((k["tri"], 0.0), (k["neg"], -1e30)):
                for d, sign in ((0, 1), (1, -1)):
                    pool.affine_select(out=buf[:, d, :], in_=buf[:, d, :], compare_op=ALU.is_ge, fill=fill,
                                       base=0, pattern=[[sign, P]], channel_multiplier=-sign)
            pool.affine_select(out=k["lower"][:, :], in_=k["lower"][:, :], compare_op=ALU.is_gt, fill=0.0,
                               base=0, pattern=[[1, P]], channel_multiplier=-1)


def normalise(nc, k, dram, hT):
    with ExitStack() as ctx:
        b = Bufs(nc, ctx, "normalise_")
        x = [b.sb(f"x{p}", [P, D]) for p in range(2)]
        xn = [b.sb(f"xn{p}", [P, D]) for p in range(2)]
        sq = b.sb("sq_junk", [P, D])
        ss = [b.sb(f"ss{p}", [P, 1]) for p in range(2)]
        rt = [b.sb(f"rt{p}", [P, 1]) for p in range(2)]
        ri = [b.sb(f"ri{p}", [P, 1]) for p in range(2)]
        tp = [b.ps(f"tp{n}", [P, 4, P]) for n in range(4)]
        loaded = [b.sem(f"x_loaded{p}") for p in range(2)]
        x_free, xn_free = b.sem("x_free"), b.sem("xn_free")
        summed, rooted, inverted, scaled = b.sem("x_summed"), b.sem("x_rooted"), b.sem("x_inverted"), b.sem("x_scaled")
        turned, copied = b.sem("x_turned"), [b.sem("x_copied0"), b.sem("x_copied1")]
        block = ctx.enter_context(nc.Block())

        @block.sync
        def _(sp):
            for p in range(2):
                sp.dma_start(x[p][:, :], dram["x"][p * P:(p + 1) * P, :]).then_inc(loaded[p], 16)
            with sp.Fori(1, NT // 2) as pair:
                i = pair * 2
                for p in range(2):
                    sp.wait_ge(x_free, i + (p - 1))
                    sp.dma_start(x[p][:, :], dram["x"][bass.ds((i + p) * P, P), :]).then_inc(loaded[p], 16)

        @block.scalar
        def _(act):
            with act.Fori(0, NT // 2) as pair:
                i = pair * 2
                for p in range(2):
                    act.wait_ge(loaded[p], i * 8 + 16)
                    act.activation(sq[:, :], x[p][:, :], ACT.Square, accum_out=ss[p][:, :]).then_inc(summed, 1)
                    act.wait_ge(summed, i + (p + 1))
                    act.activation(rt[p][:, :], ss[p][:, :], ACT.Sqrt, bias=k["eps"][:, :], scale=1.0 / D).then_inc(rooted, 1)
                    act.wait_ge(turned, i * 2 + (2 * p + 2))
                    act.activation(hT[:, 4:8, bass.ds((i + p) * P, P)], tp[2 * p + 1][:, :, :], ACT.Copy).then_inc(copied[1], 1)

        @block.vector
        def _(dve):
            with dve.Fori(0, NT // 2) as pair:
                i = pair * 2
                for p in range(2):
                    dve.wait_ge(rooted, i + (p + 1))
                    dve.reciprocal(ri[p][:, :], rt[p][:, :]).then_inc(inverted, 1)
                    dve.wait_ge(inverted, i + (p + 1))
                    dve.scalar_tensor_tensor(out=xn[p][:, :], in0=x[p][:, :], scalar=ri[p][:, :], in1=k["g1"][:, :],
                                             op0=ALU.mult, op1=ALU.mult).then_inc(scaled, 1)
                    dve.wait_ge(scaled, i + (p + 1))
                    dve.nop().then_inc(x_free, 1)
                    dve.wait_ge(turned, i * 2 + (2 * p + 1))
                    dve.tensor_copy(hT[:, 0:4, bass.ds((i + p) * P, P)], tp[2 * p][:, :, :]).then_inc(copied[0], 1)

        @block.tensor
        def _(pe):
            def tile(p, i, ready, banks):
                pe.wait_ge(scaled, ready)
                for h in range(2):
                    if banks is not None:
                        pe.wait_ge(copied[h], banks)
                    for j in range(4):
                        m = pe.transpose(tp[2 * p + h][:, j, :], xn[p][:, (4 * h + j) * P:(4 * h + j + 1) * P], k["ident"][:, :])
                    m.then_inc(turned, 1)
            for p in range(2):
                tile(p, p, p + 1, None)
            with pe.Fori(1, NT // 2) as pair:
                i = pair * 2
                for p in range(2):
                    tile(p, i, i + (p + 1), i + (p - 1))


def project(nc, k, dram, hT, feat, ab_rows):
    with ExitStack() as ctx:
        b = Bufs(nc, ctx, "project_")
        w = {j: b.sb(f"w_{j}", [P, KD, P]) for j in JOBS}
        gate_c, mix_in, mix = b.sb("gate_c", [P, T]), b.sb("mix_in", [P, PADW]), b.sb("mix", [P, PADW])
        raw = {"q": b.sb("raw_q", [P, PADW]), "k": b.sb("raw_k", [P, PADW])}
        raw["v"] = raw["q"]
        out = {"q": b.sb("conv_q", [P, PADW]), "k": b.sb("conv_k", [P, PADW]), "b": mix}
        out["v"] = out["q"]
        primer = b.sb("primer", [P, 5, CONV_TILES])
        sq, nrm = b.sb("squares", [P, PADW]), b.sb("norms", [P, PADW])
        bank = [b.ps(f"proj{c}", [P, 512]) for c in range(NCH)]
        nbank = [b.ps(f"nsum{c}", [P, 512]) for c in range(2)]
        w_loaded = {j: b.sem(f"w_loaded_{j}") for j in JOBS}
        ready = [b.sem(f"proj_ready{c}") for c in range(NCH)]
        free = [b.sem(f"proj_free{c}") for c in range(NCH)]
        nready = [b.sem(f"nsum_ready{c}") for c in range(2)]
        nfree = [b.sem(f"nsum_free{c}") for c in range(2)]
        padded, ab_ready = b.sem("pads_set"), b.sem("ab_ready")
        conv_done = {j: b.sem(f"conv_done_{j}") for j in "hqkv"}
        act_done = {j: b.sem(f"silu_done_{j}") for j in "qkv"}
        chain = b.sem("conv_taps")
        sq_done = {j: b.sem(f"squares_done_{j}") for j in "bqk"}
        inv_done = {j: b.sem(f"inverse_done_{j}") for j in "bqk"}
        norm_done = {j: b.sem(f"norm_done_{j}") for j in "bqk"}
        stored = {j: b.sem(f"stored_{j}") for j in "bqzkv"}
        block = ctx.enter_context(nc.Block())
        G = CONV_TILES
        body = slice(1, PADW - 1)

        def evacuated(eng, n, g):
            eng.wait_ge(free[NCH - 1], g * 7 + (n + 2))

        def rooted(eng, n, g):
            eng.wait_ge(nfree[1], g * 9 + (3 * n + 4))

        @block.sync
        def _(sp):
            for n, j in enumerate(JOBS):
                sp.dma_start(w[j][:, :, :], dram["w_tiles"][n]).then_inc(w_loaded[j], 16)
            with sp.Fori(1, G) as g:
                for n, j in enumerate(JOBS):
                    sp.wait_ge(ready[NCH - 1], g * 7 + (n + 1 - 7))
                    src = dram["w_tiles"][bass.ds(g * 7 + n, 1)].rearrange("a p k m -> (a p) k m")
                    sp.dma_start(w[j][:, :, :], src).then_inc(w_loaded[j], 16)
            sp.wait_ge(ready[NCH - 1], 7 * G - 6)
            sp.dma_start(w["c"][:, :, 0:16], dram["w_ab"]).then_inc(w_loaded["c"], 16)

        @block.tensor
        def _(pe):
            def job(n, j, g):
                pe.wait_ge(w_loaded[j], g * 16 + 16)
                for c in range(NCH):
                    pe.wait_ge(free[c], g * 7 + (n + 1))
                    for kt in range(KD):
                        m = pe.matmul(bank[c][:, 0:CH], w[j][:, kt, :], hT[:, kt, c * CH:(c + 1) * CH],
                                      start=kt == 0, stop=kt == KD - 1)
                    m.then_inc(ready[c], 1)

            def sums(n, j, g, weights):
                pe.wait_ge(sq_done[j], g + 1)
                for c in range(NCH):
                    pe.wait_ge(nfree[c % 2], g * 9 + (3 * n + c // 2 + 1))
                    for a, at, ln in pieces(c):
                        m = pe.matmul(nbank[c % 2][:, a:a + ln], weights, sq[:, at:at + ln], start=a == 0, stop=True,
                                      skip_group_check=True)
                    m.then_inc(nready[c % 2], 1)

            with pe.Fori(0, G) as g:
                job(0, "c", g)
                job(1, "h", g)
                job(2, "b", g)
                job(3, "q", g)
                sums(0, "b", g, k["group"][:, :])
                job(4, "z", g)
                sums(1, "q", g, k["ones"][:, :])
                job(5, "k", g)
                job(6, "v", g)
                sums(2, "k", g, k["ones"][:, :])
            pe.wait_ge(w_loaded["c"], 16 * (G + 1))
            for c in range(NCH):
                pe.wait_ge(free[c], 7 * G + 1)
                for kt in range(KD):
                    m = pe.matmul(bank[c][0:16, 0:CH], w["c"][:, kt, 0:16], hT[:, kt, c * CH:(c + 1) * CH],
                                  start=kt == 0, stop=kt == KD - 1)
                m.then_inc(ready[c], 1)

        @block.scalar
        def _(act):
            def evacuate(n, j, g, dst, func, pad):
                for c in range(NCH):
                    act.wait_ge(ready[c], g * 7 + (n + 1))
                    for a, at, ln in pieces(c):
                        at = at if pad else c * CH + a
                        m = act.activation(dst[:, at:at + ln], bank[c][:, a:a + ln], func)
                    m.then_inc(free[c], 1)

            def square(j, src):
                act.activation(sq[:, body], src[:, body], ACT.Square).then_inc(sq_done[j], 1)

            def roots(n, g, scale, bias):
                for c in range(NCH):
                    act.wait_ge(nready[c % 2], g * 9 + (3 * n + c // 2 + 1))
                    for a, at, ln in pieces(c):
                        m = act.activation(nrm[:, at:at + ln], nbank[c % 2][:, a:a + ln], ACT.Sqrt, bias=bias, scale=scale)
                    m.then_inc(nfree[c % 2], 1)

            def silu(j):
                act.activation(out[j][:, body], out[j][:, body], ACT.Silu).then_inc(act_done[j], 1)

            act.wait_ge(padded, 4)
            with act.Fori(0, G) as g:
                act.wait_ge(stored["z"], g * 16 + 16)
                evacuate(0, "c", g, gate_c, ACT.Copy, False)
                evacuated(act, 2, g)
                square("b", mix)
                act.wait_ge(conv_done["v"], g + 1)
                evacuate(3, "q", g, raw["q"], ACT.Copy, True)
                roots(0, g, 1.0 / 64, k["eps"][:, :])
                act.wait_ge(conv_done["q"], g + 1)
                silu("q")
                act.wait_ge(act_done["q"], g + 1)
                square("q", out["q"])
                evacuate(4, "z", g, gate_c, ACT.Silu, False)
                act.wait_ge(norm_done["b"], g + 1)
                roots(1, g, float(P), k["eps128"][:, :])
                act.wait_ge(conv_done["k"], g + 1)
                evacuate(5, "k", g, raw["k"], ACT.Copy, True)
                act.wait_ge(conv_done["k"], g + 2)
                silu("k")
                act.wait_ge(act_done["k"], g + 1)
                square("k", out["k"])
                evacuate(6, "v", g, raw["v"], ACT.Copy, True)
                act.wait_ge(norm_done["q"], g + 1)
                roots(2, g, 1.0, k["eps"][:, :])
                act.wait_ge(conv_done["v"], g + 2)
                silu("v")
                act.wait_ge(norm_done["k"], g + 1)
            act.wait_ge(stored["z"], 16 * G + 16)
            for c in range(NCH):
                act.wait_ge(ready[c], 7 * G + 1)
                m = act.activation(gate_c[0:16, c * CH:(c + 1) * CH], bank[c][0:16, 0:CH], ACT.Copy)
            m.then_inc(ab_ready, 1)

        def silu_k_after(act, g, silu, square):
            act.wait_ge(conv_done["k"], g + 2)
            act.activation(out["k"][:, body], out["k"][:, body], ACT.Silu).then_inc(act_done["k"], 1)
            square("k", g, out["k"], act_done["k"], g + 1)

        @block.vector
        def _(dve):
            for buf in (mix_in, raw["q"], raw["k"], nrm):
                dve.memset(buf[:, :], 0.0 if buf is not nrm else 1.0).then_inc(padded, 1)
            dve.wait_ge(padded, 4)
            for sem in free + nfree + [conv_done["k"], conv_done["v"]]:
                dve.sem_inc(sem, 1)

            def conv(j, g, src, dst, wts, n):
                dve.tensor_scalar(dst[:, body], src[:, 0:PADW - 2], wts[0], None, ALU.mult).then_inc(chain, 1)
                dve.wait_ge(chain, g * 8 + (2 * n + 1))
                dve.scalar_tensor_tensor(out=dst[:, body], in0=src[:, 1:PADW - 1], scalar=wts[1], in1=dst[:, body],
                                         op0=ALU.mult, op1=ALU.add).then_inc(chain, 1)
                dve.wait_ge(chain, g * 8 + (2 * n + 2))
                dve.scalar_tensor_tensor(out=dst[:, body], in0=src[:, 2:PADW], scalar=wts[2], in1=dst[:, body],
                                         op0=ALU.mult, op1=ALU.add).then_inc(conv_done[j], 1)

            def norm(n, j, g, gain):
                rooted(dve, n, g)
                dve.reciprocal(nrm[:, body], nrm[:, body]).then_inc(inv_done[j], 1)
                dve.wait_ge(inv_done[j], g + 1)
                if gain is None:
                    m = dve.tensor_tensor(out[j][:, body], out[j][:, body], nrm[:, body], ALU.mult)
                else:
                    m = dve.scalar_tensor_tensor(out=out[j][:, body], in0=out[j][:, body], scalar=gain, in1=nrm[:, body],
                                                 op0=ALU.mult, op1=ALU.mult)
                m.then_inc(norm_done[j], 1)

            def taps(table, at):
                return [table[:, bass.ds(at, 1), n:n + 1].rearrange("p a b -> p (a b)") for n in range(3)]

            with dve.Fori(0, G) as g:
                evacuated(dve, 0, g)
                for c in range(NCH):
                    dve.wait_ge(ready[c], g * 7 + 2)
                    for a, at, ln in pieces(c):
                        m = dve.tensor_tensor(mix_in[:, at:at + ln], bank[c][:, a:a + ln],
                                              gate_c[:, c * CH + a:c * CH + a + ln], ALU.mult)
                    m.then_inc(free[c], 1)
                evacuated(dve, 1, g)
                dve.wait_ge(stored["b"], g * 32 + 32)
                conv("h", g, mix_in, mix, taps(k["cw_mix"], g), 0)
                dve.wait_ge(conv_done["h"], g + 1)
                for c in range(NCH):
                    dve.wait_ge(ready[c], g * 7 + 3)
                    for a, at, ln in pieces(c):
                        m = dve.tensor_tensor(mix[:, at:at + ln], bank[c][:, a:a + ln], mix[:, at:at + ln], ALU.mult)
                    m.then_inc(free[c], 1)
                evacuated(dve, 3, g)
                dve.wait_ge(stored["v"], g * 32 + 32)
                conv("q", g, raw["q"], out["q"], taps(k["cw_qkv"], g), 1)
                norm(0, "b", g, k["cg_mix"][:, bass.ds(g, 1)])
                norm(1, "q", g, None)
                evacuated(dve, 5, g)
                dve.wait_ge(stored["k"], g * 32 + 32)
                conv("k", g, raw["k"], out["k"], taps(k["cw_qkv"], g + HEADS), 2)
                evacuated(dve, 6, g)
                dve.wait_ge(stored["q"], g * 32 + 64)
                conv("v", g, raw["v"], out["v"], taps(k["cw_qkv"], g + 2 * HEADS), 3)
                norm(2, "k", g, None)

        @block.gpsimd
        def _(pool):
            def store(j, row, src):
                dst = feat[bass.ds(row, 1)].rearrange("a p t -> (a p) t")
                for t0, p0, n in SEG:
                    pool.dma_start(dst[:, t0:t0 + n], src[:, p0:p0 + n]).then_inc(stored[j], 16)

            for j in "bqzkv":
                for _ in range(1 if j == "z" else 2):
                    pool.dma_start(primer[:, "bqzkv".index(j), :], dram["conv_a_norm_g"]).then_inc(stored[j], 16)
                    pool.wait_ge(stored[j], 16)
            with pool.Fori(0, G) as g:
                pool.wait_ge(norm_done["b"], g + 1)
                store("b", g + 16, mix)
                evacuated(pool, 4, g)
                pool.dma_start(feat[bass.ds(g + 12, 1)].rearrange("a p t -> (a p) t"), gate_c[:, :]).then_inc(stored["z"], 16)
                pool.wait_ge(norm_done["q"], g + 1)
                store("q", g, out["q"])
                pool.wait_ge(act_done["v"], g + 1)
                store("v", g + 8, out["v"])
                pool.wait_ge(norm_done["k"], g + 1)
                store("k", g + 4, out["k"])
            pool.wait_ge(ab_ready, 1)
            pool.dma_start(ab_rows, gate_c[0:16, :]).then_inc(stored["z"], 16)
            pool.wait_ge(stored["z"], 16 * G + 32)
            for j in "bqkv":
                pool.wait_ge(stored[j], 32 * G + 32)


def decays(nc, k, ab_rows, gates):
    with ExitStack() as ctx:
        b = Bufs(nc, ctx, "decays_")
        abT, ab = b.sb("abT", [16, T]), b.sb("ab", [P, NT, 4 * HEADS])
        loaded = b.sem("ab_loaded")
        x, nx = b.sb("ab_x", [P, NT, 8]), b.sb("ab_nx", [P, NT, 8])
        ex, lg = b.sb("ab_exp", [P, NT, 8]), b.sb("ab_log", [P, NT, 8])
        eb, eb1, rate = b.sb("ab_eb", [P, NT, 8]), b.sb("ab_eb1", [P, NT, 8]), b.sb("rate", [P, 8])
        gg = b.sb("ab_g", [P, 2, NT, HEADS])
        tail = b.sb("ab_tail", [P, 2, NT, HEADS])
        pab = b.ps("pab", [P, NT * 4 * HEADS])
        pg = [b.ps(f"pg{d}", [P, 2, NT, HEADS]) for d in range(2)]
        turned, dv, ac, g_done, sums = b.sem("ab_turned"), b.sem("ab_vector"), b.sem("ab_scalar"), b.sem("ab_g_done"), b.sem("ab_sums")
        block = ctx.enter_context(nc.Block())

        @block.sync
        def _(sp):
            sp.dma_start(abT[:, :], ab_rows).then_inc(loaded, 16)

        @block.tensor
        def _(pe):
            pe.wait_ge(loaded, 16)
            for t in range(NT):
                m = pe.transpose(pab[:, t * 16:(t + 1) * 16], abT[0:16, t * P:(t + 1) * P], k["ident"][0:16, 0:16])
            m.then_inc(turned, 1)
            pe.wait_ge(g_done, 2)
            for d in range(2):
                pe.matmul(pg[d][:, 0], k["tri"][:, d, :], gg[:, d], start=True, stop=True, skip_group_check=True)
                m = pe.matmul(pg[d][:, 1], k["ones"][:, :], gg[:, d], start=False, stop=True, skip_group_check=True)
            m.then_inc(sums, 1)

        @block.vector
        def _(dve):
            n = [0]

            def link(m):
                n[0] += 1
                m.then_inc(dv, 1)
                dve.wait_ge(dv, n[0])

            dve.wait_ge(turned, 1)
            link(dve.tensor_copy(ab[:, :, :], pab[:, :].rearrange("p (t c) -> p t c", c=16)))
            link(dve.tensor_tensor(x[:, :, :], ab[:, :, 0:8], bcast(k["dtb"][:, :], NT, 1), ALU.add))
            link(dve.tensor_scalar(nx[:, :, :], x[:, :, :], -1.0, None, ALU.mult))
            link(dve.tensor_tensor(nx[:, :, :], nx[:, :, :], x[:, :, :], ALU.min))
            dve.wait_ge(ac, 4)
            link(dve.scalar_tensor_tensor(out=x[:, :, :], in0=x[:, :, :], scalar=0.0, in1=lg[:, :, :], op0=ALU.max, op1=ALU.add))
            for d in range(2):
                dve.scalar_tensor_tensor(out=gg[:, d], in0=x[:, :, 4 * d:4 * d + 4], scalar=-1.0,
                                         in1=bcast(rate[:, 4 * d:4 * d + 4], NT, 1), op0=ALU.mult, op1=ALU.mult).then_inc(g_done, 1)
            dve.wait_ge(g_done, 2)
            link(dve.tensor_scalar(eb1[:, :, :], eb[:, :, :], 1.0, None, ALU.add))
            for d in range(2):
                dve.tensor_copy(gates[:, d, :, 16:20], gg[:, d])
                dve.reciprocal(gates[:, d, :, 4:8], eb1[:, :, 4 * d:4 * d + 4])
            dve.wait_ge(sums, 1)
            for d in range(2):
                link(dve.tensor_copy(gates[:, d, :, 0:4], pg[d][:, 0]))
                link(dve.tensor_tensor(tail[:, d], pg[d][:, 1], gates[:, d, :, 0:4], ALU.subtract))

        @block.scalar
        def _(act):
            act.activation(rate[:, :], k["alog"][:, :], ACT.Exp).then_inc(ac, 1)
            act.wait_ge(dv, 4)
            act.activation(ex[:, :, :], nx[:, :, :], ACT.Exp).then_inc(ac, 1)
            act.activation(eb[:, :, :], ab[:, :, 8:16], ACT.Exp, scale=-1.0).then_inc(ac, 1)
            act.wait_ge(ac, 3)
            act.activation(lg[:, :, :], ex[:, :, :], ACT.Ln, bias=k["one"][:, :]).then_inc(ac, 1)
            act.wait_ge(dv, 10)
            for d in range(2):
                act.activation(gates[:, d, :, 8:12], tail[:, d], ACT.Exp)
                act.activation(gates[:, d, :, 12:16], pg[d][:, 1], ACT.Exp)


def delta(nc, k, gates, feat, O):
    with ExitStack() as ctx:
        b = Bufs(nc, ctx, "delta_")
        names = "dg eg diff dec lt keT qdT kdec vtok qkT R Tm X rv vn S".split()
        L = []
        for d in range(2):
            v = {n: b.sb(f"{n}{d}", [P, HEADS, P]) for n in names}
            v["in"] = b.sb(f"qkv{d}", [P, 3 * HEADS, P])
            v["gs"] = b.sb(f"gs{d}", [P, 20])
            v["M"] = b.sb(f"M{d}", [P, LEVELS, HEADS, P])
            v["P"] = [b.ps(f"dp{d}{n}", [P, HEADS, P]) for n in range(4)]
            L.append(v)
        sems = ("loaded gates_set gsum_in gsum kk qk kturned vturned eg_set diff_set masked dec_set lt_set qkT_set keT_set "
                "qdT_set M_set kdec_set vtok_set R_set Tturned T_set X_ready X_set dR_ready kS_ready rv_set Tv_ready vn_set "
                "o_ready o_added kv_ready S_set").split()
        E = [{n: b.sem(f"{n}{d}") for n in sems} for d in range(2)]
        cleared = b.sem("o_cleared")
        runs = ((0, LT_TILES, 0, 0), (LT_TILES, NT - LT_TILES, LT_TILES, 1))
        block = ctx.enter_context(nc.Block())

        def tile(d, s, first, n):
            return s + first if d == 0 else s * -1 + (first + n - 1)

        @block.sync
        def _(sp):
            for base, n, first, r in runs:
                with sp.Fori(0, n) as s:
                    for d in range(2):
                        v, e = L[d], E[d]
                        sp.wait_ge(e["qdT_set"], s + (base + 1))
                        sp.wait_ge(e["vturned"], s + (base + 1))
                        sp.dma_start(v["in"][:, :, :], feat[0:3 * HEADS, :, bass.ds(tile(d, s, first, n) * P, P)]
                                     .rearrange("c p t -> p c t")).then_inc(e["loaded"], 16)

        @block.gpsimd
        def _(pool):
            for d in range(2):
                pool.sem_inc(E[d]["qdT_set"], 1)
                pool.sem_inc(E[d]["vturned"], 1)
            for base, n, first, r in runs:
                with pool.Fori(0, n) as s:
                    for d in range(2):
                        v, e = L[d], E[d]
                        pool.wait_ge(e["gates_set"], s + (base + 1))
                        pool.tensor_tensor(v["dg"][:, :, :], bcast(k["tri"][:, d, :], HEADS, 1), bcast(v["gs"][:, 16:20], P, 2),
                                           ALU.mult).then_inc(e["gsum_in"], 1)
                    for d in range(2):
                        v, e = L[d], E[d]
                        pool.wait_ge(e["diff_set"], s + (base + 1))
                        pool.tensor_tensor(v["diff"][:, :, :], v["diff"][:, :, :], bcast(k["neg"][:, d, :], HEADS, 1),
                                           ALU.add).then_inc(e["masked"], 1)
                    for l in range(LEVELS):
                        for d in range(2):
                            v, e = L[d], E[d]
                            pool.wait_ge(e["lt_set"], s + (base + 1))
                            pool.tensor_tensor(v["M"][:, l], v["lt"][:, :, :], bcast(k["lvl"][:, d, l, :], HEADS, 1),
                                               ALU.mult).then_inc(e["M_set"], 1)
                    for d in range(2):
                        v, e = L[d], E[d]
                        pool.wait_ge(e["eg_set"], s + (base + 1))
                        pool.tensor_tensor(v["keT"][:, :, :], v["in"][:, HEADS:2 * HEADS, :], v["eg"][:, :, :], ALU.mult).then_inc(e["keT_set"], 1)
                        pool.tensor_tensor(v["qdT"][:, :, :], v["in"][:, 0:HEADS, :], v["eg"][:, :, :], ALU.mult).then_inc(e["qdT_set"], 1)

        @block.scalar
        def _(act):
            for base, n, first, r in runs:
                with act.Fori(0, n) as s:
                    one = s + (base + 1)
                    for d in range(2):
                        v, e = L[d], E[d]
                        act.wait_ge(e["gsum"], one)
                        act.activation(v["eg"][:, :, :], v["P"][0][:, :, :], ACT.Exp).then_inc(e["eg_set"], 1)
                    for d in range(2):
                        v, e = L[d], E[d]
                        act.wait_ge(e["masked"], one)
                        act.activation(v["dec"][:, :, :], v["diff"][:, :, :], ACT.Exp).then_inc(e["dec_set"], 1)
                    for d in range(2):
                        v, e = L[d], E[d]
                        act.wait_ge(e["vturned"], s + (base + 2))
                        act.activation(v["vtok"][:, :, :], v["P"][3][:, :, :], ACT.Copy).then_inc(e["vtok_set"], 1)
                    for l in range(LEVELS - 1):
                        for d in range(2):
                            v, e = L[d], E[d]
                            act.wait_ge(e["Tturned"], s * 6 + (6 * base + l + 1))
                            act.activation(v["Tm"][:, :, :], v["P"][0][:, :, :], ACT.Copy).then_inc(e["T_set"], 1)
                        for d in range(2):
                            v, e = L[d], E[d]
                            act.wait_ge(e["X_ready"], s * 6 + (6 * base + l + 1))
                            act.activation(v["X"][:, :, :], v["P"][1][:, :, :], ACT.Copy).then_inc(e["X_set"], 1)

        @block.tensor
        def _(pe):
            for base, n, first, r in runs:
                with pe.Fori(0, n) as s:
                    one = s + (base + 1)
                    six = s * 6
                    for d in range(2):
                        v, e = L[d], E[d]
                        B = v["P"]
                        pe.wait_ge(e["S_set"], s + (base + 1 + r))
                        pe.wait_ge(e["gsum_in"], one)
                        pe.matmul(B[0][:, :, :], k["ones"][:, :], v["dg"][:, :, :], start=True, stop=True).then_inc(e["gsum"], 1)
                        pe.wait_ge(e["loaded"], s * 16 + (16 * base + 16))
                        for h in range(HEADS):
                            m = pe.matmul(B[1][:, h], v["in"][:, HEADS + h, :], v["in"][:, HEADS + h, :], start=h == 0, stop=True, skip_group_check=True)
                        m.then_inc(e["kk"], 1)
                        for h in range(HEADS):
                            m = pe.matmul(B[2][:, h], v["in"][:, HEADS + h, :], v["in"][:, h, :], start=h == 0, stop=True, skip_group_check=True)
                        m.then_inc(e["qk"], 1)
                        for h in range(HEADS):
                            m = pe.transpose(B[3][:, h], v["in"][:, HEADS + h, :], k["ident"][:, :])
                        m.then_inc(e["kturned"], 1)
                    for d in range(2):
                        v, e = L[d], E[d]
                        B = v["P"]
                        pe.wait_ge(e["kdec_set"], one)
                        for h in range(HEADS):
                            m = pe.transpose(B[3][:, h], v["in"][:, 2 * HEADS + h, :], k["ident"][:, :])
                        m.then_inc(e["vturned"], 1)
                    for l in range(1, LEVELS):
                        for d in range(2):
                            v, e = L[d], E[d]
                            pe.wait_ge(e["R_set"], s * 7 + (7 * base + l))
                            for h in range(HEADS):
                                m = pe.transpose(v["P"][0][:, h], v["R"][:, h, :], k["ident"][:, :])
                            m.then_inc(e["Tturned"], 1)
                        for d in range(2):
                            v, e = L[d], E[d]
                            pe.wait_ge(e["T_set"], six + (6 * base + l))
                            pe.wait_ge(e["M_set"], s * 7 + (7 * base + l + 1))
                            for h in range(HEADS):
                                m = pe.matmul(v["P"][1][:, h], v["M"][:, l, h, :], v["Tm"][:, h, :], start=h == 0, stop=True, skip_group_check=True)
                            m.then_inc(e["X_ready"], 1)
                        for d in range(2):
                            v, e = L[d], E[d]
                            pe.wait_ge(e["X_set"], six + (6 * base + l))
                            if l == 1:
                                pe.wait_ge(e["qkT_set"], one)
                            for h in range(HEADS):
                                m = pe.matmul(v["P"][2][:, h], v["X"][:, h, :], v["R"][:, h, :], start=h == 0, stop=True, skip_group_check=True)
                            m.then_inc(e["dR_ready"], 1)
                    for d in range(2):
                        v, e = L[d], E[d]
                        pe.wait_ge(e["keT_set"], one)
                        for h in range(HEADS):
                            m = pe.matmul(v["P"][0][:, h], v["keT"][:, h, :], v["S"][:, h, :], start=h == 0, stop=True, skip_group_check=True)
                        m.then_inc(e["kS_ready"], 1)
                    for d in range(2):
                        v, e = L[d], E[d]
                        pe.wait_ge(e["rv_set"], one)
                        for h in range(HEADS):
                            m = pe.matmul(v["P"][1][:, h], v["R"][:, h, :], v["rv"][:, h, :], start=h == 0, stop=True, skip_group_check=True)
                        m.then_inc(e["Tv_ready"], 1)
                    for d in range(2):
                        v, e = L[d], E[d]
                        pe.wait_ge(e["qdT_set"], s + (base + 2))
                        for h in range(HEADS):
                            pe.matmul(v["P"][2][:, h], v["qdT"][:, h, :], v["S"][:, h, :], start=h == 0, stop=False, skip_group_check=True)
                    for d in range(2):
                        v, e = L[d], E[d]
                        pe.wait_ge(e["vn_set"], one)
                        for h in range(HEADS):
                            m = pe.matmul(v["P"][3][:, h], v["kdec"][:, h, :], v["vn"][:, h, :], start=h == 0, stop=True, skip_group_check=True)
                        m.then_inc(e["kv_ready"], 1)
                        for h in range(HEADS):
                            m = pe.matmul(v["P"][2][:, h], v["qkT"][:, h, :], v["vn"][:, h, :], start=False, stop=True, skip_group_check=True)
                        m.then_inc(e["o_ready"], 1)

        @block.vector
        def _(dve):
            dve.memset(O[:, :, :], 0.0).then_inc(cleared, 1)
            dve.wait_ge(cleared, 1)
            for base, n, first, r in runs:
                for d in range(2):
                    if base:
                        dve.wait_ge(E[d]["S_set"], base + r)
                    dve.memset(L[d]["S"][:, :, :], 0.0).then_inc(E[d]["S_set"], 1)
                with dve.Fori(0, n) as s:
                    one = s + (base + 1)
                    for d in range(2):
                        v, e = L[d], E[d]
                        dve.wait_ge(e["S_set"], s + (base + 1 + r))
                        dve.tensor_copy(v["gs"][:, :], gates[:, d, bass.ds(tile(d, s, first, n), 1), :]
                                        .rearrange("p a c -> p (a c)")).then_inc(e["gates_set"], 1)
                    for d in range(2):
                        v, e = L[d], E[d]
                        dve.wait_ge(e["gates_set"], one)
                        dve.wait_ge(e["eg_set"], one)
                        dve.tensor_tensor(v["diff"][:, :, :], v["P"][0][:, :, :], bcast(v["gs"][:, 0:4], P, 2), ALU.subtract).then_inc(e["diff_set"], 1)
                    for d in range(2):
                        v, e = L[d], E[d]
                        dve.wait_ge(e["kturned"], one)
                        dve.tensor_tensor(v["kdec"][:, :, :], v["P"][3][:, :, :], bcast(v["gs"][:, 8:12], P, 2), ALU.mult).then_inc(e["kdec_set"], 1)
                    for d in range(2):
                        v, e = L[d], E[d]
                        dve.wait_ge(e["dec_set"], one)
                        for h in range(HEADS):
                            m = dve.scalar_tensor_tensor(out=v["lt"][:, h, :], in0=v["P"][1][:, h], scalar=v["gs"][:, 4 + h:5 + h],
                                                         in1=v["dec"][:, h, :], op0=ALU.mult, op1=ALU.mult)
                        m.then_inc(e["lt_set"], 1)
                    for d in range(2):
                        v, e = L[d], E[d]
                        dve.wait_ge(e["qk"], one)
                        dve.tensor_tensor(v["qkT"][:, :, :], v["P"][2][:, :, :], v["dec"][:, :, :], ALU.mult).then_inc(e["qkT_set"], 1)
                    for d in range(2):
                        v, e = L[d], E[d]
                        dve.wait_ge(e["M_set"], s * 7 + (7 * base + 1))
                        dve.tensor_tensor(v["R"][:, :, :], bcast(k["ident"][:, :], HEADS, 1), v["M"][:, 0], ALU.subtract).then_inc(e["R_set"], 1)
                    for l in range(1, LEVELS):
                        for d in range(2):
                            v, e = L[d], E[d]
                            dve.wait_ge(e["R_set"], s * 7 + (7 * base + l))
                            dve.wait_ge(e["dR_ready"], s * 6 + (6 * base + l))
                            dve.tensor_tensor(v["R"][:, :, :], v["R"][:, :, :], v["P"][2][:, :, :], ALU.subtract).then_inc(e["R_set"], 1)
                    for d in range(2):
                        v, e = L[d], E[d]
                        dve.wait_ge(e["vtok_set"], one)
                        dve.wait_ge(e["kS_ready"], one)
                        dve.tensor_tensor(v["rv"][:, :, :], v["vtok"][:, :, :], v["P"][0][:, :, :], ALU.subtract).then_inc(e["rv_set"], 1)
                    for d in range(2):
                        v, e = L[d], E[d]
                        dve.wait_ge(e["Tv_ready"], one)
                        dve.tensor_tensor(v["vn"][:, :, :], v["P"][1][:, :, :], bcast(v["gs"][:, 4:8], P, 2), ALU.mult).then_inc(e["vn_set"], 1)
                    for d in range(2):
                        v, e = L[d], E[d]
                        dve.wait_ge(e["o_ready"], one)
                        out = O[:, bass.ds(tile(d, s, first, n), 1), :].rearrange("p a (h c) -> p (a h) c", h=HEADS)
                        dve.tensor_tensor(out, v["P"][2][:, :, :], out, ALU.add).then_inc(e["o_added"], 1)
                        dve.wait_ge(e["kv_ready"], one)
                        for h in range(HEADS):
                            m = dve.scalar_tensor_tensor(out=v["S"][:, h, :], in0=v["S"][:, h, :], scalar=v["gs"][:, 12 + h:13 + h],
                                                         in1=v["P"][3][:, h], op0=ALU.mult, op1=ALU.add)
                        m.then_inc(e["S_set"], 1)


def software_pipeline(eng, step):
    for u in range(3):
        step(u % 2, u)
    with eng.Fori(1, (NT - 2) // 2) as j:
        step(1, j * 2 + 1)
        step(0, j * 2 + 2)
    for u in (NT - 1, NT):
        step(u % 2, u)


def parts_of(u):
    if not isinstance(u, int):
        return True, True, True
    return u < NT, u + 1 < NT, u >= 1


def wait_if_any(eng, sem, value):
    if not isinstance(value, int) or value > 0:
        eng.wait_ge(sem, value)


def output(nc, k, dram, feat, O, lg, x2_rows, xn_rows):
    with ExitStack() as ctx:
        b = Bufs(nc, ctx, "output_")
        wo, g2 = b.sb("wo", [P, KD, D]), b.sb("g2", [P, D])
        rw, rb, dg = b.sb("router_w", [P, KD, NG + NE]), b.sb("router_b", [P, NG + NE]), b.sb("dn_gain", [P, 1])
        pair = lambda name, shape: [b.sb(f"{name}{p}", shape) for p in range(2)]
        mixT, z, x = pair("mixT", [P, KD, P]), pair("z", [P, HEADS, P]), pair("xres", [P, D])
        on, x2, xn, xT = pair("on", [P, HEADS, P]), pair("x2", [P, D]), pair("xn", [P, D]), pair("xT", [P, KD, P])
        ss, rt, ri = pair("oss", [P, HEADS]), pair("ort", [P, HEADS]), pair("ori", [P, HEADS])
        ss2, rt2, ri2 = pair("xss", [P, 1]), pair("xrt", [P, 1]), pair("xri", [P, 1])
        junk, junk2 = b.sb("junk_o", [P, HEADS, P]), b.sb("junk_x", [P, D])
        tA, lgp = b.ps("on_turned", [P, HEADS, P]), b.ps("logits", [P, 512])
        Y = [b.ps(f"yo{n}", [P, 512]) for n in range(2)]
        tX = [b.ps(f"x_turned{n}", [P, 4, P]) for n in range(2)]
        names = ("o_squared o_rooted o_inverted on_set on_turned mix_set y_ready x2_set x_squared x_rooted x_inverted "
                 "xn_set x_turned xT_set lg_ready lg_set").split()
        e = {n: b.sem("out_" + n) for n in names}
        const = b.sem("out_const")
        loaded = [b.sem(f"out_loaded{p}") for p in range(2)]
        x2_st = [b.sem(f"x2_stored{p}") for p in range(2)]
        xn_st = [b.sem(f"xn_stored{p}") for p in range(2)]
        block = ctx.enter_context(nc.Block())
        CONSTS = 5 * 16

        def through_slot(eng, sem, t, p, each):
            eng.wait_ge(sem, (t - p) * (each // 2) + each)

        @block.sync
        def _(sp):
            for dst, src in ((wo[:, :, :], dram["w_o"].rearrange("(k p) n -> p k n", p=P)),
                             (g2[:, :], dram["norm2_g"].partition_broadcast(P)),
                             (rw[:, :, :], dram["router_w"].rearrange("(k p) n -> p k n", p=P)),
                             (rb[:, :], dram["router_b"].partition_broadcast(P)),
                             (dg[:, :], dram["dn_norm_g"])):
                sp.dma_start(dst, src).then_inc(const, 16)

            def load(p, t):
                cols = bass.ds(t * P, P)
                sp.dma_start(mixT[p][:, 0:4, :], feat[16:20, :, cols].rearrange("c p t -> p c t")).then_inc(loaded[p], 16)
                sp.dma_start(z[p][:, :, :], feat[12:16, :, cols].rearrange("c p t -> p c t")).then_inc(loaded[p], 16)
                sp.dma_start(x[p][:, :], dram["x"][cols, :]).then_inc(loaded[p], 16)

            def store_sum(p, t):
                sp.dma_start(x2_rows[bass.ds(t * P, P), :], x2[p][:, :]).then_inc(x2_st[p], 16)

            def store_normed(p, t):
                sp.dma_start(xn_rows[bass.ds(t * P, P), :], xn[p][:, :]).then_inc(xn_st[p], 16)

            for p in range(2):
                load(p, p)
            with sp.Fori(1, NT // 2) as j:
                for p in range(2):
                    t = j * 2 + p
                    sp.wait_ge(e["x2_set"], t - 1)
                    load(p, t)
                    store_sum(p, t - 2)
                    sp.wait_ge(e["xn_set"], t - 1)
                    store_normed(p, t - 2)
            for p in range(2):
                sp.wait_ge(e["x2_set"], NT - 1 + p)
                store_sum(p, NT - 2 + p)
                sp.wait_ge(e["xn_set"], NT - 1 + p)
                store_normed(p, NT - 2 + p)
            for p in range(2):
                sp.wait_ge(x2_st[p], 8 * NT)
                sp.wait_ge(xn_st[p], 8 * NT)

        @block.scalar
        def _(act):
            act.wait_ge(const, CONSTS)

            def begin(p, t):
                for h in range(HEADS):
                    src = O[:, bass.ds(t, 1), h * P:(h + 1) * P].rearrange("p a c -> p (a c)")
                    m = act.activation(junk[:, h, :], src, ACT.Square, accum_out=ss[p][:, h:h + 1])
                m.then_inc(e["o_squared"], 1)
                act.wait_ge(e["o_squared"], t + 1)
                act.activation(rt[p][:, :], ss[p][:, :], ACT.Sqrt, bias=k["eps"][:, :], scale=1.0 / P).then_inc(e["o_rooted"], 1)

            def step(p, u):
                project_, begin_, end_ = parts_of(u)
                t = u - 1
                if end_:
                    act.wait_ge(e["x2_set"], t + 1)
                    act.activation(junk2[:, :], x2[1 - p][:, :], ACT.Square, accum_out=ss2[1 - p][:, :]).then_inc(e["x_squared"], 1)
                    act.wait_ge(e["x_squared"], t + 1)
                    act.activation(rt2[1 - p][:, :], ss2[1 - p][:, :], ACT.Sqrt, bias=k["eps"][:, :], scale=1.0 / D).then_inc(e["x_rooted"], 1)
                if begin_:
                    begin(1 - p, u + 1)
                if end_:
                    act.wait_ge(e["x_turned"], t + 1)
                    for n in range(2):
                        m = act.activation(xT[1 - p][:, 4 * n:4 * n + 4, :], tX[n][:, :, :], ACT.Copy)
                    m.then_inc(e["xT_set"], 1)

            begin(0, 0)
            software_pipeline(act, step)

        @block.tensor
        def _(pe):
            pe.wait_ge(const, CONSTS)

            def begin(p, t):
                pe.wait_ge(e["on_set"], t + 1)
                for h in range(HEADS):
                    m = pe.transpose(tA[:, h], on[p][:, h, :], k["ident"][:, :])
                m.then_inc(e["on_turned"], 1)

            def step(p, u):
                project_, begin_, end_ = parts_of(u)
                t = u - 1
                if project_:
                    pe.wait_ge(e["mix_set"], u + 1)
                    through_slot(pe, loaded[p], u, p, 48)
                    wait_if_any(pe, e["x2_set"], u)
                    for n in range(2):
                        for kt in range(KD):
                            m = pe.matmul(Y[n][:, :], mixT[p][:, kt, :], wo[:, kt, n * 512:(n + 1) * 512], start=kt == 0, stop=kt == KD - 1)
                    m.then_inc(e["y_ready"], 1)
                if begin_:
                    begin(1 - p, u + 1)
                if end_:
                    pe.wait_ge(e["xn_set"], t + 1)
                    wait_if_any(pe, e["xT_set"], t)
                    for c in range(KD):
                        m = pe.transpose(tX[c // 4][:, c % 4, :], xn[1 - p][:, c * P:(c + 1) * P], k["ident"][:, :])
                    m.then_inc(e["x_turned"], 1)
                    pe.wait_ge(e["xT_set"], t + 1)
                    wait_if_any(pe, e["lg_set"], t)
                    for kt in range(KD):
                        m = pe.matmul(lgp[:, 0:NG + NE], xT[1 - p][:, kt, :], rw[:, kt, :], start=kt == 0, stop=kt == KD - 1)
                    m.then_inc(e["lg_ready"], 1)

            begin(0, 0)
            software_pipeline(pe, step)

        @block.vector
        def _(dve):
            dve.wait_ge(const, CONSTS)

            def begin(p, t):
                dve.wait_ge(e["o_rooted"], t + 1)
                dve.reciprocal(ri[p][:, :], rt[p][:, :]).then_inc(e["o_inverted"], 1)
                dve.wait_ge(e["o_inverted"], t + 1)
                src = O[:, bass.ds(t, 1), :].rearrange("p a (h c) -> p (a h) c", h=HEADS)
                dve.tensor_tensor(on[p][:, :, :], src, bcast(ri[p][:, :], P, 2), ALU.mult).then_inc(e["on_set"], 1)

            def gate(p, t):
                dve.wait_ge(e["on_turned"], t + 1)
                through_slot(dve, loaded[p], t, p, 48)
                dve.scalar_tensor_tensor(out=mixT[p][:, 4:8, :], in0=tA[:, :, :], scalar=dg[:, :], in1=z[p][:, :, :],
                                         op0=ALU.mult, op1=ALU.mult).then_inc(e["mix_set"], 1)

            def step(p, u):
                project_, begin_, end_ = parts_of(u)
                t = u - 1
                if end_:
                    dve.wait_ge(e["x_rooted"], t + 1)
                    dve.reciprocal(ri2[1 - p][:, :], rt2[1 - p][:, :]).then_inc(e["x_inverted"], 1)
                    dve.wait_ge(e["x_inverted"], t + 1)
                    wait_if_any(dve, xn_st[1 - p], (t - (1 - p)) * 8)
                    dve.scalar_tensor_tensor(out=xn[1 - p][:, :], in0=x2[1 - p][:, :], scalar=ri2[1 - p][:, :], in1=g2[:, :],
                                             op0=ALU.mult, op1=ALU.mult).then_inc(e["xn_set"], 1)
                if begin_:
                    begin(1 - p, u + 1)
                if project_:
                    dve.wait_ge(e["y_ready"], u + 1)
                    wait_if_any(dve, x2_st[p], (u - p) * 8)
                    for n in range(2):
                        m = dve.tensor_tensor(x2[p][:, n * 512:(n + 1) * 512], Y[n][:, :], x[p][:, n * 512:(n + 1) * 512], ALU.add)
                    m.then_inc(e["x2_set"], 1)
                if begin_:
                    gate(1 - p, u + 1)
                if end_:
                    dve.wait_ge(e["lg_ready"], t + 1)
                    dst = lg[:, bass.ds(t, 1), :].rearrange("p a c -> p (a c)")
                    dve.tensor_tensor(dst, lgp[:, 0:NG + NE], rb[:, :], ALU.add).then_inc(e["lg_set"], 1)

            begin(0, 0)
            gate(0, 0)
            software_pipeline(dve, step)


def route(nc, k, lg, gate, slot, table, idx, slot_rows):
    with ExitStack() as ctx:
        b = Bufs(nc, ctx, "route_")
        S4, S8 = [P, NT, NG], [P, NT, EPG]
        desc, it128, itb = b.sb("desc", [P, EPG]), b.sb("it128", [P, NT]), b.sb("itb", [P, MAXB])
        tok, zero = b.sb("tok", [P, NT], I32), b.sb("zero", [MAXB + 2, P], I32)
        mg, m1, m2 = (b.sb(n, [P, NT]) for n in ("mg", "m1", "m2"))
        t4, t8 = b.sb("t4", S4), b.sb("t8", S8)
        hg, h1, h2 = b.sb("hot_group", S4), b.sb("hot1", S8), b.sb("hot2", S8)
        mx4, eg4, sg = b.sb("mx4", S4), b.sb("eg4", S4), b.sb("sg", [P, NT])
        sel, es, ms = b.sb("sel", [P, NT, NG, EPG]), b.sb("es", S8), b.sb("ms", S8)
        dm, ratio, den = (b.sb(n, [P, NT]) for n in ("dm", "ratio", "den"))
        A = [b.sb(f"A{c}", [P, NT, NG, EPG]) for c in range(2)]
        both, pos, prod = b.sb("A_both", [P, NT, NE]), b.sb("pos", [P, NT, NE]), b.sb("prod", [P, NT, NE])
        off = b.sb("off", [P, NT + 1, NE])
        cmp = b.sb("cmp", [P, MAXB * NE])
        nb, cum = b.sb("nblk", [P, NE]), [b.sb(f"cum{i}", [P, NE]) for i in range(2)]
        bx = b.sb("block_expert", [P, MAXB])
        sf = [b.sb(f"slot_f{c}", [P, NT]) for c in range(2)]
        tf, tmp = b.sb("table_f", [P, 2 * MAXB + NE + 1]), b.sb("slot_tok_i", [MAXB + 2, P], I32)
        tmpf = b.sb("slot_tok_f", [MAXB + 2, P])
        H = NT // 2
        rank = [b.ps(f"rank{h}", [P, H, NE]) for h in range(2)]
        tot = [b.ps(f"tot{h}", [P, H, NE]) for h in range(2)]
        idp = b.ps("idx_turned", [P, MAXB + 2])
        dv, ac, pl, pe_s = b.sem("route_vector"), b.sem("route_scalar"), b.sem("route_pool"), b.sem("route_tensor")
        both_set, slots_set, zeroed, scattered, back, turned = (b.sem("route_" + n) for n in
            ("both_set", "slots_set", "zeroed", "scattered", "read_back", "turned"))
        exps_in, dm_in, tok_f = b.sem("route_exps_in"), b.sem("route_dm_in"), b.sem("route_tok_f")
        block = ctx.enter_context(nc.Block())

        @block.gpsimd
        def _(pool):
            pool.memset(zero[:, :], 0).then_inc(pl, 1)
            pool.iota(desc[:, :], pattern=[[-1, EPG]], base=EPG, channel_multiplier=0, allow_small_or_imprecise_dtypes=True).then_inc(pl, 1)
            pool.iota(it128[:, :], pattern=[[P, NT]], base=0, channel_multiplier=0, allow_small_or_imprecise_dtypes=True).then_inc(pl, 1)
            pool.iota(itb[:, :], pattern=[[1, MAXB]], base=0, channel_multiplier=0, allow_small_or_imprecise_dtypes=True).then_inc(pl, 1)
            pool.iota(tok[:, :], pattern=[[P, NT]], base=0, channel_multiplier=1).then_inc(pl, 1)
            pool.wait_ge(pl, 5)
            pool.wait_ge(slots_set, 1)
            pool.wait_ge(zeroed, 16)
            for t in range(NT):
                for c in range(2):
                    pool.indirect_dma_start(
                        out=slot_rows[:, :], out_offset=bass.IndirectOffsetOnAxis(ap=slot[:, c, t:t + 1], axis=0),
                        in_=tok[:, t:t + 1], in_offset=None).then_inc(scattered, 16)
            pool.wait_ge(scattered, 16 * 2 * NT)

        @block.sync
        def _(sp):
            sp.wait_ge(pl, 1)
            sp.dma_start(slot_rows.rearrange("(b p) a -> b (p a)", p=P), zero[:, :]).then_inc(zeroed, 16)
            sp.wait_ge(scattered, 16 * 2 * NT)
            sp.dma_start(tmp[:, :], slot_rows.rearrange("(b p) a -> b (p a)", p=P)).then_inc(back, 16)
            sp.wait_ge(back, 16)

        @block.scalar
        def _(act):
            act.wait_ge(exps_in, 1)
            act.activation(eg4[:, :, :], mx4[:, :, :], ACT.Exp).then_inc(ac, 1)
            act.wait_ge(dm_in, 1)
            act.activation(ratio[:, :], dm[:, :], ACT.Exp).then_inc(ac, 1)

        @block.tensor
        def _(pe):
            pe.wait_ge(both_set, 1)
            for h in range(2):
                pe.matmul(rank[h][:, :, :], k["lower"][:, :], both[:, h * H:(h + 1) * H, :], start=True, stop=True)
                m = pe.matmul(tot[h][:, :, :], k["ones"][:, :], both[:, h * H:(h + 1) * H, :], start=True, stop=True)
            m.then_inc(pe_s, 1)
            pe.wait_ge(tok_f, 1)
            pe.transpose(idp[:, :], tmpf[:, :], k["ident"][0:MAXB + 2, 0:MAXB + 2]).then_inc(turned, 1)

        @block.vector
        def _(dve):
            n = [0]

            def link(m):
                n[0] += 1
                m.then_inc(dv, 1)
                dve.wait_ge(dv, n[0])

            def first_max(v, w, top, scores, hot):
                link(dve.tensor_reduce(top[:, :], v, AX.X, ALU.max))
                link(dve.tensor_tensor(scores[:, :, :], v, bcast(top[:, :], w, 2), ALU.is_equal))
                link(dve.tensor_tensor(scores[:, :, :], scores[:, :, :], bcast(desc[:, EPG - w:EPG], NT, 1), ALU.mult))
                link(dve.tensor_reduce(sg[:, :], scores[:, :, :], AX.X, ALU.max))
                link(dve.tensor_tensor(hot[:, :, :], scores[:, :, :], bcast(sg[:, :], w, 2), ALU.is_equal))

            dve.wait_ge(pl, 5)
            groups = lg[:, :, 0:NG]
            first_max(groups, NG, mg, t4, hg)
            dve.tensor_tensor(mx4[:, :, :], groups, bcast(mg[:, :], NG, 2), ALU.subtract).then_inc(exps_in, 1)
            experts = lg[:, :, NG:NG + NE].rearrange("p t (g e) -> p t g e", g=NG)
            link(dve.tensor_tensor(sel[:, :, :, :], experts, bcast(hg[:, :, :], EPG, 3), ALU.mult))
            link(dve.tensor_reduce(es[:, :, :], sel[:, :, :, :].rearrange("p t g e -> p t e g"), AX.X, ALU.add))
            first_max(es[:, :, :], EPG, m1, t8, h1)
            link(dve.scalar_tensor_tensor(out=ms[:, :, :], in0=h1[:, :, :], scalar=-1e30, in1=es[:, :, :], op0=ALU.mult, op1=ALU.add))
            first_max(ms[:, :, :], EPG, m2, t8, h2)
            dve.tensor_tensor(dm[:, :], m2[:, :], m1[:, :], ALU.subtract).then_inc(dm_in, 1)
            for c, h in ((0, h1), (1, h2)):
                link(dve.tensor_tensor(A[c][:, :, :, :], bcast(hg[:, :, :], EPG, 3), bcast(h[:, :, :], NG, 2), ALU.mult))
            flat = [a[:, :, :, :].rearrange("p t g e -> p t (g e)") for a in A]
            dve.tensor_tensor(both[:, :, :], flat[0], flat[1], ALU.add).then_inc(both_set, 1)
            dve.wait_ge(ac, 2)
            link(dve.tensor_reduce(sg[:, :], eg4[:, :, :], AX.X, ALU.add))
            link(dve.tensor_scalar(den[:, :], ratio[:, :], 1.0, None, ALU.add))
            link(dve.tensor_tensor(den[:, :], den[:, :], sg[:, :], ALU.mult))
            link(dve.reciprocal(gate[:, 0, :], den[:, :]))
            link(dve.tensor_tensor(gate[:, 1, :], gate[:, 0, :], ratio[:, :], ALU.mult))
            link(dve.memset(off[:, 0, :], 0.0))
            dve.wait_ge(pe_s, 1)
            for t in range(NT):
                link(dve.tensor_tensor(off[:, t + 1, :], tot[t // H][:, t % H, :], off[:, t, :], ALU.add))
            for h in range(2):
                link(dve.tensor_tensor(pos[:, h * H:(h + 1) * H, :], rank[h][:, :, :], off[:, h * H:(h + 1) * H, :], ALU.add))
            blocks = cmp[:, 0:NE * NT].rearrange("p (e t) -> p e t", t=NT)
            link(dve.tensor_tensor(blocks, bcast(off[:, NT, :], NT, 2), bcast(it128[:, :], NE, 1), ALU.is_gt))
            link(dve.tensor_reduce(nb[:, :], blocks, AX.X, ALU.add))
            link(dve.tensor_copy(cum[0][:, :], nb[:, :]))
            for i in range(5):
                s, a, c = 1 << i, cum[i % 2], cum[1 - i % 2]
                link(dve.tensor_copy(c[:, 0:s], a[:, 0:s]))
                link(dve.tensor_tensor(c[:, s:NE], a[:, s:NE], a[:, 0:NE - s], ALU.add))
            end = cum[1]
            link(dve.tensor_tensor(cum[0][:, :], end[:, :], nb[:, :], ALU.subtract))
            link(dve.scalar_tensor_tensor(out=pos[:, :, :], in0=bcast(cum[0][:, :], NT, 1), scalar=float(P), in1=pos[:, :, :],
                                          op0=ALU.mult, op1=ALU.add))
            for c in range(2):
                link(dve.tensor_tensor(prod[:, :, :], flat[c], pos[:, :, :], ALU.mult))
                link(dve.tensor_reduce(sf[c][:, :], prod[:, :, :], AX.X, ALU.add))
            for c in range(2):
                link(dve.tensor_copy(slot[:, c, :], sf[c][:, :]))
            dve.sem_inc(slots_set, 1)
            ends = cmp[:, :].rearrange("p (b e) -> p b e", e=NE)
            link(dve.tensor_tensor(ends, bcast(itb[:, :], NE, 2), bcast(end[:, :], MAXB, 1), ALU.is_ge))
            link(dve.tensor_reduce(bx[:, :], ends, AX.X, ALU.add))
            link(dve.tensor_scalar(tf[:, 0:MAXB], bx[:, :], float(NE - 1), None, ALU.min))
            link(dve.tensor_copy(table[:, 0:MAXB], tf[:, 0:MAXB]))
            link(dve.tensor_single_scalar(table[:, MAXB:2 * MAXB], table[:, 0:MAXB], 1, ALU.bitwise_and))
            link(dve.tensor_scalar(tf[:, 0:NE], end[:, :], 1.0, None, ALU.add))
            link(dve.tensor_copy(table[:, 2 * MAXB:2 * MAXB + NE], tf[:, 0:NE]))
            link(dve.tensor_copy(table[:, 2 * MAXB + NE:2 * MAXB + NE + 1], end[:, NE - 1:NE]))
            dve.wait_ge(back, 16)
            dve.tensor_copy(tmpf[:, :], tmp[:, :]).then_inc(tok_f, 1)
            dve.wait_ge(turned, 1)
            dve.tensor_copy(idx[:, :], idp[:, :])


def experts(nc, k, dram, table, idx, xn_rows, y_rows):
    with ExitStack() as ctx:
        b = Bufs(nc, ctx, "experts_")
        pair = lambda name, shape, dt=F32: [b.sb(f"{name}{p}", shape, dt) for p in range(2)]
        W1, W3, W2 = b.sb("W1", [P, 2, KD, FF]), b.sb("W3", [P, 2, KD, FF]), b.sb("W2", [P, 2, FF // P, D])
        ix, xg, xT = pair("ix", [P, 1], I32), pair("xg", [P, D]), pair("xgT", [P, KD, P])
        s, g, gT, yo = b.sb("silu", [P, FF]), b.sb("gated", [P, FF]), b.sb("gatedT", [P, FF // P, P]), pair("yout", [P, D])
        tX = [b.ps(f"xg_turned{n}", [P, 4, P]) for n in range(2)]
        H1, H3, tG = b.ps("h1", [P, FF]), b.ps("h3", [P, FF]), b.ps("g_turned", [P, FF // P, P])
        Y = [b.ps(f"ye{n}", [P, 512]) for n in range(2)]
        names = "ix_set turned xTa_set xTb_set h1_ready h3_ready silu_set gated_set g_turned gT_set y_ready y_set done weights gathers_begun all_stored".split()
        e = {n: b.sem("moe_" + n) for n in names}
        gathered = [b.sem(f"moe_gathered{p}") for p in range(2)]
        y_free = [b.sem(f"moe_y_free{p}") for p in range(2)]
        w_sem = [b.sem(f"moe_w{p}") for p in range(2)]
        zero, zero_set, emptied = b.sb("zero", [P, D]), b.sem("zero_set"), b.sem("emptied")
        block = ctx.enter_context(nc.Block())
        NB = 2 * MAXB + NE
        PAIRS = MAXB // 2

        def n_blocks(eng):
            return eng.value_load(table[0:1, NB:NB + 1], min_val=1, max_val=MAXB)

        @block.sync
        def _(sp):
            def load(p, x):
                ex = bass.ds(x, 1)
                sp.dma_start(W1[:, p], dram["w1"][ex].rearrange("a (k p) n -> p (a k) n", p=P)).then_inc(w_sem[p], 16)
                sp.dma_start(W3[:, p], dram["w3"][ex].rearrange("a (k p) n -> p (a k) n", p=P)).then_inc(w_sem[p], 16)
                sp.dma_start(W2[:, p], dram["w2"][ex].rearrange("a (k p) n -> p (a k) n", p=P)).then_inc(w_sem[p], 16)

            for p in range(2):
                load(p, p)
            with sp.Fori(1, NE // 2) as j:
                for p in range(2):
                    x = j * 2 + p
                    sp.wait_ge(w_sem[p], j * 48)
                    sp.sem_inc(e["weights"], 1)
                    last = sp.value_load(table[0:1, bass.ds(x + (2 * MAXB - 2), 1)], min_val=1, max_val=MAXB + 1)
                    sp.wait_ge(e["done"], last)
                    load(p, x)
            for p in range(2):
                sp.wait_ge(w_sem[p], 48 * (NE // 2))
                sp.sem_inc(e["weights"], 1)

        @block.gpsimd
        def _(pool):
            def gather(p, blk, before):
                if before is not None:
                    pool.wait_ge(e["turned"], before)
                pool.tensor_copy(ix[p][:, :], idx[:, bass.ds(blk, 1)]).then_inc(e["ix_set"], 1)
                pool.wait_ge(e["ix_set"], blk + 1)
                pool.sem_inc(e["gathers_begun"], 1)
                pool.indirect_dma_start(out=xg[p][:, :], out_offset=None, in_=xn_rows[:, :],
                                        in_offset=bass.IndirectOffsetOnAxis(ap=ix[p][:, 0:1], axis=0)).then_inc(gathered[p], 16)

            n = n_blocks(pool)
            pool.memset(zero[:, :], 0.0).then_inc(zero_set, 1)
            gather(0, 0, None)
            gather(1, 1, None)
            pool.wait_ge(zero_set, 1)
            with pool.Fori(0, PAIRS) as j:
                with pool.If(j * 2 < n):
                    gather(0, j * 2 + 2, j * 2 + 1)
                    gather(1, j * 2 + 3, j * 2 + 2)
                with pool.If(j * -2 + (2 * PAIRS - 2) >= n):
                    dst = y_rows[bass.ds(j * (-2 * P) + (2 * PAIRS - 2) * P, 2 * P), :]
                    pool.dma_start(dst.rearrange("(a p) d -> p a d", p=P), bcast(zero[:, :], 2, 1)).then_inc(emptied, 16)
                    pool.wait_ge(emptied, j * 16 + 16)

        @block.tensor
        def _(pe):
            def turn(p, blk, gather_count, free):
                pe.wait_ge(gathered[p], gather_count)
                if free is not None:
                    pe.wait_ge(e["xTa_set"], free)
                    pe.wait_ge(e["xTb_set"], free)
                for c in range(KD):
                    m = pe.transpose(tX[c // 4][:, c % 4, :], xg[p][:, c * P:(c + 1) * P], k["ident"][:, :])
                m.then_inc(e["turned"], 1)

            def hidden(p, blk, half):
                pe.wait_ge(e["xTa_set"], blk + 1)
                pe.wait_ge(e["xTb_set"], blk + 1)
                pe.wait_ge(e["gated_set"], blk + 1)
                for H, W, name in ((H1, W1, "h1_ready"), (H3, W3, "h3_ready")):
                    for kt in range(KD):
                        rhs = W[:, half, kt, :].rearrange("p a n -> p (a n)")
                        m = pe.matmul(H[:, :], xT[p][:, kt, :], rhs, start=kt == 0, stop=kt == KD - 1)
                    m.then_inc(e[name], 1)

            def out(p, blk, half):
                pe.wait_ge(e["gated_set"], blk + 2)
                for c in range(FF // P):
                    m = pe.transpose(tG[:, c, :], g[:, c * P:(c + 1) * P], k["ident"][:, :])
                m.then_inc(e["g_turned"], 1)
                pe.wait_ge(e["gT_set"], blk + 1)
                pe.wait_ge(e["y_set"], blk + 1)
                for n in range(2):
                    for c in range(FF // P):
                        rhs = W2[:, half, c, n * 512:(n + 1) * 512].rearrange("p a n -> p (a n)")
                        m = pe.matmul(Y[n][:, :], gT[:, c, :], rhs, start=c == 0, stop=c == FF // P - 1)
                    m.then_inc(e["y_ready" if n == 0 else "done"], 1)

            n = n_blocks(pe)
            for name in ("gated_set", "y_set", "done"):
                pe.sem_inc(e[name], 1)
            turn(0, 0, 16, None)
            with pe.Fori(0, PAIRS) as j:
                with pe.If(j * 2 < n):
                    for p in range(2):
                        blk = j * 2 + p
                        x = pe.value_load(table[0:1, bass.ds(blk, 1)], min_val=0, max_val=NE - 1)
                        half = bass.ds(pe.value_load(table[0:1, bass.ds(blk + MAXB, 1)], min_val=0, max_val=1), 1)
                        pe.wait_ge(e["weights"], x + 1)
                        hidden(p, blk, half)
                        turn(1 - p, blk + 1, j * 16 + (16 if p == 0 else 32), blk + 1)
                        out(p, blk, half)

        @block.scalar
        def _(act):
            def turned(p, blk):
                act.wait_ge(e["turned"], blk + 1)
                act.activation(xT[p][:, 0:4, :], tX[0][:, :, :], ACT.Copy).then_inc(e["xTa_set"], 1)

            n = n_blocks(act)
            for p in range(2):
                act.dma_start(yo[p][0:1, :], dram["final_norm_g"].rearrange("(a n) -> a n", a=1)).then_inc(y_free[p], 16)
            turned(0, 0)
            with act.Fori(0, PAIRS) as j:
                with act.If(j * 2 < n):
                    for p in range(2):
                        blk = j * 2 + p
                        act.wait_ge(e["h1_ready"], blk + 1)
                        act.activation(s[:, :], H1[:, :], ACT.Silu).then_inc(e["silu_set"], 1)
                        turned(1 - p, blk + 1)
                        act.wait_ge(y_free[p], j * 16 + 16)
                        for c in range(2):
                            act.wait_ge(e["done" if c else "y_ready"], blk + (1 + c))
                            m = act.activation(yo[p][:, c * 512:(c + 1) * 512], Y[c][:, :], ACT.Copy)
                        m.then_inc(e["y_set"], 1)
                        act.wait_ge(e["y_set"], blk + 2)
                        act.dma_start(y_rows[bass.ds(blk * P, P), :], yo[p][:, :]).then_inc(y_free[p], 16)
            for p in range(2):
                act.wait_ge(y_free[p], (n + 1) // 2 * 16 + 16)
                act.sem_inc(e["all_stored"], 1)

        @block.vector
        def _(dve):
            def turned(p, blk):
                dve.wait_ge(e["turned"], blk + 1)
                dve.tensor_copy(xT[p][:, 4:8, :], tX[1][:, :, :]).then_inc(e["xTb_set"], 1)

            n = n_blocks(dve)
            turned(0, 0)
            with dve.Fori(0, PAIRS) as j:
                with dve.If(j * 2 < n):
                    for p in range(2):
                        blk = j * 2 + p
                        dve.wait_ge(e["silu_set"], blk + 1)
                        dve.wait_ge(e["h3_ready"], blk + 1)
                        dve.tensor_tensor(g[:, :], H3[:, :], s[:, :], ALU.mult).then_inc(e["gated_set"], 1)
                        turned(1 - p, blk + 1)
                        dve.wait_ge(e["g_turned"], blk + 1)
                        dve.tensor_copy(gT[:, :, :], tG[:, :, :]).then_inc(e["gT_set"], 1)


def combine(nc, k, dram, gate, slot, x2_rows, y_rows, y):
    with ExitStack() as ctx:
        b = Bufs(nc, ctx, "combine_")
        pair = lambda name, shape, dt=F32: [b.sb(f"{name}{p}", shape, dt) for p in range(2)]
        gf, junk = b.sb("final_gain", [P, D]), b.sb("junk_f", [P, D])
        ix, x = pair("cix", [P, 2], I32), pair("cx", [P, D])
        r = [pair(f"crow{c}", [P, D]) for c in range(2)]
        ss, rt, ri = pair("css", [P, 1]), pair("crt", [P, 1]), pair("cri", [P, 1])
        names = "ix_set gathers_begun sum1 sum2 squared rooted inverted out_set".split()
        e = {n: b.sem("fin_" + n) for n in names}
        const = b.sem("fin_const")
        x_ld = [b.sem(f"fin_x{p}") for p in range(2)]
        r_ld = [b.sem(f"fin_rows{p}") for p in range(2)]
        stored = [b.sem(f"fin_stored{p}") for p in range(2)]
        block = ctx.enter_context(nc.Block())

        @block.sync
        def _(sp):
            sp.dma_start(gf[:, :], dram["final_norm_g"].partition_broadcast(P)).then_inc(const, 16)
            for p in range(2):
                sp.dma_start(x[p][:, :], x2_rows[p * P:(p + 1) * P, :]).then_inc(x_ld[p], 16)
            with sp.Fori(1, NT // 2) as j:
                for p in range(2):
                    t = j * 2 + p
                    sp.wait_ge(e["out_set"], t - 1)
                    sp.dma_start(y[bass.ds(t * P - 2 * P, P), :], r[0][p][:, :]).then_inc(stored[p], 16)
                    sp.dma_start(x[p][:, :], x2_rows[bass.ds(t * P, P), :]).then_inc(x_ld[p], 16)
            for p in range(2):
                sp.wait_ge(e["out_set"], NT - 1 + p)
                sp.dma_start(y[(NT - 2 + p) * P:(NT - 1 + p) * P, :], r[0][p][:, :]).then_inc(stored[p], 16)
            for p in range(2):
                sp.wait_ge(stored[p], 8 * NT)

        @block.gpsimd
        def _(pool):
            def rows(p, t):
                pool.tensor_copy(ix[p][:, :], slot[:, :, bass.ds(t, 1)].rearrange("p c a -> p (c a)")).then_inc(e["ix_set"], 1)
                pool.wait_ge(e["ix_set"], t + 1)
                pool.sem_inc(e["gathers_begun"], 1)
                for c in range(2):
                    pool.indirect_dma_start(out=r[c][p][:, :], out_offset=None, in_=y_rows[:, :],
                                            in_offset=bass.IndirectOffsetOnAxis(ap=ix[p][:, c:c + 1], axis=0)).then_inc(r_ld[p], 16)

            for p in range(2):
                rows(p, p)
            with pool.Fori(1, NT // 2) as j:
                for p in range(2):
                    pool.wait_ge(stored[p], j * 16)
                    rows(p, j * 2 + p)

        @block.vector
        def _(dve):
            dve.wait_ge(const, 16)
            with dve.Fori(0, NT // 2) as j:
                for p in range(2):
                    t = j * 2 + p
                    dve.wait_ge(x_ld[p], j * 16 + 16)
                    dve.wait_ge(r_ld[p], j * 32 + 32)
                    g = [gate[:, c, bass.ds(t, 1)] for c in range(2)]
                    dve.scalar_tensor_tensor(out=x[p][:, :], in0=r[0][p][:, :], scalar=g[0], in1=x[p][:, :],
                                             op0=ALU.mult, op1=ALU.add).then_inc(e["sum1"], 1)
                    dve.wait_ge(e["sum1"], t + 1)
                    dve.scalar_tensor_tensor(out=x[p][:, :], in0=r[1][p][:, :], scalar=g[1], in1=x[p][:, :],
                                             op0=ALU.mult, op1=ALU.add).then_inc(e["sum2"], 1)
                    dve.wait_ge(e["rooted"], t + 1)
                    dve.reciprocal(ri[p][:, :], rt[p][:, :]).then_inc(e["inverted"], 1)
                    dve.wait_ge(e["inverted"], t + 1)
                    dve.scalar_tensor_tensor(out=r[0][p][:, :], in0=x[p][:, :], scalar=ri[p][:, :], in1=gf[:, :],
                                             op0=ALU.mult, op1=ALU.mult).then_inc(e["out_set"], 1)

        @block.scalar
        def _(act):
            with act.Fori(0, NT // 2) as j:
                for p in range(2):
                    t = j * 2 + p
                    act.wait_ge(e["sum2"], t + 1)
                    act.activation(junk[:, :], x[p][:, :], ACT.Square, accum_out=ss[p][:, :]).then_inc(e["squared"], 1)
                    act.wait_ge(e["squared"], t + 1)
                    act.activation(rt[p][:, :], ss[p][:, :], ACT.Sqrt, bias=k["eps"][:, :], scale=1.0 / D).then_inc(e["rooted"], 1)


def encoder(nc, dram, y):
    with ExitStack() as ctx:
        b = Bufs(nc, ctx)
        k = {
            "ident": b.sb("ident", [P, P]), "ones": b.sb("ones", [P, P]), "group": b.sb("group", [P, P]),
            "tri": b.sb("tri", [P, 2, P]), "neg": b.sb("neg", [P, 2, P]), "lower": b.sb("lower", [P, P]),
            "lvl": b.sb("lvl", [P, 2, LEVELS, P]), "g1": b.sb("g1", [P, D]),
            "cw_mix": b.sb("cw_mix", [P, CONV_TILES, 3]), "cg_mix": b.sb("cg_mix", [P, CONV_TILES]),
            "cw_qkv": b.sb("cw_qkv", [P, 3 * HEADS, 3]), "alog": b.sb("alog", [P, 2 * HEADS]),
            "dtb": b.sb("dtb", [P, 2 * HEADS]),
            "eps": b.sb("eps", [P, 1]), "eps128": b.sb("eps128", [P, 1]), "one": b.sb("one", [P, 1]),
        }
        feat = nc.dram_tensor("feat", (20, P, T), F32).ap()
        constants(nc, k, dram)
        ab_rows = nc.dram_tensor("ab_rows", (16, T), F32).ap()
        with ExitStack() as c2:
            hT = Bufs(nc, c2).sb("hT", [P, KD, T])
            with nc.cleanup_on_exit():
                normalise(nc, k, dram, hT)
            with nc.cleanup_on_exit():
                project(nc, k, dram, hT, feat, ab_rows)
        gates = b.sb("gates", [P, 2, NT, 5 * HEADS])
        decays(nc, k, ab_rows, gates)
        lg = b.sb("lg", [P, NT, NG + NE])
        x2_rows = nc.dram_tensor("x2_rows", (T, D), F32).ap()
        xn_rows = nc.dram_tensor("xn_rows", (T, D), F32).ap()
        y_rows = nc.dram_tensor("y_rows", (SLOTS, D), F32).ap()
        slot_rows = nc.dram_tensor("slot_rows", (SLOTS + 2 * P, 1), I32).ap()
        with ExitStack() as c2:
            O = Bufs(nc, c2).sb("O", [P, NT, HEADS * P])
            with nc.cleanup_on_exit():
                delta(nc, k, gates, feat, O)
            with nc.cleanup_on_exit():
                output(nc, k, dram, feat, O, lg, x2_rows, xn_rows)
        gate, slot = b.sb("gate", [P, 2, NT]), b.sb("slot", [P, 2, NT], I32)
        table, idx = b.sb("table", [P, 2 * MAXB + NE + 1], I32), b.sb("idx", [P, MAXB + 2], I32)
        route(nc, k, lg, gate, slot, table, idx, slot_rows)
        experts(nc, k, dram, table, idx, xn_rows, y_rows)
        combine(nc, k, dram, gate, slot, x2_rows, y_rows, y)


def lay_out(inputs):
    a = {name: np.asarray(v) for name, v in inputs.items()}
    w_in = a["w_in"][0]
    start = {"b": 0, "c": 512, "h": 1024, "q": 1536, "k": 2048, "v": 2560, "z": 3072}
    tiles = [w_in[:, start[job] + g * P:start[job] + (g + 1) * P] for g in range(HEADS) for job in JOBS]
    by_tap = lambda w: w.reshape(3, -1, P).transpose(2, 1, 0)
    return {
        "x": np.concatenate([a["x_prompt"][0], a["x_sample"][0]], 0),
        "w_tiles": np.stack(tiles).reshape(len(tiles), KD, P, P).transpose(0, 2, 1, 3),
        "w_ab": w_in[:, 3584:].reshape(KD, P, 4 * HEADS).transpose(1, 0, 2),
        "norm1_g": a["norm1_g"][0],
        "conv_a_w": by_tap(a["conv_a_w"][0]),
        "conv_a_norm_g": a["conv_a_norm_g"][0].reshape(CONV_TILES, P).T,
        "dn_conv_w": by_tap(a["dn_conv_w"][0]),
        "dn_a_log": a["dn_a_log"][0].reshape(-1),
        "dn_dt_bias": a["dn_dt_bias"][0].reshape(-1),
        "dn_norm_g": a["dn_norm_g"][0].reshape(P, 1),
        "w_o": a["w_o"][0],
        "norm2_g": a["norm2_g"][0],
        "router_w": np.concatenate([a["router_group_w"][0], a["router_expert_w"][0]], 1),
        "router_b": np.concatenate([a["router_group_b"][0], a["router_expert_b"][0]]),
        "w1": a["w1"][0], "w3": a["w3"][0], "w2": a["w2"][0],
        "final_norm_g": a["final_norm_g"],
    }


def kernel(**inputs):
    import concourse.bacc as bacc
    from concourse.bass_utils import run_bass_kernel_spmd

    nc = bacc.Bacc("TRN2", target_bir_lowering=False, num_devices=1)
    arrays, dram = {}, {}
    for name, array in lay_out(inputs).items():
        arrays[f"in_{name}_dram"] = np.ascontiguousarray(array)
        dram[name] = nc.dram_tensor(f"in_{name}_dram", array.shape, mybir.dt.from_np(array.dtype), kind="ExternalInput").ap()
    y = nc.dram_tensor("out_0_dram", (T, D), F32, kind="ExternalOutput").ap()
    encoder(nc, dram, y)
    r = run_bass_kernel_spmd(nc, [arrays], core_ids=[0])
    rows = r.results[0]["out_0_dram"]
    return rows[None, :LONG], rows[None, LONG:]
```

```python
from contextlib import ExitStack

import numpy as np

import concourse.bass as bass
from concourse import mybir

F32 = mybir.dt.float32
F32R = mybir.dt.float32r
I32 = mybir.dt.int32
ALU = mybir.AluOpType
ACT = mybir.ActivationFunctionType
AX = mybir.AxisListType

P = 128
LONG, SHORT = 2048, 256
T = LONG + SHORT
NT = T // P
LT_TILES = LONG // P
D = 1024
KD = D // P
HEADS = 4
CONV_TILES = 4
EPS = 1e-6
PADW = T + 3
SEG = ((0, 1, LONG), (LONG, LONG + 2, SHORT))
NCH = 6
CH = T // NCH
JOBS = "chbqzkv"
NG, EPG, NE, FF = 4, 8, 32, 512
MAXB = (2 * T + NE * (P - 1)) // P
MAXB += 1 - MAXB % 2
SLOTS = MAXB * P
LEVELS = 7


def bcast(ap, n, axis):
    v = ap.unsqueeze(axis)
    shape = list(v.shape)
    shape[axis] = n
    return v.broadcast_to(shape)


class Bufs:

    def __init__(self, nc, ctx, phase=""):
        self.nc, self.ctx, self.phase = nc, ctx, phase

    def sb(self, name, shape, dt=F32):
        return self.ctx.enter_context(self.nc.sbuf_tensor(self.phase + name, shape, dt))

    def ps(self, name, shape):
        return self.ctx.enter_context(self.nc.psum_tensor(self.phase + name, shape, F32))

    def sem(self, name):
        return self.nc.alloc_semaphore(name=self.phase + name)


def over(nc, b, names, shape):
    with ExitStack() as first:
        whole = [Bufs(nc, first, b.phase).sb(f"{n}_whole", shape) for n in names]
    return whole, [b.sb(f"{n}_low", shape, F32R) for n in names]


def pieces(c):
    out = []
    for t0, p0, n in SEG:
        a, b = max(c * CH, t0), min((c + 1) * CH, t0 + n)
        if a < b:
            out.append((a - c * CH, p0 + a - t0, b - a))
    return out


def constants(nc, k, dram):
    with ExitStack() as ctx:
        b = Bufs(nc, ctx, "constants_")
        cleared, loaded = b.sem("ident_cleared"), b.sem("gain_loaded")
        block = ctx.enter_context(nc.Block())

        @block.sync
        def _(sp):
            sp.dma_start(k["g1"][:, :], dram["norm1_g"].partition_broadcast(P)).then_inc(loaded, 16)
            sp.wait_ge(loaded, 16)

        @block.vector
        def _(dve):
            dve.memset(k["eps"][:, :], EPS)
            dve.memset(k["eps128"][:, :], EPS * P)
            dve.memset(k["one"][:, :], 1.0)

        @block.gpsimd
        def _(pool):
            pool.memset(k["ident"][:, :], 0.0).then_inc(cleared, 1)
            pool.wait_ge(cleared, 1)
            pool.affine_select(out=k["ident"][:, :], in_=k["ident"][:, :], compare_op=ALU.not_equal, fill=1.0,
                               base=0, pattern=[[-1, P]], channel_multiplier=1)


def small_inputs(sp, k, dram, small):
    n = 0
    for dst, src in (
        (k["cw_mix"][:, :, :], dram["conv_a_w"]),
        (k["cg_mix"][:, :], dram["conv_a_norm_g"]),
        (k["cw_qkv"][:, :, :], dram["dn_conv_w"]),
        (k["alog"][:, :], dram["dn_a_log"].partition_broadcast(P)),
        (k["dtb"][:, :], dram["dn_dt_bias"].partition_broadcast(P)),
    ):
        sp.dma_start(dst, src).then_inc(small, 16)
        n += 16
    sp.wait_ge(small, n)


def masks(pool, k, set0, sel):
    fills = [(k["ones"], 1.0), (k["tri"], 1.0), (k["neg"], 0.0), (k["lower"], 1.0), (k["group"], 1.0), (k["lvl"], 0.0)]
    for buf, v in fills:
        pool.memset(buf[:], v).then_inc(set0, 1)
    n = len(fills)
    pool.wait_ge(set0, n)
    halves = k["group"][:, :].rearrange("p (b r) -> p b r", b=2)
    pool.affine_select(out=halves, in_=halves, compare_op=ALU.is_ge, fill=0.0, base=0,
                       pattern=[[-64, 2], [0, 64]], channel_multiplier=1).then_inc(sel, 1)
    pool.wait_ge(sel, 1)
    pool.affine_select(out=halves, in_=halves, compare_op=ALU.is_ge, fill=0.0, base=63,
                       pattern=[[64, 2], [0, 64]], channel_multiplier=-1)
    levels = [(1 << l, d, k["lvl"][:, d, l, :].rearrange("p (b h r) -> p b h r", h=2, r=1 << l)[:, :, 1 - d, :])
              for l in range(LEVELS) for d in range(2)]
    for s, d, v in levels:
        pool.memset(v, 1.0).then_inc(set0, 1)
    pool.wait_ge(set0, n + len(levels))
    for s, d, v in levels:
        pool.affine_select(out=v, in_=v, compare_op=ALU.is_ge, fill=0.0, base=-s * d,
                           pattern=[[-2 * s, P // (2 * s)], [0, s]], channel_multiplier=1).then_inc(sel, 1)
    pool.wait_ge(sel, len(levels) + 1)
    for s, d, v in levels:
        pool.affine_select(out=v, in_=v, compare_op=ALU.is_ge, fill=0.0, base=s * d + s - 1,
                           pattern=[[2 * s, P // (2 * s)], [0, s]], channel_multiplier=-1)
    for buf, fill in ((k["tri"], 0.0), (k["neg"], -1e30)):
        for d, sign in ((0, 1), (1, -1)):
            pool.affine_select(out=buf[:, d, :], in_=buf[:, d, :], compare_op=ALU.is_ge, fill=fill,
                               base=0, pattern=[[sign, P]], channel_multiplier=-sign)
    pool.affine_select(out=k["lower"][:, :], in_=k["lower"][:, :], compare_op=ALU.is_gt, fill=0.0,
                       base=0, pattern=[[1, P]], channel_multiplier=-1)


def normalise(nc, k, dram, hT):
    with ExitStack() as ctx:
        b = Bufs(nc, ctx, "normalise_")
        U = 3
        ring = lambda name, shape: [b.sb(f"{name}{p}", shape) for p in range(U)]
        x, xn = ring("x", [P, D]), ring("xn", [P, D])
        sq = b.sb("sq_junk", [P, D])
        ss, rt, ri = ring("ss", [P, 1]), ring("rt", [P, 1]), ring("ri", [P, 1])
        tp = [[b.ps(f"tp{p}{h}", [P, 4, P]) for h in range(2)] for p in range(U)]
        loaded = [b.sem(f"x_loaded{p}") for p in range(U)]
        summed, rooted, inverted, scaled = b.sem("x_summed"), b.sem("x_rooted"), b.sem("x_inverted"), b.sem("x_scaled")
        turned, copied = b.sem("x_turned"), [b.sem("x_copied0"), b.sem("x_copied1")]
        small, filled, selected = b.sem("small_loaded"), b.sem("masks_filled"), b.sem("masks_selected")
        block = ctx.enter_context(nc.Block())

        def through_tiles(eng, first, last, step):
            with eng.Fori(first, last) as j:
                for p in range(U):
                    step(p, j, j * U + p)

        @block.sync
        def _(sp):
            def load(p, t):
                sp.dma_start(x[p][:, :], dram["x"][bass.ds(t * P, P), :]).then_inc(loaded[p], 16)

            def reload(p, j, t):
                sp.wait_ge(scaled, t - (U - 1))
                load(p, t)

            for p in range(U):
                load(p, p)
            through_tiles(sp, 1, NT // U, reload)
            small_inputs(sp, k, dram, small)

        @block.scalar
        def _(act):
            def root(p, j, t):
                act.wait_ge(loaded[p], j * 16 + 16)
                act.activation(sq[:, :], x[p][:, :], ACT.Square, accum_out=ss[p][:, :]).then_inc(summed, 1)
                act.wait_ge(summed, t + 1)
                act.activation(rt[p][:, :], ss[p][:, :], ACT.Sqrt, bias=k["eps"][:, :], scale=1.0 / D).then_inc(rooted, 1)

            def copy(p, t):
                act.wait_ge(turned, t * 2 + 2)
                act.activation(hT[:, 4:8, bass.ds(t * P, P)], tp[p][1][:, :, :], ACT.Copy).then_inc(copied[1], 1)

            def both(p, j, t):
                root((p + 1) % U, j + (p + 1) // U, t + 1)
                copy(p, t)

            root(0, 0, 0)
            through_tiles(act, 0, NT // U - 1, both)
            for p in range(U):
                t = NT - U + p
                if p + 1 < U:
                    both(p, NT // U - 1, t)
                else:
                    copy(p, t)

        @block.vector
        def _(dve):
            def scale(p, t):
                dve.wait_ge(rooted, t + 1)
                dve.reciprocal(ri[p][:, :], rt[p][:, :]).then_inc(inverted, 1)
                dve.wait_ge(inverted, t + 1)
                dve.scalar_tensor_tensor(out=xn[p][:, :], in0=x[p][:, :], scalar=ri[p][:, :], in1=k["g1"][:, :],
                                         op0=ALU.mult, op1=ALU.mult).then_inc(scaled, 1)

            def copy(p, t):
                dve.wait_ge(turned, t * 2 + 1)
                dve.tensor_copy(hT[:, 0:4, bass.ds(t * P, P)], tp[p][0][:, :, :]).then_inc(copied[0], 1)

            def both(p, j, t):
                scale((p + 1) % U, t + 1)
                copy(p, t)

            scale(0, 0)
            through_tiles(dve, 0, NT // U - 1, both)
            for p in range(U):
                t = NT - U + p
                if p + 1 < U:
                    both(p, NT // U - 1, t)
                else:
                    copy(p, t)

        @block.tensor
        def _(pe):
            def turn(p, j, t, banks_used=True):
                pe.wait_ge(scaled, t + 1)
                for h in range(2):
                    if banks_used:
                        pe.wait_ge(copied[h], t - (U - 1))
                    for c in range(4):
                        m = pe.transpose(tp[p][h][:, c, :], xn[p][:, (4 * h + c) * P:(4 * h + c + 1) * P], k["ident"][:, :])
                    m.then_inc(turned, 1)

            for p in range(U):
                turn(p, 0, p, banks_used=False)
            through_tiles(pe, 1, NT // U, turn)

        @block.gpsimd
        def _(pool):
            masks(pool, k, filled, selected)


def project(nc, k, dram, hT, feat, ab_rows):
    with ExitStack() as ctx:
        b = Bufs(nc, ctx, "project_")
        w = {j: b.sb(f"w_{j}", [P, KD, P]) for j in JOBS}
        gate_c, mix_in, mix = b.sb("gate_c", [P, T]), b.sb("mix_in", [P, PADW]), b.sb("mix", [P, PADW])
        raw = {"q": b.sb("raw_q", [P, PADW]), "k": b.sb("raw_k", [P, PADW])}
        raw["v"] = raw["q"]
        out = {"q": b.sb("conv_q", [P, PADW]), "k": b.sb("conv_k", [P, PADW]), "b": mix}
        out["v"] = out["q"]
        primer = b.sb("primer", [P, 5, CONV_TILES])
        sq, nrm = b.sb("squares", [P, PADW]), b.sb("norms", [P, PADW])
        bank = [b.ps(f"proj{c}", [P, 512]) for c in range(NCH)]
        nbank = [b.ps(f"nsum{c}", [P, 512]) for c in range(2)]
        w_loaded = {j: b.sem(f"w_loaded_{j}") for j in JOBS}
        ready = [b.sem(f"proj_ready{c}") for c in range(NCH)]
        free = [b.sem(f"proj_free{c}") for c in range(NCH)]
        nready = [b.sem(f"nsum_ready{c}") for c in range(2)]
        nfree = [b.sem(f"nsum_free{c}") for c in range(2)]
        padded, ab_ready = b.sem("pads_set"), b.sem("ab_ready")
        conv_done = {j: b.sem(f"conv_done_{j}") for j in "hqkv"}
        act_done = {j: b.sem(f"silu_done_{j}") for j in "qkv"}
        chain = b.sem("conv_taps")
        sq_done = {j: b.sem(f"squares_done_{j}") for j in "bqk"}
        inv_done = {j: b.sem(f"inverse_done_{j}") for j in "bqk"}
        norm_done = {j: b.sem(f"norm_done_{j}") for j in "bqk"}
        stored = {j: b.sem(f"stored_{j}") for j in "bqzkv"}
        block = ctx.enter_context(nc.Block())
        G = CONV_TILES
        body = slice(1, PADW - 1)

        def evacuated(eng, n, g):
            eng.wait_ge(free[NCH - 1], g * 7 + (n + 2))

        def rooted(eng, n, g):
            eng.wait_ge(nfree[1], g * 9 + (3 * n + 4))

        @block.sync
        def _(sp):
            for n, j in enumerate(JOBS):
                sp.dma_start(w[j][:, :, :], dram["w_tiles"][n]).then_inc(w_loaded[j], 16)
            with sp.Fori(1, G) as g:
                for n, j in enumerate(JOBS):
                    sp.wait_ge(ready[NCH - 1], g * 7 + (n + 1 - 7))
                    src = dram["w_tiles"][bass.ds(g * 7 + n, 1)].rearrange("a p k m -> (a p) k m")
                    sp.dma_start(w[j][:, :, :], src).then_inc(w_loaded[j], 16)
            sp.wait_ge(ready[NCH - 1], 7 * G - 6)
            sp.dma_start(w["c"][:, :, 0:16], dram["w_ab"]).then_inc(w_loaded["c"], 16)

        @block.tensor
        def _(pe):
            def job(n, j, g):
                pe.wait_ge(w_loaded[j], g * 16 + 16)
                for c in range(NCH):
                    pe.wait_ge(free[c], g * 7 + (n + 1))
                    for kt in range(KD):
                        m = pe.matmul(bank[c][:, 0:CH], w[j][:, kt, :], hT[:, kt, c * CH:(c + 1) * CH],
                                      start=kt == 0, stop=kt == KD - 1)
                    m.then_inc(ready[c], 1)

            def sums(n, j, g, weights):
                pe.wait_ge(sq_done[j], g + 1)
                for c in range(NCH):
                    pe.wait_ge(nfree[c % 2], g * 9 + (3 * n + c // 2 + 1))
                    for a, at, ln in pieces(c):
                        m = pe.matmul(nbank[c % 2][:, a:a + ln], weights, sq[:, at:at + ln], start=a == 0, stop=True,
                                      skip_group_check=True)
                    m.then_inc(nready[c % 2], 1)

            with pe.Fori(0, G) as g:
                job(0, "c", g)
                job(1, "h", g)
                job(2, "b", g)
                job(3, "q", g)
                sums(0, "b", g, k["group"][:, :])
                job(4, "z", g)
                sums(1, "q", g, k["ones"][:, :])
                job(5, "k", g)
                job(6, "v", g)
                sums(2, "k", g, k["ones"][:, :])
            pe.wait_ge(w_loaded["c"], 16 * (G + 1))
            for c in range(NCH):
                pe.wait_ge(free[c], 7 * G + 1)
                for kt in range(KD):
                    m = pe.matmul(bank[c][0:16, 0:CH], w["c"][:, kt, 0:16], hT[:, kt, c * CH:(c + 1) * CH],
                                  start=kt == 0, stop=kt == KD - 1)
                m.then_inc(ready[c], 1)

        @block.scalar
        def _(act):
            def evacuate(n, j, g, dst, func, pad):
                for c in range(NCH):
                    act.wait_ge(ready[c], g * 7 + (n + 1))
                    for a, at, ln in pieces(c):
                        at = at if pad else c * CH + a
                        m = act.activation(dst[:, at:at + ln], bank[c][:, a:a + ln], func)
                    m.then_inc(free[c], 1)

            def square(j, src):
                act.activation(sq[:, body], src[:, body], ACT.Square).then_inc(sq_done[j], 1)

            def roots(n, g, scale, bias):
                for c in range(NCH):
                    act.wait_ge(nready[c % 2], g * 9 + (3 * n + c // 2 + 1))
                    for a, at, ln in pieces(c):
                        m = act.activation(nrm[:, at:at + ln], nbank[c % 2][:, a:a + ln], ACT.Sqrt, bias=bias, scale=scale)
                    m.then_inc(nfree[c % 2], 1)

            def silu(j):
                act.activation(out[j][:, body], out[j][:, body], ACT.Silu).then_inc(act_done[j], 1)

            act.wait_ge(padded, 4)
            with act.Fori(0, G) as g:
                act.wait_ge(stored["z"], g * 16 + 16)
                evacuate(0, "c", g, gate_c, ACT.Copy, False)
                evacuated(act, 2, g)
                square("b", mix)
                act.wait_ge(conv_done["v"], g + 1)
                evacuate(3, "q", g, raw["q"], ACT.Copy, True)
                roots(0, g, 1.0 / 64, k["eps"][:, :])
                act.wait_ge(conv_done["q"], g + 1)
                silu("q")
                act.wait_ge(act_done["q"], g + 1)
                square("q", out["q"])
                evacuate(4, "z", g, gate_c, ACT.Silu, False)
                act.wait_ge(norm_done["b"], g + 1)
                roots(1, g, float(P), k["eps128"][:, :])
                act.wait_ge(conv_done["k"], g + 1)
                evacuate(5, "k", g, raw["k"], ACT.Copy, True)
                act.wait_ge(conv_done["k"], g + 2)
                silu("k")
                act.wait_ge(act_done["k"], g + 1)
                square("k", out["k"])
                evacuate(6, "v", g, raw["v"], ACT.Copy, True)
                act.wait_ge(norm_done["q"], g + 1)
                roots(2, g, 1.0, k["eps"][:, :])
                act.wait_ge(conv_done["v"], g + 2)
                silu("v")
                act.wait_ge(norm_done["k"], g + 1)
            act.wait_ge(stored["z"], 16 * G + 16)
            for c in range(NCH):
                act.wait_ge(ready[c], 7 * G + 1)
                m = act.activation(gate_c[0:16, c * CH:(c + 1) * CH], bank[c][0:16, 0:CH], ACT.Copy)
            m.then_inc(ab_ready, 1)

        def silu_k_after(act, g, silu, square):
            act.wait_ge(conv_done["k"], g + 2)
            act.activation(out["k"][:, body], out["k"][:, body], ACT.Silu).then_inc(act_done["k"], 1)
            square("k", g, out["k"], act_done["k"], g + 1)

        @block.vector
        def _(dve):
            for buf in (mix_in, raw["q"], raw["k"], nrm):
                dve.memset(buf[:, :], 0.0 if buf is not nrm else 1.0).then_inc(padded, 1)
            dve.wait_ge(padded, 4)
            for sem in free + nfree + [conv_done["k"], conv_done["v"]]:
                dve.sem_inc(sem, 1)

            def conv(j, g, src, dst, wts, n):
                dve.tensor_scalar(dst[:, body], src[:, 0:PADW - 2], wts[0], None, ALU.mult).then_inc(chain, 1)
                dve.wait_ge(chain, g * 8 + (2 * n + 1))
                dve.scalar_tensor_tensor(out=dst[:, body], in0=src[:, 1:PADW - 1], scalar=wts[1], in1=dst[:, body],
                                         op0=ALU.mult, op1=ALU.add).then_inc(chain, 1)
                dve.wait_ge(chain, g * 8 + (2 * n + 2))
                dve.scalar_tensor_tensor(out=dst[:, body], in0=src[:, 2:PADW], scalar=wts[2], in1=dst[:, body],
                                         op0=ALU.mult, op1=ALU.add).then_inc(conv_done[j], 1)

            def norm(n, j, g, gain):
                rooted(dve, n, g)
                dve.reciprocal(nrm[:, body], nrm[:, body]).then_inc(inv_done[j], 1)
                dve.wait_ge(inv_done[j], g + 1)
                if gain is None:
                    m = dve.tensor_tensor(out[j][:, body], out[j][:, body], nrm[:, body], ALU.mult)
                else:
                    m = dve.scalar_tensor_tensor(out=out[j][:, body], in0=out[j][:, body], scalar=gain, in1=nrm[:, body],
                                                 op0=ALU.mult, op1=ALU.mult)
                m.then_inc(norm_done[j], 1)

            def taps(table, at):
                return [table[:, bass.ds(at, 1), n:n + 1].rearrange("p a b -> p (a b)") for n in range(3)]

            with dve.Fori(0, G) as g:
                evacuated(dve, 0, g)
                for c in range(NCH):
                    dve.wait_ge(ready[c], g * 7 + 2)
                    for a, at, ln in pieces(c):
                        m = dve.tensor_tensor(mix_in[:, at:at + ln], bank[c][:, a:a + ln],
                                              gate_c[:, c * CH + a:c * CH + a + ln], ALU.mult)
                    m.then_inc(free[c], 1)
                evacuated(dve, 1, g)
                dve.wait_ge(stored["b"], g * 32 + 32)
                conv("h", g, mix_in, mix, taps(k["cw_mix"], g), 0)
                dve.wait_ge(conv_done["h"], g + 1)
                for c in range(NCH):
                    dve.wait_ge(ready[c], g * 7 + 3)
                    for a, at, ln in pieces(c):
                        m = dve.tensor_tensor(mix[:, at:at + ln], bank[c][:, a:a + ln], mix[:, at:at + ln], ALU.mult)
                    m.then_inc(free[c], 1)
                evacuated(dve, 3, g)
                dve.wait_ge(stored["v"], g * 32 + 32)
                conv("q", g, raw["q"], out["q"], taps(k["cw_qkv"], g), 1)
                norm(0, "b", g, k["cg_mix"][:, bass.ds(g, 1)])
                norm(1, "q", g, None)
                evacuated(dve, 5, g)
                dve.wait_ge(stored["k"], g * 32 + 32)
                conv("k", g, raw["k"], out["k"], taps(k["cw_qkv"], g + HEADS), 2)
                evacuated(dve, 6, g)
                dve.wait_ge(stored["q"], g * 32 + 64)
                conv("v", g, raw["v"], out["v"], taps(k["cw_qkv"], g + 2 * HEADS), 3)
                norm(2, "k", g, None)

        @block.gpsimd
        def _(pool):
            def store(j, row, src):
                dst = feat[bass.ds(row, 1)].rearrange("a p t -> (a p) t")
                for t0, p0, n in SEG:
                    pool.dma_start(dst[:, t0:t0 + n], src[:, p0:p0 + n]).then_inc(stored[j], 16)

            for j in "bqzkv":
                for _ in range(1 if j == "z" else 2):
                    pool.dma_start(primer[:, "bqzkv".index(j), :], dram["conv_a_norm_g"]).then_inc(stored[j], 16)
                    pool.wait_ge(stored[j], 16)
            with pool.Fori(0, G) as g:
                pool.wait_ge(norm_done["b"], g + 1)
                store("b", g + 16, mix)
                evacuated(pool, 4, g)
                pool.dma_start(feat[bass.ds(g + 12, 1)].rearrange("a p t -> (a p) t"), gate_c[:, :]).then_inc(stored["z"], 16)
                pool.wait_ge(norm_done["q"], g + 1)
                store("q", g, out["q"])
                pool.wait_ge(act_done["v"], g + 1)
                store("v", g + 8, out["v"])
                pool.wait_ge(norm_done["k"], g + 1)
                store("k", g + 4, out["k"])
            pool.wait_ge(ab_ready, 1)
            pool.dma_start(ab_rows, gate_c[0:16, :]).then_inc(stored["z"], 16)
            pool.wait_ge(stored["z"], 16 * G + 32)
            for j in "bqkv":
                pool.wait_ge(stored[j], 32 * G + 32)


def decays(nc, k, ab_rows, gates):
    with ExitStack() as ctx:
        b = Bufs(nc, ctx, "decays_")
        abT, ab = b.sb("abT", [16, T]), b.sb("ab", [P, NT, 4 * HEADS])
        loaded = b.sem("ab_loaded")
        x, nx = b.sb("ab_x", [P, NT, 8]), b.sb("ab_nx", [P, NT, 8])
        ex, lg = b.sb("ab_exp", [P, NT, 8]), b.sb("ab_log", [P, NT, 8])
        eb, eb1, rate = b.sb("ab_eb", [P, NT, 8]), b.sb("ab_eb1", [P, NT, 8]), b.sb("rate", [P, 8])
        gg = b.sb("ab_g", [P, 2, NT, HEADS])
        tail = b.sb("ab_tail", [P, 2, NT, HEADS])
        pab = b.ps("pab", [P, NT * 4 * HEADS])
        pg = [b.ps(f"pg{d}", [P, 2, NT, HEADS]) for d in range(2)]
        turned, dv, ac, g_done, sums = b.sem("ab_turned"), b.sem("ab_vector"), b.sem("ab_scalar"), b.sem("ab_g_done"), b.sem("ab_sums")
        block = ctx.enter_context(nc.Block())

        @block.sync
        def _(sp):
            sp.dma_start(abT[:, :], ab_rows).then_inc(loaded, 16)

        @block.tensor
        def _(pe):
            pe.wait_ge(loaded, 16)
            for t in range(NT):
                m = pe.transpose(pab[:, t * 16:(t + 1) * 16], abT[0:16, t * P:(t + 1) * P], k["ident"][0:16, 0:16])
            m.then_inc(turned, 1)
            pe.wait_ge(g_done, 2)
            for d in range(2):
                pe.matmul(pg[d][:, 0], k["tri"][:, d, :], gg[:, d], start=True, stop=True, skip_group_check=True)
                m = pe.matmul(pg[d][:, 1], k["ones"][:, :], gg[:, d], start=False, stop=True, skip_group_check=True)
            m.then_inc(sums, 1)

        @block.vector
        def _(dve):
            n = [0]

            def link(m):
                n[0] += 1
                m.then_inc(dv, 1)
                dve.wait_ge(dv, n[0])

            dve.wait_ge(turned, 1)
            link(dve.tensor_copy(ab[:, :, :], pab[:, :].rearrange("p (t c) -> p t c", c=16)))
            link(dve.tensor_tensor(x[:, :, :], ab[:, :, 0:8], bcast(k["dtb"][:, :], NT, 1), ALU.add))
            link(dve.tensor_scalar(nx[:, :, :], x[:, :, :], -1.0, None, ALU.mult))
            link(dve.tensor_tensor(nx[:, :, :], nx[:, :, :], x[:, :, :], ALU.min))
            dve.wait_ge(ac, 4)
            link(dve.scalar_tensor_tensor(out=x[:, :, :], in0=x[:, :, :], scalar=0.0, in1=lg[:, :, :], op0=ALU.max, op1=ALU.add))
            for d in range(2):
                dve.scalar_tensor_tensor(out=gg[:, d], in0=x[:, :, 4 * d:4 * d + 4], scalar=-1.0,
                                         in1=bcast(rate[:, 4 * d:4 * d + 4], NT, 1), op0=ALU.mult, op1=ALU.mult).then_inc(g_done, 1)
            dve.wait_ge(g_done, 2)
            link(dve.tensor_scalar(eb1[:, :, :], eb[:, :, :], 1.0, None, ALU.add))
            for d in range(2):
                dve.tensor_copy(gates[:, d, :, 16:20], gg[:, d])
                dve.reciprocal(gates[:, d, :, 4:8], eb1[:, :, 4 * d:4 * d + 4])
            dve.wait_ge(sums, 1)
            for d in range(2):
                link(dve.tensor_copy(gates[:, d, :, 0:4], pg[d][:, 0]))
                link(dve.tensor_tensor(tail[:, d], pg[d][:, 1], gates[:, d, :, 0:4], ALU.subtract))

        @block.scalar
        def _(act):
            act.activation(rate[:, :], k["alog"][:, :], ACT.Exp).then_inc(ac, 1)
            act.wait_ge(dv, 4)
            act.activation(ex[:, :, :], nx[:, :, :], ACT.Exp).then_inc(ac, 1)
            act.activation(eb[:, :, :], ab[:, :, 8:16], ACT.Exp, scale=-1.0).then_inc(ac, 1)
            act.wait_ge(ac, 3)
            act.activation(lg[:, :, :], ex[:, :, :], ACT.Ln, bias=k["one"][:, :]).then_inc(ac, 1)
            act.wait_ge(dv, 10)
            for d in range(2):
                act.activation(gates[:, d, :, 8:12], tail[:, d], ACT.Exp)
                act.activation(gates[:, d, :, 12:16], pg[d][:, 1], ACT.Exp)


def delta(nc, k, gates, feat, O):
    with ExitStack() as ctx:
        b = Bufs(nc, ctx, "delta_")
        L = []
        for d in range(2):
            v = {n: b.sb(f"{n}{d}", [P, HEADS, P]) for n in "dg eg diff dec lt Tm X rv vn S".split()}
            for n in "keT qdT kdec vtok qkT R".split():
                v[n] = [b.sb(f"{n}{d}_{r}", [P, HEADS, P]) for r in range(2)]
            v["gs"] = [b.sb(f"gs{d}_{r}", [P, 20]) for r in range(2)]
            v["in"] = b.sb(f"qkv{d}", [P, 3 * HEADS, P])
            v["M"] = b.sb(f"M{d}", [P, LEVELS, HEADS, P])
            v["A"] = [b.ps(f"prep{d}{n}", [P, HEADS, P]) for n in range(2)]
            v["B"] = [b.ps(f"scan{d}{n}", [P, HEADS, P]) for n in range(2)]
            L.append(v)
        sems = ("loaded gates_set gsum_in gsum kk qk kturned vturned eg_set diff_set masked dec_set lt_set qkT_set keT_set "
                "qdT_set M_set kdec_set vtok_set R_set Tturned T_set X_ready X_set dR_ready kS_ready rv_set Tv_ready vn_set "
                "o_ready o_added kv_ready S_set").split()
        E = [{n: b.sem(f"{n}{d}") for n in sems} for d in range(2)]
        cleared = b.sem("o_cleared")
        block = ctx.enter_context(nc.Block())
        lanes = [(d, L[d], E[d]) for d in range(2)]

        def tile(d, s):
            if isinstance(s, int) and s >= LT_TILES:
                return s if d == 0 else NT - 1 - (s - LT_TILES)
            return s if d == 0 else s * -1 + (LT_TILES - 1)

        def run(eng, step):
            step(0, None, 0)
            with eng.Fori(0, (LT_TILES - 2) // 2) as j:
                step(j * 2 + 1, j * 2, 1)
                step(j * 2 + 2, j * 2 + 1, 0)
            for a in range(LT_TILES - 1, NT):
                step(a, a - 1, a % 2)
            step(None, NT - 1, 0)

        def state(c):
            return c + 2 if isinstance(c, int) and c >= LT_TILES else c + 1

        @block.sync
        def _(sp):
            def step(a, c, r):
                if a is None:
                    return
                for d, v, e in lanes:
                    wait_if_any(sp, e["qdT_set"], a)
                    wait_if_any(sp, e["qk"], a)
                    sp.dma_start(v["in"][:, :, :], feat[0:3 * HEADS, :, bass.ds(tile(d, a) * P, P)]
                                 .rearrange("c p t -> p c t")).then_inc(e["loaded"], 16)

            run(sp, step)

        @block.gpsimd
        def _(pool):
            def decays(a, r):
                for d, v, e in lanes:
                    pool.wait_ge(e["gates_set"], a + 1)
                    wait_if_any(pool, e["gsum"], a)
                    pool.tensor_tensor(v["dg"][:, :, :], bcast(k["tri"][:, d, :], HEADS, 1), bcast(v["gs"][r][:, 16:20], P, 2),
                                       ALU.mult).then_inc(e["gsum_in"], 1)

            def step(a, c, r):
                if a is None:
                    return
                for d, v, e in lanes:
                    pool.wait_ge(e["diff_set"], a + 1)
                    pool.tensor_tensor(v["diff"][:, :, :], v["diff"][:, :, :], bcast(k["neg"][:, d, :], HEADS, 1),
                                       ALU.add).then_inc(e["masked"], 1)
                for l in range(LEVELS):
                    for d, v, e in lanes:
                        if l == 0:
                            wait_if_any(pool, e["X_ready"], a * 6)
                            pool.wait_ge(e["lt_set"], a + 1)
                        pool.tensor_tensor(v["M"][:, l], v["lt"][:, :, :], bcast(k["lvl"][:, d, l, :], HEADS, 1),
                                           ALU.mult).then_inc(e["M_set"], 1)
                for d, v, e in lanes:
                    pool.wait_ge(e["eg_set"], a + 1)
                    if not isinstance(a, int) or a >= 2:
                        pool.wait_ge(e["o_ready"], c)
                    pool.tensor_tensor(v["keT"][r][:, :, :], v["in"][:, HEADS:2 * HEADS, :], v["eg"][:, :, :], ALU.mult).then_inc(e["keT_set"], 1)
                    pool.tensor_tensor(v["qdT"][r][:, :, :], v["in"][:, 0:HEADS, :], v["eg"][:, :, :], ALU.mult).then_inc(e["qdT_set"], 1)
                if not isinstance(a, int) or a + 1 < NT:
                    decays(a + 1, 1 - r)

            decays(0, 0)
            run(pool, step)

        @block.scalar
        def _(act):
            def step(a, c, r):
                if a is None:
                    return
                for d, v, e in lanes:
                    act.wait_ge(e["gsum"], a + 1)
                    wait_if_any(act, e["qdT_set"], a)
                    act.activation(v["eg"][:, :, :], v["A"][0][:, :, :], ACT.Exp).then_inc(e["eg_set"], 1)
                for d, v, e in lanes:
                    act.wait_ge(e["masked"], a + 1)
                    wait_if_any(act, e["qkT_set"], a)
                    act.activation(v["dec"][:, :, :], v["diff"][:, :, :], ACT.Exp).then_inc(e["dec_set"], 1)
                for d, v, e in lanes:
                    act.wait_ge(e["vturned"], a + 1)
                    if not isinstance(a, int) or a >= 2:
                        act.wait_ge(e["rv_set"], c)
                    act.activation(v["vtok"][r][:, :, :], v["A"][1][:, :, :], ACT.Copy).then_inc(e["vtok_set"], 1)
                for l in range(1, LEVELS):
                    for d, v, e in lanes:
                        act.wait_ge(e["Tturned"], a * 6 + l)
                        act.activation(v["Tm"][:, :, :], v["A"][0][:, :, :], ACT.Copy).then_inc(e["T_set"], 1)
                    for d, v, e in lanes:
                        act.wait_ge(e["X_ready"], a * 6 + l)
                        act.activation(v["X"][:, :, :], v["A"][1][:, :, :], ACT.Copy).then_inc(e["X_set"], 1)

            run(act, step)

        @block.tensor
        def _(pe):
            def by_heads(out, lhsT, rhs, start=True, stop=True):
                for h in range(HEADS):
                    m = pe.matmul(out[:, h], lhsT(h), rhs(h), start=start and h == 0, stop=stop, skip_group_check=True)
                return m

            def turn(out, src):
                for h in range(HEADS):
                    m = pe.transpose(out[:, h], src(h), k["ident"][:, :])
                return m

            def products(a, r, n):
                for d, v, e in lanes:
                    q, kk, vv = (lambda h, o=o: v["in"][:, o * HEADS + h, :] for o in range(3))
                    if n == 0:
                        wait_if_any(pe, e["R_set"], a * 7)
                        pe.wait_ge(e["gsum_in"], a + 1)
                        pe.matmul(v["A"][0][:, :, :], k["ones"][:, :], v["dg"][:, :, :], start=True, stop=True).then_inc(e["gsum"], 1)
                    elif n == 1:
                        pe.wait_ge(e["loaded"], a * 16 + 16)
                        turn(v["A"][1], kk).then_inc(e["kturned"], 1)
                    elif n == 2:
                        pe.wait_ge(e["eg_set"], a + 1)
                        pe.wait_ge(e["diff_set"], a + 1)
                        by_heads(v["A"][0], kk, kk).then_inc(e["kk"], 1)
                    elif n == 3:
                        pe.wait_ge(e["kdec_set"], a + 1)
                        turn(v["A"][1], vv).then_inc(e["vturned"], 1)
                    else:
                        pe.wait_ge(e["vtok_set"], a + 1)
                        by_heads(v["A"][1], kk, q).then_inc(e["qk"], 1)

            def inverse(a, r, l, n):
                for d, v, e in lanes:
                    R = lambda h: v["R"][r][:, h, :]
                    if n == 0:
                        pe.wait_ge(e["R_set"], a * 7 + l)
                        turn(v["A"][0], R).then_inc(e["Tturned"], 1)
                    elif n == 1:
                        pe.wait_ge(e["T_set"], a * 6 + l)
                        pe.wait_ge(e["M_set"], a * 7 + (l + 1))
                        if l == 1:
                            pe.wait_ge(e["qkT_set"], a + 1)
                        by_heads(v["A"][1], lambda h: v["M"][:, l, h, :], lambda h: v["Tm"][:, h, :]).then_inc(e["X_ready"], 1)
                    else:
                        pe.wait_ge(e["X_set"], a * 6 + l)
                        by_heads(v["A"][0], lambda h: v["X"][:, h, :], R).then_inc(e["dR_ready"], 1)

            def scan(c, r, n):
                for d, v, e in lanes:
                    of = lambda name: lambda h: v[name][r][:, h, :]
                    S, rv, vn = (lambda h, x=x: v[x][:, h, :] for x in ("S", "rv", "vn"))
                    if n == 0:
                        pe.wait_ge(e["S_set"], state(c))
                        pe.wait_ge(e["keT_set"], c + 1)
                        by_heads(v["B"][0], of("keT"), S).then_inc(e["kS_ready"], 1)
                    elif n == 1:
                        pe.wait_ge(e["rv_set"], c + 1)
                        pe.wait_ge(e["R_set"], c * 7 + 7)
                        by_heads(v["B"][1], of("R"), rv).then_inc(e["Tv_ready"], 1)
                    elif n == 2:
                        pe.wait_ge(e["qdT_set"], c + 1)
                        by_heads(v["B"][0], of("qdT"), S, stop=False)
                    elif n == 3:
                        pe.wait_ge(e["vn_set"], c + 1)
                        by_heads(v["B"][1], of("kdec"), vn).then_inc(e["kv_ready"], 1)
                    else:
                        by_heads(v["B"][0], of("qkT"), vn, start=False).then_inc(e["o_ready"], 1)

            def step(a, c, r):
                s = (lambda n: scan(c, 1 - r, n)) if c is not None else (lambda n: None)
                if a is None:
                    for n in range(5):
                        s(n)
                    return
                products(a, r, 0)
                products(a, r, 1)
                s(0)
                products(a, r, 2)
                products(a, r, 3)
                s(1)
                products(a, r, 4)
                s(2)
                for l in range(1, LEVELS):
                    inverse(a, r, l, 0)
                    if l == 1:
                        s(3)
                    inverse(a, r, l, 1)
                    if l == 1:
                        s(4)
                    inverse(a, r, l, 2)

            run(pe, step)

        @block.vector
        def _(dve):
            def take_gates(a, r):
                for d, v, e in lanes:
                    if not isinstance(a, int) or a >= 2:
                        dve.wait_ge(e["gsum_in"], a - 1)
                    dve.tensor_copy(v["gs"][r][:, :], gates[:, d, bass.ds(tile(d, a), 1), :]
                                    .rearrange("p a c -> p (a c)")).then_inc(e["gates_set"], 1)

            def residual(c, r):
                for d, v, e in lanes:
                    dve.wait_ge(e["vtok_set"], c + 1)
                    dve.wait_ge(e["kS_ready"], c + 1)
                    dve.tensor_tensor(v["rv"][:, :, :], v["vtok"][r][:, :, :], v["B"][0][:, :, :], ALU.subtract).then_inc(e["rv_set"], 1)

            def new_values(c, r):
                for d, v, e in lanes:
                    dve.wait_ge(e["Tv_ready"], c + 1)
                    dve.tensor_tensor(v["vn"][:, :, :], v["B"][1][:, :, :], bcast(v["gs"][r][:, 4:8], P, 2), ALU.mult).then_inc(e["vn_set"], 1)

            def finish(d, c, r):
                v, e = L[d], E[d]
                dve.wait_ge(e["o_ready"], c + 1)
                wait_if_any(dve, E[1 - d]["o_added"], c)
                out = O[:, bass.ds(tile(d, c), 1), :].rearrange("p a (h c) -> p (a h) c", h=HEADS)
                dve.tensor_tensor(out, v["B"][0][:, :, :], out, ALU.add).then_inc(e["o_added"], 1)
                dve.wait_ge(e["kv_ready"], c + 1)
                dve.wait_ge(e["S_set"], state(c))
                for h in range(HEADS):
                    m = dve.scalar_tensor_tensor(out=v["S"][:, h, :], in0=v["S"][:, h, :], scalar=v["gs"][r][:, 12 + h:13 + h],
                                                 in1=v["B"][1][:, h], op0=ALU.mult, op1=ALU.add)
                m.then_inc(e["S_set"], 1)

            def clear_state(c):
                for d, v, e in lanes:
                    if c:
                        dve.wait_ge(e["S_set"], c + 1)
                    dve.memset(v["S"][:, :, :], 0.0).then_inc(e["S_set"], 1)

            def step(a, c, r):
                if a is None:
                    residual(c, 1 - r)
                    new_values(c, 1 - r)
                    for d in range(2):
                        finish(d, c, 1 - r)
                    return
                if isinstance(c, int) and c == LT_TILES:
                    clear_state(c)
                for d, v, e in lanes:
                    dve.wait_ge(e["gates_set"], a + 1)
                    wait_if_any(dve, e["dec_set"], a)
                    dve.wait_ge(e["eg_set"], a + 1)
                    dve.tensor_tensor(v["diff"][:, :, :], v["A"][0][:, :, :], bcast(v["gs"][r][:, 0:4], P, 2), ALU.subtract).then_inc(e["diff_set"], 1)
                for d, v, e in lanes:
                    dve.wait_ge(e["kturned"], a + 1)
                    dve.tensor_tensor(v["kdec"][r][:, :, :], v["A"][1][:, :, :], bcast(v["gs"][r][:, 8:12], P, 2), ALU.mult).then_inc(e["kdec_set"], 1)
                if c is not None:
                    residual(c, 1 - r)
                for d, v, e in lanes:
                    dve.wait_ge(e["dec_set"], a + 1)
                    dve.wait_ge(e["kk"], a + 1)
                    wait_if_any(dve, e["M_set"], a * 7)
                    for h in range(HEADS):
                        m = dve.scalar_tensor_tensor(out=v["lt"][:, h, :], in0=v["A"][0][:, h], scalar=v["gs"][r][:, 4 + h:5 + h],
                                                     in1=v["dec"][:, h, :], op0=ALU.mult, op1=ALU.mult)
                    m.then_inc(e["lt_set"], 1)
                if c is not None:
                    new_values(c, 1 - r)
                for d, v, e in lanes:
                    dve.wait_ge(e["qk"], a + 1)
                    dve.tensor_tensor(v["qkT"][r][:, :, :], v["A"][1][:, :, :], v["dec"][:, :, :], ALU.mult).then_inc(e["qkT_set"], 1)
                for d, v, e in lanes:
                    dve.wait_ge(e["M_set"], a * 7 + 1)
                    dve.tensor_tensor(v["R"][r][:, :, :], bcast(k["ident"][:, :], HEADS, 1), v["M"][:, 0], ALU.subtract).then_inc(e["R_set"], 1)
                for l in range(1, LEVELS):
                    for d, v, e in lanes:
                        dve.wait_ge(e["R_set"], a * 7 + l)
                        dve.wait_ge(e["dR_ready"], a * 6 + l)
                        dve.tensor_tensor(v["R"][r][:, :, :], v["R"][r][:, :, :], v["A"][0][:, :, :], ALU.subtract).then_inc(e["R_set"], 1)
                    if c is not None and l <= 2:
                        finish(l - 1, c, 1 - r)
                if not isinstance(a, int) or a + 1 < NT:
                    take_gates(a + 1, 1 - r)

            dve.memset(O[:, :, :], 0.0).then_inc(cleared, 1)
            dve.wait_ge(cleared, 1)
            clear_state(0)
            take_gates(0, 0)
            run(dve, step)


def software_pipeline(eng, step):
    for u in range(3):
        step(u % 2, u)
    with eng.Fori(1, (NT - 2) // 2) as j:
        step(1, j * 2 + 1)
        step(0, j * 2 + 2)
    for u in (NT - 1, NT):
        step(u % 2, u)


def parts_of(u):
    if not isinstance(u, int):
        return True, True, True
    return u < NT, u + 1 < NT, u >= 1


def wait_if_any(eng, sem, value):
    if not isinstance(value, int) or value > 0:
        eng.wait_ge(sem, value)


def output(nc, k, dram, feat, O, lg, x2_rows, xn_rows):
    with ExitStack() as ctx:
        b = Bufs(nc, ctx, "output_")
        (wo,), (wl,) = over(nc, b, ("wo",), [P, KD, D])
        wh, g2 = b.sb("wo_high", [P, KD, D], F32R), b.sb("g2", [P, D])
        rw, rb, dg = b.sb("router_w", [P, KD, NG + NE]), b.sb("router_b", [P, NG + NE]), b.sb("dn_gain", [P, 1])
        pair = lambda name, shape, dt=F32: [b.sb(f"{name}{p}", shape, dt) for p in range(2)]
        mh, ml = pair("mixT_high", [P, KD, P], F32R), pair("mixT_low", [P, KD, P], F32R)
        mixT, z, x = pair("mixT", [P, KD, P]), pair("z", [P, HEADS, P]), pair("xres", [P, D])
        on, x2, xn, xT = pair("on", [P, HEADS, P]), pair("x2", [P, D]), pair("xn", [P, D]), pair("xT", [P, KD, P])
        ss, rt, ri = pair("oss", [P, HEADS]), pair("ort", [P, HEADS]), pair("ori", [P, HEADS])
        ss2, rt2, ri2 = pair("xss", [P, 1]), pair("xrt", [P, 1]), pair("xri", [P, 1])
        junk, junk2 = b.sb("junk_o", [P, HEADS, P]), b.sb("junk_x", [P, D])
        tA, lgp = b.ps("on_turned", [P, HEADS, P]), b.ps("logits", [P, 512])
        Y = [b.ps(f"yo{n}", [P, 512]) for n in range(2)]
        tX = [b.ps(f"x_turned{n}", [P, 4, P]) for n in range(2)]
        names = ("o_squared o_rooted o_inverted on_set on_turned mix_set y_ready x2_set x_squared x_rooted x_inverted "
                 "xn_set x_turned xT_set lg_ready lg_set w_high w_split m_high m_split splits_begun").split()
        e = {n: b.sem("out_" + n) for n in names}
        const = b.sem("out_const")
        loaded = [b.sem(f"out_loaded{p}") for p in range(2)]
        x2_st = [b.sem(f"x2_stored{p}") for p in range(2)]
        xn_st = [b.sem(f"xn_stored{p}") for p in range(2)]
        block = ctx.enter_context(nc.Block())
        wo_in = [b.sem(f"wo_loaded{i}") for i in range(KD)]
        CONSTS = 4 * 16

        def through_slot(eng, sem, t, p, each):
            eng.wait_ge(sem, (t - p) * (each // 2) + each)

        @block.sync
        def _(sp):
            def load(p, t):
                cols = bass.ds(t * P, P)
                sp.dma_start(mixT[p][:, 0:4, :], feat[16:20, :, cols].rearrange("c p t -> p c t")).then_inc(loaded[p], 16)
                sp.dma_start(z[p][:, :, :], feat[12:16, :, cols].rearrange("c p t -> p c t")).then_inc(loaded[p], 16)
                sp.dma_start(x[p][:, :], dram["x"][cols, :]).then_inc(loaded[p], 16)

            def store_sum(p, t):
                sp.dma_start(x2_rows[bass.ds(t * P, P), :], x2[p][:, :]).then_inc(x2_st[p], 16)

            def store_normed(p, t):
                sp.dma_start(xn_rows[bass.ds(t * P, P), :], xn[p][:, :]).then_inc(xn_st[p], 16)

            sp.dma_start(dg[:, :], dram["dn_norm_g"]).then_inc(const, 16)
            for p in range(2):
                load(p, p)
            for dst, src in ((g2[:, :], dram["norm2_g"].partition_broadcast(P)),
                             (rw[:, :, :], dram["router_w"].rearrange("(k p) n -> p k n", p=P)),
                             (rb[:, :], dram["router_b"].partition_broadcast(P))):
                sp.dma_start(dst, src).then_inc(const, 16)
            for i in range(KD):
                sp.dma_start(wo[:, i, :], dram["w_o"][i * P:(i + 1) * P, :]).then_inc(wo_in[i], 16)
            with sp.Fori(1, NT // 2) as j:
                for p in range(2):
                    t = j * 2 + p
                    sp.wait_ge(e["x2_set"], t - 1)
                    load(p, t)
                    store_sum(p, t - 2)
                    sp.wait_ge(e["xn_set"], t - 1)
                    store_normed(p, t - 2)
            for p in range(2):
                sp.wait_ge(e["x2_set"], NT - 1 + p)
                store_sum(p, NT - 2 + p)
                sp.wait_ge(e["xn_set"], NT - 1 + p)
                store_normed(p, NT - 2 + p)
            for p in range(2):
                sp.wait_ge(x2_st[p], 8 * NT)
                sp.wait_ge(xn_st[p], 8 * NT)

        @block.scalar
        def _(act):
            def begin(p, t):
                for h in range(HEADS):
                    src = O[:, bass.ds(t, 1), h * P:(h + 1) * P].rearrange("p a c -> p (a c)")
                    m = act.activation(junk[:, h, :], src, ACT.Square, accum_out=ss[p][:, h:h + 1])
                m.then_inc(e["o_squared"], 1)
                act.wait_ge(e["o_squared"], t + 1)
                act.activation(rt[p][:, :], ss[p][:, :], ACT.Sqrt, bias=k["eps"][:, :], scale=1.0 / P).then_inc(e["o_rooted"], 1)

            def step(p, u):
                project_, begin_, end_ = parts_of(u)
                t = u - 1
                if end_:
                    act.wait_ge(e["x2_set"], t + 1)
                    act.activation(junk2[:, :], x2[1 - p][:, :], ACT.Square, accum_out=ss2[1 - p][:, :]).then_inc(e["x_squared"], 1)
                    act.wait_ge(e["x_squared"], t + 1)
                    act.activation(rt2[1 - p][:, :], ss2[1 - p][:, :], ACT.Sqrt, bias=k["eps"][:, :], scale=1.0 / D).then_inc(e["x_rooted"], 1)
                if begin_:
                    begin(1 - p, u + 1)
                if end_:
                    act.wait_ge(e["x_turned"], t + 1)
                    for n in range(2):
                        m = act.activation(xT[1 - p][:, 4 * n:4 * n + 4, :], tX[n][:, :, :], ACT.Copy)
                    m.then_inc(e["xT_set"], 1)

            begin(0, 0)
            for i in range(KD):
                act.wait_ge(wo_in[i], 16)
                act.activation(wh[:, i, :], wo[:, i, :], ACT.Copy).then_inc(e["w_high"], 1)
            software_pipeline(act, step)

        @block.tensor
        def _(pe):
            def begin(p, t):
                pe.wait_ge(e["on_set"], t + 1)
                for h in range(HEADS):
                    m = pe.transpose(tA[:, h], on[p][:, h, :], k["ident"][:, :])
                m.then_inc(e["on_turned"], 1)

            def project_half(p, u, n):
                for kt in range(KD):
                    if n == 0 and isinstance(u, int) and u == 0:
                        pe.wait_ge(e["w_split"], kt + 1)
                    high, low = (t[:, kt, n * 512:(n + 1) * 512] for t in (wh, wl))
                    for i, (x, w) in enumerate(((mh, high), (mh, low), (ml, high))):
                        m = pe.matmul(Y[n][:, :], x[p][:, kt, :], w, start=kt == 0 and i == 0, stop=kt == KD - 1 and i == 2)
                return m

            def step(p, u):
                project_, begin_, end_ = parts_of(u)
                t = u - 1
                if project_:
                    pe.wait_ge(e["m_split"], u * 2 + 2)
                    wait_if_any(pe, e["x2_set"], u)
                    project_half(p, u, 0)
                if begin_:
                    begin(1 - p, u + 1)
                if end_:
                    pe.wait_ge(e["xn_set"], t + 1)
                    wait_if_any(pe, e["xT_set"], t)
                    for c in range(KD):
                        m = pe.transpose(tX[c // 4][:, c % 4, :], xn[1 - p][:, c * P:(c + 1) * P], k["ident"][:, :])
                    m.then_inc(e["x_turned"], 1)
                if project_:
                    project_half(p, u, 1).then_inc(e["y_ready"], 1)
                if end_:
                    pe.wait_ge(e["xT_set"], t + 1)
                    wait_if_any(pe, e["lg_set"], t)
                    for kt in range(KD):
                        m = pe.matmul(lgp[:, 0:NG + NE], xT[1 - p][:, kt, :], rw[:, kt, :], start=kt == 0, stop=kt == KD - 1)
                    m.then_inc(e["lg_ready"], 1)

            begin(0, 0)
            pe.wait_ge(const, CONSTS)
            software_pipeline(pe, step)

        @block.vector
        def _(dve):
            def begin(p, t):
                dve.wait_ge(e["o_rooted"], t + 1)
                dve.reciprocal(ri[p][:, :], rt[p][:, :]).then_inc(e["o_inverted"], 1)
                dve.wait_ge(e["o_inverted"], t + 1)
                src = O[:, bass.ds(t, 1), :].rearrange("p a (h c) -> p (a h) c", h=HEADS)
                dve.tensor_tensor(on[p][:, :, :], src, bcast(ri[p][:, :], P, 2), ALU.mult).then_inc(e["on_set"], 1)

            def gate(p, t):
                dve.wait_ge(e["on_turned"], t + 1)
                through_slot(dve, loaded[p], t, p, 48)
                dve.scalar_tensor_tensor(out=mixT[p][:, 4:8, :], in0=tA[:, :, :], scalar=dg[:, :], in1=z[p][:, :, :],
                                         op0=ALU.mult, op1=ALU.mult).then_inc(e["mix_set"], 1)

            def step(p, u):
                project_, begin_, end_ = parts_of(u)
                t = u - 1
                if end_:
                    dve.wait_ge(e["x_rooted"], t + 1)
                    dve.reciprocal(ri2[1 - p][:, :], rt2[1 - p][:, :]).then_inc(e["x_inverted"], 1)
                    dve.wait_ge(e["x_inverted"], t + 1)
                    wait_if_any(dve, xn_st[1 - p], (t - (1 - p)) * 8)
                    dve.scalar_tensor_tensor(out=xn[1 - p][:, :], in0=x2[1 - p][:, :], scalar=ri2[1 - p][:, :], in1=g2[:, :],
                                             op0=ALU.mult, op1=ALU.mult).then_inc(e["xn_set"], 1)
                if begin_:
                    begin(1 - p, u + 1)
                if begin_:
                    gate(1 - p, u + 1)
                if project_:
                    dve.wait_ge(e["y_ready"], u + 1)
                    wait_if_any(dve, x2_st[p], (u - p) * 8)
                    for n in range(2):
                        m = dve.tensor_tensor(x2[p][:, n * 512:(n + 1) * 512], Y[n][:, :], x[p][:, n * 512:(n + 1) * 512], ALU.add)
                    m.then_inc(e["x2_set"], 1)
                if end_:
                    dve.wait_ge(e["lg_ready"], t + 1)
                    dst = lg[:, bass.ds(t, 1), :].rearrange("p a c -> p (a c)")
                    dve.tensor_tensor(dst, lgp[:, 0:NG + NE], rb[:, :], ALU.add).then_inc(e["lg_set"], 1)

            begin(0, 0)
            dve.wait_ge(const, CONSTS)
            gate(0, 0)
            for i in range(KD):
                dve.wait_ge(e["w_high"], i + 1)
                dve.tensor_tensor(wl[:, i, :], wo[:, i, :], wh[:, i, :].bitcast(F32), ALU.subtract).then_inc(e["w_split"], 1)
            software_pipeline(dve, step)

        @block.gpsimd
        def _(pool):
            def split(p, t):
                for half in range(2):
                    ks = slice(4 * half, 4 * half + 4)
                    if half:
                        pool.wait_ge(e["mix_set"], t + 1)
                    else:
                        through_slot(pool, loaded[p], t, p, 48)
                        if not isinstance(t, int) or t >= 2:
                            pool.wait_ge(e["y_ready"], t - 1)
                    pool.sem_inc(e["splits_begun"], 1)
                    pool.tensor_copy(mh[p][:, ks, :], mixT[p][:, ks, :]).then_inc(e["m_high"], 1)
                    pool.wait_ge(e["m_high"], t * 2 + (half + 1))
                    pool.tensor_tensor(ml[p][:, ks, :], mixT[p][:, ks, :], mh[p][:, ks, :].bitcast(F32), ALU.subtract).then_inc(e["m_split"], 1)

            for p in range(2):
                split(p, p)
            with pool.Fori(1, NT // 2) as j:
                for p in range(2):
                    split(p, j * 2 + p)


def route(nc, k, lg, gate, slot, table, idx):
    with ExitStack() as ctx:
        b = Bufs(nc, ctx, "route_")
        S4, S8 = [P, NT, NG], [P, NT, EPG]
        desc, it128, itb = b.sb("desc", [P, EPG]), b.sb("it128", [P, NT]), b.sb("itb", [P, MAXB + 2])
        tok, itr = b.sb("tok", [P, NT]), b.sb("itr", [P, P])
        mg, m1, m2 = (b.sb(n, [P, NT]) for n in ("mg", "m1", "m2"))
        t4, t8 = b.sb("t4", S4), b.sb("t8", S8)
        hg, h1, h2 = b.sb("hot_group", S4), b.sb("hot1", S8), b.sb("hot2", S8)
        mx4, eg4, sg = b.sb("mx4", S4), b.sb("eg4", S4), b.sb("sg", [P, NT])
        sel, es, ms = b.sb("sel", [P, NT, NG, EPG]), b.sb("es", S8), b.sb("ms", S8)
        dm, ratio, den = (b.sb(n, [P, NT]) for n in ("dm", "ratio", "den"))
        A = [b.sb(f"A{c}", [P, NT, NG, EPG]) for c in range(2)]
        both, pos, prod = b.sb("A_both", [P, NT, NE]), b.sb("pos", [P, NT, NE]), b.sb("prod", [P, NT, NE])
        off = b.sb("off", [P, NT + 1, NE])
        cmp = b.sb("cmp", [P, MAXB * NE])
        nb, cum = b.sb("nblk", [P, NE]), [b.sb(f"cum{i}", [P, NE]) for i in range(2)]
        bx = b.sb("block_expert", [P, MAXB])
        sf = [b.sb(f"slot_f{c}", [P, NT]) for c in range(2)]
        tf = b.sb("table_f", [P, 2 * MAXB + NE + 1])
        row_i = b.sb("slot_row_i", [P, 2, NT], I32)
        row, blk = ([b.sb(f"slot_{n}{c}", [P, NT]) for c in range(2)] for n in ("row", "block"))
        hot_row = [b.sb(f"hot_row{c}", [P, NT, P]) for c in range(2)]
        hot_block = [b.sb(f"hot_block{c}", [P, NT, MAXB + 2]) for c in range(2)]
        H = NT // 2
        rank = [b.ps(f"rank{h}", [P, H, NE]) for h in range(2)]
        tot = [b.ps(f"tot{h}", [P, H, NE]) for h in range(2)]
        idp = b.ps("idx_turned", [P, MAXB + 2])
        dv, ac, pl, pe_s = b.sem("route_vector"), b.sem("route_scalar"), b.sem("route_pool"), b.sem("route_tensor")
        both_set, rows_set, hot_set, hot_blocks_set, placed = (b.sem("route_" + n) for n in
            ("both_set", "rows_set", "hot_set", "hot_blocks_set", "placed"))
        exps_in, dm_in = b.sem("route_exps_in"), b.sem("route_dm_in")
        block = ctx.enter_context(nc.Block())

        @block.gpsimd
        def _(pool):
            pool.iota(itr[:, :], pattern=[[1, P]], base=0, channel_multiplier=0, allow_small_or_imprecise_dtypes=True).then_inc(pl, 1)
            pool.iota(desc[:, :], pattern=[[-1, EPG]], base=EPG, channel_multiplier=0, allow_small_or_imprecise_dtypes=True).then_inc(pl, 1)
            pool.iota(it128[:, :], pattern=[[P, NT]], base=0, channel_multiplier=0, allow_small_or_imprecise_dtypes=True).then_inc(pl, 1)
            pool.iota(itb[:, :], pattern=[[1, MAXB + 2]], base=0, channel_multiplier=0, allow_small_or_imprecise_dtypes=True).then_inc(pl, 1)
            pool.iota(tok[:, :], pattern=[[P, NT]], base=0, channel_multiplier=1, allow_small_or_imprecise_dtypes=True).then_inc(pl, 1)
            pool.wait_ge(pl, 5)
            for c in range(2):
                pool.wait_ge(hot_set, 2 * c + 1)
                pool.tensor_tensor(hot_block[c][:, :, :], hot_block[c][:, :, :], bcast(tok[:, :], MAXB + 2, 2), ALU.mult).then_inc(hot_blocks_set, 1)

        @block.scalar
        def _(act):
            act.wait_ge(exps_in, 1)
            act.activation(eg4[:, :, :], mx4[:, :, :], ACT.Exp).then_inc(ac, 1)
            act.wait_ge(dm_in, 1)
            act.activation(ratio[:, :], dm[:, :], ACT.Exp).then_inc(ac, 1)

        @block.tensor
        def _(pe):
            pe.wait_ge(both_set, 1)
            for h in range(2):
                pe.matmul(rank[h][:, :, :], k["lower"][:, :], both[:, h * H:(h + 1) * H, :], start=True, stop=True)
                m = pe.matmul(tot[h][:, :, :], k["ones"][:, :], both[:, h * H:(h + 1) * H, :], start=True, stop=True)
            m.then_inc(pe_s, 1)
            for c in range(2):
                pe.wait_ge(hot_set, 2 * c + 2)
                pe.wait_ge(hot_blocks_set, c + 1)
                for t in range(NT):
                    m = pe.matmul(idp[:, :], hot_row[c][:, t, :], hot_block[c][:, t, :], start=c + t == 0, stop=c == 1 and t == NT - 1)
            m.then_inc(placed, 1)

        @block.vector
        def _(dve):
            n = [0]

            def link(m):
                n[0] += 1
                m.then_inc(dv, 1)
                dve.wait_ge(dv, n[0])

            def first_max(v, w, top, scores, hot):
                link(dve.tensor_reduce(top[:, :], v, AX.X, ALU.max))
                link(dve.tensor_tensor(scores[:, :, :], v, bcast(top[:, :], w, 2), ALU.is_equal))
                link(dve.tensor_tensor(scores[:, :, :], scores[:, :, :], bcast(desc[:, EPG - w:EPG], NT, 1), ALU.mult))
                link(dve.tensor_reduce(sg[:, :], scores[:, :, :], AX.X, ALU.max))
                link(dve.tensor_tensor(hot[:, :, :], scores[:, :, :], bcast(sg[:, :], w, 2), ALU.is_equal))

            dve.wait_ge(pl, 5)
            groups = lg[:, :, 0:NG]
            first_max(groups, NG, mg, t4, hg)
            dve.tensor_tensor(mx4[:, :, :], groups, bcast(mg[:, :], NG, 2), ALU.subtract).then_inc(exps_in, 1)
            experts = lg[:, :, NG:NG + NE].rearrange("p t (g e) -> p t g e", g=NG)
            link(dve.tensor_tensor(sel[:, :, :, :], experts, bcast(hg[:, :, :], EPG, 3), ALU.mult))
            link(dve.tensor_reduce(es[:, :, :], sel[:, :, :, :].rearrange("p t g e -> p t e g"), AX.X, ALU.add))
            first_max(es[:, :, :], EPG, m1, t8, h1)
            link(dve.scalar_tensor_tensor(out=ms[:, :, :], in0=h1[:, :, :], scalar=-1e30, in1=es[:, :, :], op0=ALU.mult, op1=ALU.add))
            first_max(ms[:, :, :], EPG, m2, t8, h2)
            dve.tensor_tensor(dm[:, :], m2[:, :], m1[:, :], ALU.subtract).then_inc(dm_in, 1)
            for c, h in ((0, h1), (1, h2)):
                link(dve.tensor_tensor(A[c][:, :, :, :], bcast(hg[:, :, :], EPG, 3), bcast(h[:, :, :], NG, 2), ALU.mult))
            flat = [a[:, :, :, :].rearrange("p t g e -> p t (g e)") for a in A]
            dve.tensor_tensor(both[:, :, :], flat[0], flat[1], ALU.add).then_inc(both_set, 1)
            dve.wait_ge(ac, 2)
            link(dve.tensor_reduce(sg[:, :], eg4[:, :, :], AX.X, ALU.add))
            link(dve.tensor_scalar(den[:, :], ratio[:, :], 1.0, None, ALU.add))
            link(dve.tensor_tensor(den[:, :], den[:, :], sg[:, :], ALU.mult))
            link(dve.reciprocal(gate[:, 0, :], den[:, :]))
            link(dve.tensor_tensor(gate[:, 1, :], gate[:, 0, :], ratio[:, :], ALU.mult))
            link(dve.memset(off[:, 0, :], 0.0))
            dve.wait_ge(pe_s, 1)
            for t in range(NT):
                link(dve.tensor_tensor(off[:, t + 1, :], tot[t // H][:, t % H, :], off[:, t, :], ALU.add))
            for h in range(2):
                link(dve.tensor_tensor(pos[:, h * H:(h + 1) * H, :], rank[h][:, :, :], off[:, h * H:(h + 1) * H, :], ALU.add))
            blocks = cmp[:, 0:NE * NT].rearrange("p (e t) -> p e t", t=NT)
            link(dve.tensor_tensor(blocks, bcast(off[:, NT, :], NT, 2), bcast(it128[:, :], NE, 1), ALU.is_gt))
            link(dve.tensor_reduce(nb[:, :], blocks, AX.X, ALU.add))
            link(dve.tensor_copy(cum[0][:, :], nb[:, :]))
            for i in range(5):
                s, a, c = 1 << i, cum[i % 2], cum[1 - i % 2]
                link(dve.tensor_copy(c[:, 0:s], a[:, 0:s]))
                link(dve.tensor_tensor(c[:, s:NE], a[:, s:NE], a[:, 0:NE - s], ALU.add))
            end = cum[1]
            link(dve.tensor_tensor(cum[0][:, :], end[:, :], nb[:, :], ALU.subtract))
            link(dve.scalar_tensor_tensor(out=pos[:, :, :], in0=bcast(cum[0][:, :], NT, 1), scalar=float(P), in1=pos[:, :, :],
                                          op0=ALU.mult, op1=ALU.add))
            for c in range(2):
                link(dve.tensor_tensor(prod[:, :, :], flat[c], pos[:, :, :], ALU.mult))
                link(dve.tensor_reduce(sf[c][:, :], prod[:, :, :], AX.X, ALU.add))
            for c in range(2):
                link(dve.tensor_copy(slot[:, c, :], sf[c][:, :]))
                link(dve.tensor_single_scalar(row_i[:, c, :], slot[:, c, :], P - 1, ALU.bitwise_and))
                dve.tensor_copy(row[c][:, :], row_i[:, c, :]).then_inc(rows_set, 1)
            for c in range(2):
                dve.wait_ge(rows_set, c + 1)
                link(dve.tensor_tensor(blk[c][:, :], sf[c][:, :], row[c][:, :], ALU.subtract))
                link(dve.tensor_scalar(blk[c][:, :], blk[c][:, :], 1.0 / P, None, ALU.mult))
                dve.tensor_tensor(hot_block[c][:, :, :], bcast(itb[:, :], NT, 1), bcast(blk[c][:, :], MAXB + 2, 2), ALU.is_equal).then_inc(hot_set, 1)
                dve.tensor_tensor(hot_row[c][:, :, :], bcast(itr[:, :], NT, 1), bcast(row[c][:, :], P, 2), ALU.is_equal).then_inc(hot_set, 1)
            ends = cmp[:, :].rearrange("p (b e) -> p b e", e=NE)
            link(dve.tensor_tensor(ends, bcast(itb[:, 0:MAXB], NE, 2), bcast(end[:, :], MAXB, 1), ALU.is_ge))
            link(dve.tensor_reduce(bx[:, :], ends, AX.X, ALU.add))
            link(dve.tensor_scalar(tf[:, 0:MAXB], bx[:, :], float(NE - 1), None, ALU.min))
            link(dve.tensor_copy(table[:, 0:MAXB], tf[:, 0:MAXB]))
            link(dve.tensor_single_scalar(table[:, MAXB:2 * MAXB], table[:, 0:MAXB], 1, ALU.bitwise_and))
            link(dve.tensor_scalar(tf[:, 0:NE], end[:, :], 1.0, None, ALU.add))
            link(dve.tensor_copy(table[:, 2 * MAXB:2 * MAXB + NE], tf[:, 0:NE]))
            link(dve.tensor_copy(table[:, 2 * MAXB + NE:2 * MAXB + NE + 1], end[:, NE - 1:NE]))
            dve.wait_ge(placed, 1)
            dve.tensor_copy(idx[:, :], idp[:, :])


def experts(nc, k, dram, table, idx, xn_rows, y_rows):
    with ExitStack() as ctx:
        b = Bufs(nc, ctx, "experts_")
        pair = lambda name, shape, dt=F32: [b.sb(f"{name}{p}", shape, dt) for p in range(2)]

        whole, lows = over(nc, b, ("w1", "w3"), [P, 2, KD, FF])
        W = {n: (b.sb(f"{n}_high", [P, 2, KD, FF], F32R), low, w) for n, low, w in zip(("w1", "w3"), lows, whole)}
        raw, xl = over(nc, b, ("xT0", "xT1"), [P, KD, P])
        W2 = b.sb("W2", [P, 2, FF // P, D])
        ix, xg = pair("ix", [P, 1], I32), pair("xg", [P, D])
        xh = pair("xT_high", [P, KD, P], F32R)
        s, h3, g = b.sb("silu", [P, FF]), b.sb("h3_copy", [P, FF]), b.sb("gated", [P, FF])
        gT, yo = b.sb("gatedT", [P, FF // P, P]), pair("yout", [P, D])
        tX = [b.ps(f"xg_turned{n}", [P, 4, P]) for n in range(2)]
        H1, H3, tG = b.ps("h1", [P, FF]), b.ps("h3", [P, FF]), b.ps("g_turned", [P, FF // P, P])
        Y = [b.ps(f"ye{n}", [P, 512]) for n in range(2)]
        names = ("ix_set turned raw_set high_set low_set h1_ready h3_ready silu_set h3_set gated_set g_turned gT_set "
                 "y_ready y_set done split w2_here gathers_begun all_stored w_high_set pairs_through").split()
        e = {n: b.sem("moe_" + n) for n in names}
        gathered = [b.sem(f"moe_gathered{p}") for p in range(2)]
        y_free = [b.sem(f"moe_y_free{p}") for p in range(2)]
        PARTS = [(n, q) for n in ("w1", "w3") for q in range(2)]
        KQ = KD // 2
        w_sem = [{n: b.sem(f"moe_{n[0]}_{n[1]}_{p}") for n in PARTS} for p in range(2)]
        w2_sem = [b.sem(f"moe_w2_{p}") for p in range(2)]
        zero, zero_set, emptied = b.sb("zero", [P, D // 4]), b.sem("zero_set"), b.sem("emptied")
        block = ctx.enter_context(nc.Block())
        NB = 2 * MAXB + NE
        PAIRS = (MAXB - 1) // 2

        def n_blocks(eng):
            return eng.value_load(table[0:1, NB:NB + 1], min_val=1, max_val=MAXB)

        def through_blocks(eng, n, step, and_then=None):
            step(0, 0, 0)
            with eng.Fori(0, PAIRS) as j:
                with eng.If(j * 2 + 1 < n):
                    step(1, j * 2 + 1, j)
                    step(0, j * 2 + 2, j + 1)
                if and_then is not None:
                    and_then(j)

        @block.sync
        def _(sp):
            def load(p, x, ends):
                ex = bass.ds(x, 1)
                if ends:
                    last = sp.value_load(table[0:1, bass.ds(x + (2 * MAXB - 2), 1)], min_val=1, max_val=MAXB + 1)
                    sp.wait_ge(e["h3_ready"], last)
                for n, q in PARTS:
                    sp.dma_start(W[n][2][:, p, q * KQ:(q + 1) * KQ],
                                 dram[n][ex, q * KQ * P:(q + 1) * KQ * P, :].rearrange("a (k p) n -> p (a k) n", p=P)).then_inc(w_sem[p][n, q], 16)
                if ends:
                    sp.wait_ge(e["done"], last)
                sp.dma_start(W2[:, p], dram["w2"][ex].rearrange("a (k p) n -> p (a k) n", p=P)).then_inc(w2_sem[p], 16)

            for p in range(2):
                load(p, p, False)
            with sp.Fori(1, NE // 2) as j:
                for p in range(2):
                    load(p, j * 2 + p, True)

        @block.vector
        def _(dve):
            with dve.Fori(0, NE // 2) as j:
                for p in range(2):
                    x = j * 2 + p
                    for i, (n, q) in enumerate(PARTS):
                        high, low, loaded = (t[:, p, q * KQ:(q + 1) * KQ, :] for t in W[n])
                        dve.wait_ge(w_sem[p][n, q], j * 16 + 16)
                        dve.tensor_copy(high, loaded).then_inc(e["w_high_set"], 1)
                        dve.wait_ge(e["w_high_set"], x * 4 + (i + 1))
                        m = dve.tensor_tensor(low, loaded, high.bitcast(F32), ALU.subtract)
                        if q:
                            m.then_inc(e["split"], 1)
                    dve.wait_ge(w2_sem[p], j * 16 + 16)
                    dve.sem_inc(e["w2_here"], 1)

        @block.gpsimd
        def _(pool):
            def gather(p, blk):
                pool.tensor_copy(ix[p][:, :], idx[:, bass.ds(blk, 1)]).then_inc(e["ix_set"], 1)
                pool.wait_ge(e["ix_set"], blk + 1)
                pool.sem_inc(e["gathers_begun"], 1)
                pool.indirect_dma_start(out=xg[p][:, :], out_offset=None, in_=xn_rows[:, :],
                                        in_offset=bass.IndirectOffsetOnAxis(ap=ix[p][:, 0:1], axis=0)).then_inc(gathered[p], 16)

            def low(p, blk):
                pool.wait_ge(e["raw_set"], blk + 1)
                pool.wait_ge(e["high_set"], blk + 1)
                pool.tensor_tensor(xl[p][:, :, :], raw[p][:, :, :], xh[p][:, :, :].bitcast(F32), ALU.subtract).then_inc(e["low_set"], 1)

            def step(p, blk, j):
                pool.wait_ge(e["turned"], blk + 1)
                gather(p, blk + 2)
                low(1 - p, blk + 1)
                pool.wait_ge(e["silu_set"], blk + 1)
                pool.wait_ge(e["h3_set"], blk + 1)
                wait_if_any(pool, e["g_turned"], blk)
                pool.tensor_tensor(g[:, :], h3[:, :], s[:, :], ALU.mult).then_inc(e["gated_set"], 1)

            def empty_rows(j):
                with pool.If(j * -2 + (2 * PAIRS - 1) >= n):
                    dst = y_rows[bass.ds(j * (-2 * P) + (2 * PAIRS - 1) * P, 2 * P), :]
                    pool.dma_start(dst.rearrange("(p a) (c d) -> p (a c) d", p=P, c=4), bcast(zero[:, :], 8, 1)).then_inc(emptied, 16)
                    pool.wait_ge(emptied, j * 16 + 16)
                pool.sem_inc(e["pairs_through"], 1)

            n = n_blocks(pool)
            pool.memset(zero[:, :], 0.0).then_inc(zero_set, 1)
            gather(0, 0)
            gather(1, 1)
            pool.wait_ge(zero_set, 1)
            low(0, 0)
            through_blocks(pool, n, step, empty_rows)

        @block.tensor
        def _(pe):
            def turn(p, blk, arrived):
                pe.wait_ge(gathered[p], arrived)
                wait_if_any(pe, e["high_set"], blk)
                wait_if_any(pe, e["raw_set"], blk)
                for c in range(KD):
                    m = pe.transpose(tX[c // 4][:, c % 4, :], xg[p][:, c * P:(c + 1) * P], k["ident"][:, :])
                m.then_inc(e["turned"], 1)

            def hidden(name, out, p, half):
                for kt in range(KD):
                    high, low = (t[:, half, kt, :].rearrange("p a n -> p (a n)") for t in W[name][0:2])
                    for i, (x, w) in enumerate(((xh, high), (xh, low), (xl, high))):
                        m = pe.matmul(out[:, :], x[p][:, kt, :], w, start=kt == 0 and i == 0, stop=kt == KD - 1 and i == 2)
                return m

            def turn_gated(blk):
                pe.wait_ge(e["gated_set"], blk + 1)
                for c in range(FF // P):
                    m = pe.transpose(tG[:, c, :], g[:, c * P:(c + 1) * P], k["ident"][:, :])
                m.then_inc(e["g_turned"], 1)

            def output(blk):
                x = pe.value_load(table[0:1, bass.ds(blk, 1)], min_val=0, max_val=NE - 1)
                half = bass.ds(pe.value_load(table[0:1, bass.ds(blk + MAXB, 1)], min_val=0, max_val=1), 1)
                pe.wait_ge(e["w2_here"], x + 1)
                pe.wait_ge(e["gT_set"], blk + 1)
                wait_if_any(pe, e["y_set"], blk)
                for n in range(2):
                    for c in range(FF // P):
                        rhs = W2[:, half, c, n * 512:(n + 1) * 512].rearrange("p a n -> p (a n)")
                        m = pe.matmul(Y[n][:, :], gT[:, c, :], rhs, start=c == 0, stop=c == FF // P - 1)
                    m.then_inc(e["done" if n else "y_ready"], 1)

            def step(p, blk, j):
                x = pe.value_load(table[0:1, bass.ds(blk, 1)], min_val=0, max_val=NE - 1)
                half = bass.ds(pe.value_load(table[0:1, bass.ds(blk + MAXB, 1)], min_val=0, max_val=1), 1)
                pe.wait_ge(e["low_set"], blk + 1)
                pe.wait_ge(e["split"], x * 2 + 1)
                wait_if_any(pe, e["silu_set"], blk)
                hidden("w1", H1, p, half).then_inc(e["h1_ready"], 1)
                first = isinstance(blk, int) and blk == 0
                if not first:
                    turn_gated(blk - 1)
                turn(1 - p, blk + 1, (j + p) * 16 + 16)
                pe.wait_ge(e["split"], x * 2 + 2)
                wait_if_any(pe, e["h3_set"], blk)
                hidden("w3", H3, p, half).then_inc(e["h3_ready"], 1)
                if not first:
                    output(blk - 1)

            n = n_blocks(pe)
            for name in ("h3_ready", "done"):
                pe.sem_inc(e[name], 1)
            turn(0, 0, 16)
            through_blocks(pe, n, step)
            last = n // 2 * 2
            turn_gated(last)
            output(last)

        @block.scalar
        def _(act):
            def turned(p, blk):
                act.wait_ge(e["turned"], blk + 1)
                for n in range(2):
                    m = act.activation(raw[p][:, 4 * n:4 * n + 4, :], tX[n][:, :, :], ACT.Copy)
                m.then_inc(e["raw_set"], 1)
                for n in range(2):
                    m = act.activation(xh[p][:, 4 * n:4 * n + 4, :], tX[n][:, :, :], ACT.Copy)
                m.then_inc(e["high_set"], 1)

            def turned_gate(blk):
                act.wait_ge(e["g_turned"], blk + 1)
                act.activation(gT[:, :, :], tG[:, :, :], ACT.Copy).then_inc(e["gT_set"], 1)

            def output(p, blk, j):
                act.wait_ge(y_free[p], j * 16 + 16)
                for c in range(2):
                    act.wait_ge(e["done" if c else "y_ready"], blk + (1 + c))
                    m = act.activation(yo[p][:, c * 512:(c + 1) * 512], Y[c][:, :], ACT.Copy)
                m.then_inc(e["y_set"], 1)
                act.wait_ge(e["y_set"], blk + 1)
                act.dma_start(y_rows[bass.ds(blk * P, P), :], yo[p][:, :]).then_inc(y_free[p], 16)

            def step(p, blk, j):
                act.wait_ge(e["h1_ready"], blk + 1)
                wait_if_any(act, e["gated_set"], blk)
                act.activation(s[:, :], H1[:, :], ACT.Silu).then_inc(e["silu_set"], 1)
                first = isinstance(blk, int) and blk == 0
                if not first:
                    turned_gate(blk - 1)
                turned(1 - p, blk + 1)
                act.wait_ge(e["h3_ready"], blk + 2)
                act.activation(h3[:, :], H3[:, :], ACT.Copy).then_inc(e["h3_set"], 1)
                if not first:
                    output(1 - p, blk - 1, j if p else j - 1)

            n = n_blocks(act)
            for p in range(2):
                act.dma_start(yo[p][0:1, :], dram["final_norm_g"].rearrange("(a n) -> a n", a=1)).then_inc(y_free[p], 16)
            turned(0, 0)
            through_blocks(act, n, step)
            turned_gate(n // 2 * 2)
            output(0, n // 2 * 2, n // 2)
            for p in range(2):
                act.wait_ge(y_free[p], n // 2 * 16 + (32 if p == 0 else 16))
                act.sem_inc(e["all_stored"], 1)


def combine(nc, k, dram, gate, slot, x2_rows, y_rows, y):
    with ExitStack() as ctx:
        b = Bufs(nc, ctx, "combine_")
        U = 3
        ring = lambda name, shape, dt=F32: [b.sb(f"{name}{p}", shape, dt) for p in range(U)]
        gf, junk = b.sb("final_gain", [P, D]), b.sb("junk_f", [P, D])
        ix, x, out = ring("cix", [P, 2], I32), ring("cx", [P, D]), ring("out", [P, D])
        r = [ring(f"crow{c}", [P, D]) for c in range(2)]
        ss, rt, ri = ring("css", [P, 1]), ring("crt", [P, 1]), ring("cri", [P, 1])
        names = "ix_set gathers_begun sum1 sum2 squared rooted inverted out_set".split()
        e = {n: b.sem("fin_" + n) for n in names}
        const = b.sem("fin_const")
        x_ld = [b.sem(f"fin_x{p}") for p in range(U)]
        r_ld = [b.sem(f"fin_rows{p}") for p in range(U)]
        stored = [b.sem(f"fin_stored{p}") for p in range(U)]
        block = ctx.enter_context(nc.Block())

        def through_tiles(eng, first, last, step):
            with eng.Fori(first, last) as j:
                for p in range(U):
                    step(p, j, j * U + p)

        @block.sync
        def _(sp):
            def store(p, t):
                sp.wait_ge(e["out_set"], t + 1)
                sp.dma_start(y[bass.ds(t * P, P), :], out[p][:, :]).then_inc(stored[p], 16)

            def step(p, j, t):
                sp.wait_ge(e["out_set"], t - (U - 1))
                sp.dma_start(x[p][:, :], x2_rows[bass.ds(t * P, P), :]).then_inc(x_ld[p], 16)
                store(p, t - U)

            for p in range(U):
                sp.dma_start(x[p][:, :], x2_rows[p * P:(p + 1) * P, :]).then_inc(x_ld[p], 16)
            sp.dma_start(gf[:, :], dram["final_norm_g"].partition_broadcast(P)).then_inc(const, 16)
            through_tiles(sp, 1, NT // U, step)
            for p in range(U):
                store(p, NT - U + p)
            for p in range(U):
                sp.wait_ge(stored[p], 16 * NT // U)

        @block.gpsimd
        def _(pool):
            def rows(p, t):
                pool.tensor_copy(ix[p][:, :], slot[:, :, bass.ds(t, 1)].rearrange("p c a -> p (c a)")).then_inc(e["ix_set"], 1)
                pool.wait_ge(e["ix_set"], t + 1)
                pool.sem_inc(e["gathers_begun"], 1)
                for c in range(2):
                    pool.indirect_dma_start(out=r[c][p][:, :], out_offset=None, in_=y_rows[:, :],
                                            in_offset=bass.IndirectOffsetOnAxis(ap=ix[p][:, c:c + 1], axis=0)).then_inc(r_ld[p], 16)

            def step(p, j, t):
                pool.wait_ge(e["sum2"], t - (U - 1))
                rows(p, t)

            for p in range(U):
                rows(p, p)
            through_tiles(pool, 1, NT // U, step)

        @block.vector
        def _(dve):
            def sums(p, j, t):
                dve.wait_ge(x_ld[p], j * 16 + 16)
                dve.wait_ge(r_ld[p], j * 32 + 32)
                g = [gate[:, c, bass.ds(t, 1)] for c in range(2)]
                dve.scalar_tensor_tensor(out=x[p][:, :], in0=r[0][p][:, :], scalar=g[0], in1=x[p][:, :],
                                         op0=ALU.mult, op1=ALU.add).then_inc(e["sum1"], 1)
                dve.wait_ge(e["sum1"], t + 1)
                dve.scalar_tensor_tensor(out=x[p][:, :], in0=r[1][p][:, :], scalar=g[1], in1=x[p][:, :],
                                         op0=ALU.mult, op1=ALU.add).then_inc(e["sum2"], 1)

            def norm(p, j, t, first=False):
                dve.wait_ge(e["rooted"], t + 1)
                dve.reciprocal(ri[p][:, :], rt[p][:, :]).then_inc(e["inverted"], 1)
                dve.wait_ge(e["inverted"], t + 1)
                if not first:
                    dve.wait_ge(stored[p], j * 16)
                dve.scalar_tensor_tensor(out=out[p][:, :], in0=x[p][:, :], scalar=ri[p][:, :], in1=gf[:, :],
                                         op0=ALU.mult, op1=ALU.mult).then_inc(e["out_set"], 1)

            def step(p, j, t):
                sums(p, j, t)
                norm((p - 1) % U, j if p else j - 1, t - 1, isinstance(t, int) and t <= U)

            dve.wait_ge(const, 16)
            sums(0, 0, 0)
            for t in range(1, U + 1):
                step(t % U, t // U, t)
            for t in range(U + 1, 2 * U):
                step(t % U, t // U, t)
            through_tiles(dve, 2, NT // U, step)
            norm(U - 1, NT // U - 1, NT - 1)

        @block.scalar
        def _(act):
            def step(p, j, t):
                act.wait_ge(e["sum2"], t + 1)
                act.activation(junk[:, :], x[p][:, :], ACT.Square, accum_out=ss[p][:, :]).then_inc(e["squared"], 1)
                act.wait_ge(e["squared"], t + 1)
                act.activation(rt[p][:, :], ss[p][:, :], ACT.Sqrt, bias=k["eps"][:, :], scale=1.0 / D).then_inc(e["rooted"], 1)

            through_tiles(act, 0, NT // U, step)


def encoder(nc, dram, y):
    with ExitStack() as ctx:
        b = Bufs(nc, ctx)
        feat = nc.dram_tensor("feat", (20, P, T), F32).ap()
        ab_rows = nc.dram_tensor("ab_rows", (16, T), F32).ap()
        x2_rows = nc.dram_tensor("x2_rows", (T, D), F32).ap()
        xn_rows = nc.dram_tensor("xn_rows", (T, D), F32).ap()
        y_rows = nc.dram_tensor("y_rows", (SLOTS, D), F32).ap()
        k = {"ident": b.sb("ident", [P, P]), "ones": b.sb("ones", [P, P]), "lower": b.sb("lower", [P, P]), "eps": b.sb("eps", [P, 1])}
        lg = b.sb("lg", [P, NT, NG + NE])
        with ExitStack() as mixers:
            m = Bufs(nc, mixers)
            k.update({
                "group": m.sb("group", [P, P]), "tri": m.sb("tri", [P, 2, P]), "neg": m.sb("neg", [P, 2, P]),
                "lvl": m.sb("lvl", [P, 2, LEVELS, P]), "g1": m.sb("g1", [P, D]),
                "cw_mix": m.sb("cw_mix", [P, CONV_TILES, 3]), "cg_mix": m.sb("cg_mix", [P, CONV_TILES]),
                "cw_qkv": m.sb("cw_qkv", [P, 3 * HEADS, 3]), "alog": m.sb("alog", [P, 2 * HEADS]),
                "dtb": m.sb("dtb", [P, 2 * HEADS]), "eps128": m.sb("eps128", [P, 1]), "one": m.sb("one", [P, 1]),
            })
            constants(nc, k, dram)
            with ExitStack() as c2:
                hT = Bufs(nc, c2).sb("hT", [P, KD, T])
                with nc.cleanup_on_exit():
                    normalise(nc, k, dram, hT)
                with nc.cleanup_on_exit():
                    project(nc, k, dram, hT, feat, ab_rows)
            gates = m.sb("gates", [P, 2, NT, 5 * HEADS])
            decays(nc, k, ab_rows, gates)
            with ExitStack() as c2:
                O = Bufs(nc, c2).sb("O", [P, NT, HEADS * P])
                with nc.cleanup_on_exit():
                    delta(nc, k, gates, feat, O)
                with nc.cleanup_on_exit():
                    output(nc, k, dram, feat, O, lg, x2_rows, xn_rows)
        gate, slot = b.sb("gate", [P, 2, NT]), b.sb("slot", [P, 2, NT], I32)
        table, idx = b.sb("table", [P, 2 * MAXB + NE + 1], I32), b.sb("idx", [P, MAXB + 2], I32)
        route(nc, k, lg, gate, slot, table, idx)
        experts(nc, k, dram, table, idx, xn_rows, y_rows)
        combine(nc, k, dram, gate, slot, x2_rows, y_rows, y)


def lay_out(inputs):
    a = {name: np.asarray(v) for name, v in inputs.items()}
    w_in = a["w_in"][0]
    start = {"b": 0, "c": 512, "h": 1024, "q": 1536, "k": 2048, "v": 2560, "z": 3072}
    tiles = [w_in[:, start[job] + g * P:start[job] + (g + 1) * P] for g in range(HEADS) for job in JOBS]
    by_tap = lambda w: w.reshape(3, -1, P).transpose(2, 1, 0)
    return {
        "x": np.concatenate([a["x_prompt"][0], a["x_sample"][0]], 0),
        "w_tiles": np.stack(tiles).reshape(len(tiles), KD, P, P).transpose(0, 2, 1, 3),
        "w_ab": w_in[:, 3584:].reshape(KD, P, 4 * HEADS).transpose(1, 0, 2),
        "norm1_g": a["norm1_g"][0],
        "conv_a_w": by_tap(a["conv_a_w"][0]),
        "conv_a_norm_g": a["conv_a_norm_g"][0].reshape(CONV_TILES, P).T,
        "dn_conv_w": by_tap(a["dn_conv_w"][0]),
        "dn_a_log": a["dn_a_log"][0].reshape(-1),
        "dn_dt_bias": a["dn_dt_bias"][0].reshape(-1),
        "dn_norm_g": a["dn_norm_g"][0].reshape(P, 1),
        "w_o": a["w_o"][0],
        "norm2_g": a["norm2_g"][0],
        "router_w": np.concatenate([a["router_group_w"][0], a["router_expert_w"][0]], 1),
        "router_b": np.concatenate([a["router_group_b"][0], a["router_expert_b"][0]]),
        "w1": a["w1"][0], "w3": a["w3"][0], "w2": a["w2"][0],
        "final_norm_g": a["final_norm_g"],
    }


def kernel(**inputs):
    import concourse.bacc as bacc
    from concourse.bass_utils import run_bass_kernel_spmd

    nc = bacc.Bacc("TRN2", target_bir_lowering=False, num_devices=1)
    arrays, dram = {}, {}
    for name, array in lay_out(inputs).items():
        arrays[f"in_{name}_dram"] = np.ascontiguousarray(array)
        dram[name] = nc.dram_tensor(f"in_{name}_dram", array.shape, mybir.dt.from_np(array.dtype), kind="ExternalInput").ap()
    y = nc.dram_tensor("out_0_dram", (T, D), F32, kind="ExternalOutput").ap()
    encoder(nc, dram, y)
    r = run_bass_kernel_spmd(nc, [arrays], core_ids=[0])
    rows = r.results[0]["out_0_dram"]
    return rows[None, :LONG], rows[None, LONG:]
```

```python
from contextlib import ExitStack

import numpy as np

import concourse.bass as bass
from concourse import mybir

F32 = mybir.dt.float32
F32R = mybir.dt.float32r
I32 = mybir.dt.int32
ALU = mybir.AluOpType
ACT = mybir.ActivationFunctionType
AX = mybir.AxisListType

P = 128
LONG, SHORT = 2048, 256
T = LONG + SHORT
NT = T // P
LT_TILES = LONG // P
D = 1024
KD = D // P
HEADS = 4
CONV_TILES = 4
EPS = 1e-6
NCH = 6
CH = T // NCH
JOBS = "chbqzkv"


def chunks():
    cuts = [0] + [LONG * i // 5 // 2 * 2 + 1 for i in range(1, 5)] + [LONG]
    return [(max(a - 1, 0), min(z + 1, LONG), a, z) for a, z in zip(cuts, cuts[1:])] + [(LONG, T, LONG, T)]


CHUNKS = chunks()
CW = max(hi - lo for lo, hi, _, _ in CHUNKS)
NG, EPG, NE, FF = 4, 8, 32, 512
MAXB = (2 * T + NE * (P - 1)) // P
MAXB += 1 - MAXB % 2
SLOTS = MAXB * P
LEVELS = 7


def bcast(ap, n, axis):
    v = ap.unsqueeze(axis)
    shape = list(v.shape)
    shape[axis] = n
    return v.broadcast_to(shape)


class Bufs:

    def __init__(self, nc, ctx, phase=""):
        self.nc, self.ctx, self.phase = nc, ctx, phase

    def sb(self, name, shape, dt=F32):
        return self.ctx.enter_context(self.nc.sbuf_tensor(self.phase + name, shape, dt))

    def ps(self, name, shape):
        return self.ctx.enter_context(self.nc.psum_tensor(self.phase + name, shape, F32))

    def sem(self, name):
        return self.nc.alloc_semaphore(name=self.phase + name)


def over(nc, b, names, shape):
    with ExitStack() as first:
        whole = [Bufs(nc, first, b.phase).sb(f"{n}_whole", shape) for n in names]
    return whole, [b.sb(f"{n}_low", shape, F32R) for n in names]


def constants(nc, k, dram):
    with ExitStack() as ctx:
        b = Bufs(nc, ctx, "constants_")
        cleared, loaded = b.sem("ident_cleared"), b.sem("gain_loaded")
        block = ctx.enter_context(nc.Block())

        @block.sync
        def _(sp):
            sp.dma_start(k["g1"][:, :], dram["norm1_g"].partition_broadcast(P)).then_inc(loaded, 16)
            sp.wait_ge(loaded, 16)

        @block.vector
        def _(dve):
            dve.memset(k["eps"][:, :], EPS)
            dve.memset(k["eps128"][:, :], EPS * P)
            dve.memset(k["one"][:, :], 1.0)

        @block.gpsimd
        def _(pool):
            pool.memset(k["ident"][:, :], 0.0).then_inc(cleared, 1)
            pool.wait_ge(cleared, 1)
            pool.affine_select(out=k["ident"][:, :], in_=k["ident"][:, :], compare_op=ALU.not_equal, fill=1.0,
                               base=0, pattern=[[-1, P]], channel_multiplier=1)


def small_inputs(sp, k, dram, small):
    n = 0
    for dst, src in (
        (k["cw_mix"][:, :, :], dram["conv_a_w"]),
        (k["cg_mix"][:, :], dram["conv_a_norm_g"]),
        (k["cw_qkv"][:, :, :], dram["dn_conv_w"]),
        (k["alog"][:, :], dram["dn_a_log"].partition_broadcast(P)),
        (k["dtb"][:, :], dram["dn_dt_bias"].partition_broadcast(P)),
    ):
        sp.dma_start(dst, src).then_inc(small, 16)
        n += 16
    sp.wait_ge(small, n)


def masks(pool, k, set0, sel):
    fills = [(k["ones"], 1.0), (k["tri"], 1.0), (k["neg"], 0.0), (k["lower"], 1.0), (k["group"], 1.0), (k["lvl"], 0.0)]
    for buf, v in fills:
        pool.memset(buf[:], v).then_inc(set0, 1)
    n = len(fills)
    pool.wait_ge(set0, n)
    halves = k["group"][:, :].rearrange("p (b r) -> p b r", b=2)
    pool.affine_select(out=halves, in_=halves, compare_op=ALU.is_ge, fill=0.0, base=0,
                       pattern=[[-64, 2], [0, 64]], channel_multiplier=1).then_inc(sel, 1)
    pool.wait_ge(sel, 1)
    pool.affine_select(out=halves, in_=halves, compare_op=ALU.is_ge, fill=0.0, base=63,
                       pattern=[[64, 2], [0, 64]], channel_multiplier=-1)
    levels = [(1 << l, d, k["lvl"][:, d, l, :].rearrange("p (b h r) -> p b h r", h=2, r=1 << l)[:, :, 1 - d, :])
              for l in range(LEVELS) for d in range(2)]
    for s, d, v in levels:
        pool.memset(v, 1.0).then_inc(set0, 1)
    pool.wait_ge(set0, n + len(levels))
    for s, d, v in levels:
        pool.affine_select(out=v, in_=v, compare_op=ALU.is_ge, fill=0.0, base=-s * d,
                           pattern=[[-2 * s, P // (2 * s)], [0, s]], channel_multiplier=1).then_inc(sel, 1)
    pool.wait_ge(sel, len(levels) + 1)
    for s, d, v in levels:
        pool.affine_select(out=v, in_=v, compare_op=ALU.is_ge, fill=0.0, base=s * d + s - 1,
                           pattern=[[2 * s, P // (2 * s)], [0, s]], channel_multiplier=-1)
    for buf, fill in ((k["tri"], 0.0), (k["neg"], -1e30)):
        for d, sign in ((0, 1), (1, -1)):
            pool.affine_select(out=buf[:, d, :], in_=buf[:, d, :], compare_op=ALU.is_ge, fill=fill,
                               base=0, pattern=[[sign, P]], channel_multiplier=-sign)
    pool.affine_select(out=k["lower"][:, :], in_=k["lower"][:, :], compare_op=ALU.is_gt, fill=0.0,
                       base=0, pattern=[[1, P]], channel_multiplier=-1)


def normalise(nc, k, dram, hT):
    with ExitStack() as ctx:
        b = Bufs(nc, ctx, "normalise_")
        U = 3
        ring = lambda name, shape: [b.sb(f"{name}{p}", shape) for p in range(U)]
        x, xn = ring("x", [P, D]), ring("xn", [P, D])
        sq = b.sb("sq_junk", [P, D])
        ss, rt, ri = ring("ss", [P, 1]), ring("rt", [P, 1]), ring("ri", [P, 1])
        tp = [[b.ps(f"tp{p}{h}", [P, 4, P]) for h in range(2)] for p in range(U)]
        loaded = [b.sem(f"x_loaded{p}") for p in range(U)]
        summed, rooted, inverted, scaled = b.sem("x_summed"), b.sem("x_rooted"), b.sem("x_inverted"), b.sem("x_scaled")
        turned, copied = b.sem("x_turned"), [b.sem("x_copied0"), b.sem("x_copied1")]
        small, filled, selected = b.sem("small_loaded"), b.sem("masks_filled"), b.sem("masks_selected")
        block = ctx.enter_context(nc.Block())

        def through_tiles(eng, first, last, step):
            with eng.Fori(first, last) as j:
                for p in range(U):
                    step(p, j, j * U + p)

        @block.sync
        def _(sp):
            def load(p, t):
                sp.dma_start(x[p][:, :], dram["x"][bass.ds(t * P, P), :]).then_inc(loaded[p], 16)

            def reload(p, j, t):
                sp.wait_ge(scaled, t - (U - 1))
                load(p, t)

            for p in range(U):
                load(p, p)
            through_tiles(sp, 1, NT // U, reload)
            small_inputs(sp, k, dram, small)

        @block.scalar
        def _(act):
            def root(p, j, t):
                act.wait_ge(loaded[p], j * 16 + 16)
                act.activation(sq[:, :], x[p][:, :], ACT.Square, accum_out=ss[p][:, :]).then_inc(summed, 1)
                act.wait_ge(summed, t + 1)
                act.activation(rt[p][:, :], ss[p][:, :], ACT.Sqrt, bias=k["eps"][:, :], scale=1.0 / D).then_inc(rooted, 1)

            def copy(p, t):
                for h in range(2):
                    act.wait_ge(turned, t * 2 + (h + 1))
                    act.activation(hT[0][:, 4 * h:4 * h + 4, bass.ds(t * P, P)], tp[p][h][:, :, :], ACT.Copy).then_inc(copied[0], 1)

            def both(p, j, t):
                root((p + 1) % U, j + (p + 1) // U, t + 1)
                copy(p, t)

            root(0, 0, 0)
            through_tiles(act, 0, NT // U - 1, both)
            for p in range(U):
                t = NT - U + p
                if p + 1 < U:
                    both(p, NT // U - 1, t)
                else:
                    copy(p, t)

        @block.vector
        def _(dve):
            def scale(p, t):
                dve.wait_ge(rooted, t + 1)
                dve.reciprocal(ri[p][:, :], rt[p][:, :]).then_inc(inverted, 1)
                dve.wait_ge(inverted, t + 1)
                dve.scalar_tensor_tensor(out=xn[p][:, :], in0=x[p][:, :], scalar=ri[p][:, :], in1=k["g1"][:, :],
                                         op0=ALU.mult, op1=ALU.mult).then_inc(scaled, 1)

            def copy(p, t):
                for h in range(2):
                    high, low = (x[:, 4 * h:4 * h + 4, bass.ds(t * P, P)] for x in hT)
                    dve.wait_ge(copied[0], t * 2 + (h + 1))
                    dve.tensor_tensor(low, tp[p][h][:, :, :], high.bitcast(F32), ALU.subtract).then_inc(copied[1], 1)

            def both(p, j, t):
                scale((p + 1) % U, t + 1)
                copy(p, t)

            scale(0, 0)
            through_tiles(dve, 0, NT // U - 1, both)
            for p in range(U):
                t = NT - U + p
                if p + 1 < U:
                    both(p, NT // U - 1, t)
                else:
                    copy(p, t)

        @block.tensor
        def _(pe):
            def turn(p, j, t, banks_used=True):
                pe.wait_ge(scaled, t + 1)
                for h in range(2):
                    if banks_used:
                        pe.wait_ge(copied[1], t * 2 + (h + 1 - 2 * U))
                    for c in range(4):
                        m = pe.transpose(tp[p][h][:, c, :], xn[p][:, (4 * h + c) * P:(4 * h + c + 1) * P], k["ident"][:, :])
                    m.then_inc(turned, 1)

            for p in range(U):
                turn(p, 0, p, banks_used=False)
            through_tiles(pe, 1, NT // U, turn)

        @block.gpsimd
        def _(pool):
            masks(pool, k, filled, selected)


def project(nc, k, dram, hT, feat, ab_rows):
    with ExitStack() as ctx:
        b = Bufs(nc, ctx, "project_")
        hT_high, hT_low = hT
        whole, low = over(nc, b, [f"w{s}" for s in range(4)], [P, KD, P])
        high = [b.sb(f"w{s}_high", [P, KD, P], F32R) for s in range(4)]
        ring = lambda name, n: [b.sb(f"{name}{i}", [P, CW]) for i in range(n)]
        raw, out, side = ring("raw", 2), ring("out", 4), ring("side", 2)
        sq, nrm = b.sb("squares", [P, CW]), b.sb("norms", [P, CW])
        primer, zero = b.sb("primer", [P, CONV_TILES]), b.sb("zero", [P, 1])
        bank = [b.ps(f"proj{c}", [P, 512]) for c in range(6)]
        nbank = [b.ps(f"nsum{c}", [P, 512]) for c in range(2)]
        sems = lambda name, n: [b.sem(f"{name}{i}") for i in range(n)]
        w_loaded, w_split = sems("w_loaded", 4), sems("w_split", 4)
        ready, free = sems("proj_ready", 6), sems("proj_free", 6)
        nready, nfree = sems("nsum_ready", 2), sems("nsum_free", 2)
        stored, side_stored = sems("stored", 4), sems("side_stored", 2)
        w_high, chain, convolved, silued, squared, inverted, normed, begun, cleared, ab_set = (b.sem(n) for n in
            "w_high conv_taps convolved silued squared inverted normed splits_begun zero_cleared ab_set".split())
        block = ctx.enter_context(nc.Block())
        G, NC = CONV_TILES, len(CHUNKS)
        SLOT = dict(zip(JOBS, (0, 1, 2, 3, 0, 1, 2)))
        USE = dict(zip(JOBS, ((0, 2), (0, 2), (0, 2), (0, 1), (1, 2), (1, 2), (1, 2))))
        UNITS, ITEMS, NORMS = 7 * NC, 4 * NC, 3 * NC

        def unit(j, c):
            return {"c": 3 * c, "h": 3 * c + 1, "b": 3 * c + 2, "q": 3 * NC + 2 * c, "z": 3 * NC + 2 * c + 1,
                    "k": 5 * NC + 2 * c, "v": 5 * NC + 2 * c + 1}[j]

        def item(j, c):
            return {"b": c, "q": NC + c, "k": 2 * NC + 2 * c, "v": 2 * NC + 2 * c + 1}[j]

        def norm_no(j, c):
            return "bqk".index(j) * NC + c

        def silu_no(j, c):
            return item(j, c) - NC

        def geometry(c):
            lo, hi, a, z = CHUNKS[c]
            return hi - lo, lo - (a - 1), a - lo, z - a

        def computed(eng, j, c, g):
            u = unit(j, c)
            eng.wait_ge(ready[u % 6], g * (UNITS // 6) + (u // 6 + 1))

        def evacuated(eng, j, c, g):
            u = unit(j, c)
            eng.wait_ge(free[u % 6], g * (UNITS // 6) + (u // 6 + 2))

        def is_convolved(eng, i, g):
            eng.wait_ge(convolved, g * ITEMS + (i + 3))

        @block.sync
        def _(sp):
            def load(j, g, after=None):
                if after is not None:
                    computed(sp, after[0], NC - 1, after[1])
                s = SLOT[j]
                sp.dma_start(whole[s][:, :, :], dram["w_tiles"][bass.ds(g * 7 + JOBS.index(j), 1)]
                             .rearrange("a p k m -> (a p) k m")).then_inc(w_loaded[s], 16)

            def store(j, c, g):
                lo, hi, a, z = CHUNKS[c]
                row = g + {"q": 0, "k": HEADS, "v": 2 * HEADS, "z": 3 * HEADS, "b": 4 * HEADS}[j]
                dst = feat[bass.ds(row, 1), :, a:z].rearrange("a p t -> (a p) t")
                if j == "z":
                    evacuated(sp, "z", c, g)
                    sp.dma_start(dst, side[c % 2][:, 0:z - a]).then_inc(side_stored[c % 2], 16)
                    return
                if j == "v":
                    sp.wait_ge(silued, g * NORMS + (silu_no("v", c) + 1))
                else:
                    sp.wait_ge(normed, g * NORMS + (norm_no(j, c) + 2))
                s = item(j, c) % 4
                sp.dma_start(dst, out[s][:, 0:z - a]).then_inc(stored[s], 16)

            def iteration(g, more):
                for c in range(1, NC):
                    if c == NC - 1:
                        load("z", g, ("c", g))
                        load("k", g, ("h", g))
                    store("b", c - 1, g)
                load("v", g, ("b", g))
                for c in range(NC):
                    store(*(("q", c - 1) if c else ("b", NC - 1)), g)
                    store("z", c, g)
                if more:
                    load("q", g + 1, ("q", g))
                    load("c", g + 1, ("z", g))
                for c in range(NC):
                    if c == NC - 1 and more:
                        load("h", g + 1, ("k", g))
                    store(*(("k", c - 1) if c else ("q", NC - 1)), g)
                    if c == NC - 1 and more:
                        load("b", g + 1, ("v", g))
                    store("v", c, g)
                store("k", NC - 1, g)

            for j in "chbq":
                load(j, 0)
            for sem in stored + side_stored:
                sp.dma_start(primer[:, :], dram["conv_a_norm_g"]).then_inc(sem, 16)
                sp.wait_ge(sem, 16)
            with sp.Fori(0, G - 1) as g:
                iteration(g, True)
            iteration(G - 1, False)
            sp.dma_start(whole[3][:, :, 0:16], dram["w_ab"]).then_inc(w_loaded[3], 16)
            for c in range(NCH):
                sp.wait_ge(ab_set, c + 1)
                sp.dma_start(ab_rows[:, c * CH:(c + 1) * CH], side[c % 2][0:16, 0:CH]).then_inc(side_stored[c % 2], 16)
            for sem in stored:
                sp.wait_ge(sem, 16 * (G * ITEMS // 4 + 1))
            for sem in side_stored:
                sp.wait_ge(sem, 16 * (G * NC // 2 + NCH // 2 + 1))

        @block.gpsimd
        def _(pool):
            def split(j, g, n):
                s = SLOT[j]
                at, uses = USE[j]
                pool.wait_ge(w_loaded[s], g * (16 * uses) + 16 * (at + 1))
                pool.sem_inc(begun, 1)
                pool.tensor_copy(high[s][:, :, :], whole[s][:, :, :]).then_inc(w_high, 1)
                pool.wait_ge(w_high, n)
                pool.tensor_tensor(low[s][:, :, :], whole[s][:, :, :], high[s][:, :, :].bitcast(F32), ALU.subtract).then_inc(w_split[s], 1)

            for i, j in enumerate("chbq"):
                split(j, 0, i + 1)
            with pool.Fori(0, G - 1) as g:
                for i, j in enumerate("zkv"):
                    split(j, g, g * 7 + (i + 5))
                for i, j in enumerate("qchb"):
                    split(j, g + 1, g * 7 + (i + 8))
            for i, j in enumerate("zkv"):
                split(j, G - 1, (G - 1) * 7 + i + 5)
            pool.wait_ge(w_loaded[3], 16 * (G + 1))
            pool.tensor_copy(high[3][:, :, 0:16], whole[3][:, :, 0:16]).then_inc(w_high, 1)
            pool.wait_ge(w_high, G * 7 + 1)
            pool.tensor_tensor(low[3][:, :, 0:16], whole[3][:, :, 0:16], high[3][:, :, 0:16].bitcast(F32), ALU.subtract).then_inc(w_split[3], 1)

        @block.tensor
        def _(pe):
            def product(dst, s, m, lo, hi):
                for kt in range(KD):
                    for i, (w, x) in enumerate(((high, hT_high), (high, hT_low), (low, hT_high))):
                        r = pe.matmul(dst, w[s][:, kt, 0:m], x[:, kt, lo:hi], start=kt == 0 and i == 0, stop=kt == KD - 1 and i == 2)
                return r

            def job(j, c, g):
                lo, hi, a, z = CHUNKS[c]
                u, s = unit(j, c), SLOT[j]
                if c == 0:
                    at, uses = USE[j]
                    pe.wait_ge(w_split[s], g * uses + (at + 1))
                pe.wait_ge(free[u % 6], g * (UNITS // 6) + (u // 6 + 1))
                product(bank[u % 6][:, 0:hi - lo], s, P, lo, hi).then_inc(ready[u % 6], 1)

            def sums(j, c, g):
                n, cols = norm_no(j, c), geometry(c)[3]
                pe.wait_ge(squared, g * NORMS + (n + 1))
                pe.wait_ge(nfree[n % 2], g * (NORMS // 2) + (n // 2 + 1))
                weights = k["group"] if j == "b" else k["ones"]
                pe.matmul(nbank[n % 2][:, 0:cols], weights[:, :], sq[:, 0:cols], start=True, stop=True).then_inc(nready[n % 2], 1)

            with pe.Fori(0, G) as g:
                for c in range(NC):
                    job("c", c, g)
                    job("h", c, g)
                    if c:
                        sums("b", c - 1, g)
                    job("b", c, g)
                for c in range(NC):
                    job("q", c, g)
                    sums(*(("q", c - 1) if c else ("b", NC - 1)), g)
                    job("z", c, g)
                for c in range(NC):
                    job("k", c, g)
                    sums(*(("k", c - 1) if c else ("q", NC - 1)), g)
                    job("v", c, g)
                sums("k", NC - 1, g)
            pe.wait_ge(w_split[3], G + 1)
            for c in range(NCH):
                pe.wait_ge(free[c], G * (UNITS // 6) + 1)
                product(bank[c][0:16, 0:CH], 3, 16, c * CH, (c + 1) * CH).then_inc(ready[c], 1)

        @block.scalar
        def _(act):
            def to_raw(j, c, g):
                u, i = unit(j, c), item(j, c)
                proj, at, _, cols = geometry(c)
                is_convolved(act, i - 2, g)
                if at:
                    act.activation(raw[i % 2][:, 0:1], zero[:, :], ACT.Copy)
                if at + proj < cols + 2:
                    act.activation(raw[i % 2][:, cols + 1:cols + 2], zero[:, :], ACT.Copy)
                computed(act, j, c, g)
                act.activation(raw[i % 2][:, at:at + proj], bank[u % 6][:, 0:proj], ACT.Copy).then_inc(free[u % 6], 1)

            def to_side(j, c, g):
                u = unit(j, c)
                proj, _, first, cols = geometry(c)
                if j == "c":
                    if c < 2:
                        act.wait_ge(side_stored[c], g * (8 * NC) + 16)
                    else:
                        evacuated(act, "h", c - 2, g)
                    computed(act, j, c, g)
                    m = act.activation(side[c % 2][:, 0:proj], bank[u % 6][:, 0:proj], ACT.Copy)
                else:
                    evacuated(act, "h", NC - 2 + c % 2, g)
                    act.wait_ge(side_stored[c % 2], g * (8 * NC) + 16 * (c // 2 + 1))
                    computed(act, j, c, g)
                    m = act.activation(side[c % 2][:, 0:cols], bank[u % 6][:, first:first + cols], ACT.Silu)
                m.then_inc(free[u % 6], 1)

            def silu(j, c, g):
                cols, o = geometry(c)[3], out[item(j, c) % 4]
                is_convolved(act, item(j, c), g)
                act.activation(o[:, 0:cols], o[:, 0:cols], ACT.Silu).then_inc(silued, 1)

            def square(j, c, g):
                cols, o = geometry(c)[3], out[item(j, c) % 4]
                if j == "b":
                    evacuated(act, "b", c, g)
                else:
                    act.wait_ge(silued, g * NORMS + (silu_no(j, c) + 1))
                act.activation(sq[:, 0:cols], o[:, 0:cols], ACT.Square).then_inc(squared, 1)

            def roots(j, c, g):
                cols, n = geometry(c)[3], norm_no(j, c)
                scale, bias = {"b": (1.0 / 64, k["eps"]), "q": (float(P), k["eps128"]), "k": (1.0, k["eps"])}[j]
                act.wait_ge(nready[n % 2], g * (NORMS // 2) + (n // 2 + 1))
                act.wait_ge(normed, g * NORMS + (n + 1))
                act.activation(nrm[:, 0:cols], nbank[n % 2][:, 0:cols], ACT.Sqrt, bias=bias[:, :], scale=scale).then_inc(nfree[n % 2], 1)

            act.wait_ge(cleared, 1)
            with act.Fori(0, G) as g:
                for c in range(NC):
                    to_side("c", c, g)
                    if c:
                        square("b", c - 1, g)
                        roots("b", c - 1, g)
                square("b", NC - 1, g)
                for c in range(NC):
                    to_raw("q", c, g)
                    roots(*(("q", c - 1) if c else ("b", NC - 1)), g)
                    to_side("z", c, g)
                    silu("q", c, g)
                    square("q", c, g)
                for c in range(NC):
                    to_raw("k", c, g)
                    roots(*(("k", c - 1) if c else ("q", NC - 1)), g)
                    to_raw("v", c, g)
                    silu("k", c, g)
                    square("k", c, g)
                    silu("v", c, g)
                roots("k", NC - 1, g)
            for c in range(NCH):
                act.wait_ge(side_stored[c % 2], 16 * (G * NC // 2 + c // 2 + 1))
                act.wait_ge(ready[c], G * (UNITS // 6) + 1)
                act.activation(side[c % 2][0:16, 0:CH], bank[c][0:16, 0:CH], ACT.Copy).then_inc(ab_set, 1)

        @block.vector
        def _(dve):
            dve.memset(zero[:, :], 0.0).then_inc(cleared, 1)
            for sem in free + nfree + [convolved, convolved, normed]:
                dve.sem_inc(sem, 1)

            def gate_h(c, g):
                u, i = unit("h", c), item("b", c)
                proj, at, _, cols = geometry(c)
                is_convolved(dve, i - 2, g)
                if at:
                    dve.memset(raw[i % 2][:, 0:1], 0.0)
                if at + proj < cols + 2:
                    dve.memset(raw[i % 2][:, cols + 1:cols + 2], 0.0)
                evacuated(dve, "c", c, g)
                computed(dve, "h", c, g)
                dve.tensor_tensor(raw[i % 2][:, at:at + proj], bank[u % 6][:, 0:proj], side[c % 2][:, 0:proj], ALU.mult).then_inc(free[u % 6], 1)

            def conv(j, c, g):
                i, cols = item(j, c), geometry(c)[3]
                src, dst = raw[i % 2], out[i % 4][:, 0:cols]
                table, row = (k["cw_mix"], g) if j == "b" else (k["cw_qkv"], g + "qkv".index(j) * HEADS)
                w = [table[:, bass.ds(row, 1), n:n + 1].rearrange("p a b -> p (a b)") for n in range(3)]
                evacuated(dve, "h" if j == "b" else j, c, g)
                dve.wait_ge(stored[i % 4], g * (16 * ITEMS // 4) + 16 * (i // 4 + 1))
                dve.tensor_scalar(dst, src[:, 0:cols], w[0], None, ALU.mult).then_inc(chain, 1)
                dve.wait_ge(chain, g * (2 * ITEMS) + (2 * i + 1))
                dve.scalar_tensor_tensor(out=dst, in0=src[:, 1:cols + 1], scalar=w[1], in1=dst, op0=ALU.mult, op1=ALU.add).then_inc(chain, 1)
                dve.wait_ge(chain, g * (2 * ITEMS) + (2 * i + 2))
                dve.scalar_tensor_tensor(out=dst, in0=src[:, 2:cols + 2], scalar=w[2], in1=dst, op0=ALU.mult, op1=ALU.add).then_inc(convolved, 1)

            def gate_b(c, g):
                u, i = unit("b", c), item("b", c)
                _, _, first, cols = geometry(c)
                o = out[i % 4][:, 0:cols]
                is_convolved(dve, i, g)
                computed(dve, "b", c, g)
                dve.tensor_tensor(o, bank[u % 6][:, first:first + cols], o, ALU.mult).then_inc(free[u % 6], 1)

            def norm(j, c, g):
                n, cols = norm_no(j, c), geometry(c)[3]
                o, r = out[item(j, c) % 4][:, 0:cols], nrm[:, 0:cols]
                dve.wait_ge(nfree[n % 2], g * (NORMS // 2) + (n // 2 + 2))
                dve.reciprocal(r, r).then_inc(inverted, 1)
                dve.wait_ge(inverted, g * NORMS + (n + 1))
                if j == "b":
                    m = dve.scalar_tensor_tensor(out=o, in0=o, scalar=k["cg_mix"][:, bass.ds(g, 1)], in1=r, op0=ALU.mult, op1=ALU.mult)
                else:
                    m = dve.tensor_tensor(o, o, r, ALU.mult)
                m.then_inc(normed, 1)

            with dve.Fori(0, G) as g:
                for c in range(NC):
                    gate_h(c, g)
                    conv("b", c, g)
                    if c:
                        norm("b", c - 1, g)
                    gate_b(c, g)
                for c in range(NC):
                    conv("q", c, g)
                    norm(*(("q", c - 1) if c else ("b", NC - 1)), g)
                for c in range(NC):
                    conv("k", c, g)
                    norm(*(("k", c - 1) if c else ("q", NC - 1)), g)
                    conv("v", c, g)
                norm("k", NC - 1, g)


def decays(nc, k, ab_rows, gates, O):
    with ExitStack() as ctx:
        b = Bufs(nc, ctx, "decays_")
        abT, ab = b.sb("abT", [16, T]), b.sb("ab", [P, NT, 4 * HEADS])
        loaded = b.sem("ab_loaded")
        x, nx = b.sb("ab_x", [P, NT, 8]), b.sb("ab_nx", [P, NT, 8])
        ex, lg = b.sb("ab_exp", [P, NT, 8]), b.sb("ab_log", [P, NT, 8])
        eb, eb1, rate = b.sb("ab_eb", [P, NT, 8]), b.sb("ab_eb1", [P, NT, 8]), b.sb("rate", [P, 8])
        gg = b.sb("ab_g", [P, 2, NT, HEADS])
        tail = b.sb("ab_tail", [P, 2, NT, HEADS])
        pab = b.ps("pab", [P, NT * 4 * HEADS])
        pg = [b.ps(f"pg{d}", [P, 2, NT, HEADS]) for d in range(2)]
        turned, dv, ac, g_done, sums = b.sem("ab_turned"), b.sem("ab_vector"), b.sem("ab_scalar"), b.sem("ab_g_done"), b.sem("ab_sums")
        block = ctx.enter_context(nc.Block())

        @block.sync
        def _(sp):
            sp.dma_start(abT[:, :], ab_rows).then_inc(loaded, 16)

        @block.gpsimd
        def _(pool):
            pool.memset(O[:, :, :], 0.0)

        @block.tensor
        def _(pe):
            pe.wait_ge(loaded, 16)
            for t in range(NT):
                m = pe.transpose(pab[:, t * 16:(t + 1) * 16], abT[0:16, t * P:(t + 1) * P], k["ident"][0:16, 0:16])
            m.then_inc(turned, 1)
            pe.wait_ge(g_done, 2)
            for d in range(2):
                pe.matmul(pg[d][:, 0], k["tri"][:, d, :], gg[:, d], start=True, stop=True, skip_group_check=True)
                m = pe.matmul(pg[d][:, 1], k["ones"][:, :], gg[:, d], start=False, stop=True, skip_group_check=True)
            m.then_inc(sums, 1)

        @block.vector
        def _(dve):
            n = [0]

            def link(m):
                n[0] += 1
                m.then_inc(dv, 1)
                dve.wait_ge(dv, n[0])

            dve.wait_ge(turned, 1)
            link(dve.tensor_copy(ab[:, :, :], pab[:, :].rearrange("p (t c) -> p t c", c=16)))
            link(dve.tensor_tensor(x[:, :, :], ab[:, :, 0:8], bcast(k["dtb"][:, :], NT, 1), ALU.add))
            link(dve.tensor_scalar(nx[:, :, :], x[:, :, :], -1.0, None, ALU.mult))
            link(dve.tensor_tensor(nx[:, :, :], nx[:, :, :], x[:, :, :], ALU.min))
            dve.wait_ge(ac, 4)
            link(dve.scalar_tensor_tensor(out=x[:, :, :], in0=x[:, :, :], scalar=0.0, in1=lg[:, :, :], op0=ALU.max, op1=ALU.add))
            for d in range(2):
                dve.scalar_tensor_tensor(out=gg[:, d], in0=x[:, :, 4 * d:4 * d + 4], scalar=-1.0,
                                         in1=bcast(rate[:, 4 * d:4 * d + 4], NT, 1), op0=ALU.mult, op1=ALU.mult).then_inc(g_done, 1)
            dve.wait_ge(g_done, 2)
            link(dve.tensor_scalar(eb1[:, :, :], eb[:, :, :], 1.0, None, ALU.add))
            for d in range(2):
                dve.tensor_copy(gates[:, d, :, 16:20], gg[:, d])
                dve.reciprocal(gates[:, d, :, 4:8], eb1[:, :, 4 * d:4 * d + 4])
            dve.wait_ge(sums, 1)
            for d in range(2):
                link(dve.tensor_copy(gates[:, d, :, 0:4], pg[d][:, 0]))
                link(dve.tensor_tensor(tail[:, d], pg[d][:, 1], gates[:, d, :, 0:4], ALU.subtract))

        @block.scalar
        def _(act):
            act.activation(rate[:, :], k["alog"][:, :], ACT.Exp).then_inc(ac, 1)
            act.wait_ge(dv, 4)
            act.activation(ex[:, :, :], nx[:, :, :], ACT.Exp).then_inc(ac, 1)
            act.activation(eb[:, :, :], ab[:, :, 8:16], ACT.Exp, scale=-1.0).then_inc(ac, 1)
            act.wait_ge(ac, 3)
            act.activation(lg[:, :, :], ex[:, :, :], ACT.Ln, bias=k["one"][:, :]).then_inc(ac, 1)
            act.wait_ge(dv, 10)
            for d in range(2):
                act.activation(gates[:, d, :, 8:12], tail[:, d], ACT.Exp)
                act.activation(gates[:, d, :, 12:16], pg[d][:, 1], ACT.Exp)


def delta(nc, k, gates, feat, O):
    with ExitStack() as ctx:
        b = Bufs(nc, ctx, "delta_")
        L = []
        for d in range(2):
            v = {n: b.sb(f"{n}{d}", [P, HEADS, P]) for n in "dg eg diff dec lt Tm X rv vn S".split()}
            for n in "keT qdT kdec vtok qkT R".split():
                v[n] = [b.sb(f"{n}{d}_{r}", [P, HEADS, P]) for r in range(2)]
            v["gs"] = [b.sb(f"gs{d}_{r}", [P, 20]) for r in range(2)]
            v["in"] = b.sb(f"qkv{d}", [P, 3 * HEADS, P])
            v["M"] = b.sb(f"M{d}", [P, LEVELS, HEADS, P])
            v["A"] = [b.ps(f"prep{d}{n}", [P, HEADS, P]) for n in range(2)]
            v["B"] = [b.ps(f"scan{d}{n}", [P, HEADS, P]) for n in range(2)]
            L.append(v)
        sems = ("loaded gates_set gsum_in gsum kk qk kturned vturned eg_set diff_set masked dec_set lt_set qkT_set keT_set "
                "qdT_set M_set kdec_set vtok_set R_set Tturned T_set T_last_set X_ready X_set dR_ready kS_ready rv_set Tv_ready vn_set "
                "o_ready o_added kv_ready S_set").split()
        E = [{n: b.sem(f"{n}{d}") for n in sems} for d in range(2)]
        block = ctx.enter_context(nc.Block())
        lanes = [(d, L[d], E[d]) for d in range(2)]

        def tile(d, s):
            if isinstance(s, int) and s >= LT_TILES:
                return s if d == 0 else NT - 1 - (s - LT_TILES)
            return s if d == 0 else s * -1 + (LT_TILES - 1)

        def run(eng, step):
            step(0, None, 0)
            with eng.Fori(0, (LT_TILES - 2) // 2) as j:
                step(j * 2 + 1, j * 2, 1)
                step(j * 2 + 2, j * 2 + 1, 0)
            for a in range(LT_TILES - 1, NT):
                step(a, a - 1, a % 2)
            step(None, NT - 1, 0)

        def state(c):
            return c + 2 if isinstance(c, int) and c >= LT_TILES else c + 1

        @block.sync
        def _(sp):
            def step(a, c, r):
                if a is None:
                    return
                for d, v, e in lanes:
                    wait_if_any(sp, e["qdT_set"], a)
                    wait_if_any(sp, e["qk"], a)
                    sp.dma_start(v["in"][:, :, :], feat[0:3 * HEADS, :, bass.ds(tile(d, a) * P, P)]
                                 .rearrange("c p t -> p c t")).then_inc(e["loaded"], 16)

            run(sp, step)

        @block.gpsimd
        def _(pool):
            def decays(a, r):
                for d, v, e in lanes:
                    pool.wait_ge(e["gates_set"], a + 1)
                    wait_if_any(pool, e["gsum"], a)
                    pool.tensor_tensor(v["dg"][:, :, :], bcast(k["tri"][:, d, :], HEADS, 1), bcast(v["gs"][r][:, 16:20], P, 2),
                                       ALU.mult).then_inc(e["gsum_in"], 1)

            def step(a, c, r):
                if a is None:
                    return
                for d, v, e in lanes:
                    pool.wait_ge(e["diff_set"], a + 1)
                    pool.tensor_tensor(v["diff"][:, :, :], v["diff"][:, :, :], bcast(k["neg"][:, d, :], HEADS, 1),
                                       ALU.add).then_inc(e["masked"], 1)
                for l in range(LEVELS):
                    for d, v, e in lanes:
                        if l == 0:
                            wait_if_any(pool, e["X_ready"], a * 6)
                            pool.wait_ge(e["lt_set"], a + 1)
                        pool.tensor_tensor(v["M"][:, l], v["lt"][:, :, :], bcast(k["lvl"][:, d, l, :], HEADS, 1),
                                           ALU.mult).then_inc(e["M_set"], 1)
                for d, v, e in lanes:
                    pool.wait_ge(e["eg_set"], a + 1)
                    if not isinstance(a, int) or a >= 2:
                        pool.wait_ge(e["o_ready"], c)
                    pool.tensor_tensor(v["keT"][r][:, :, :], v["in"][:, HEADS:2 * HEADS, :], v["eg"][:, :, :], ALU.mult).then_inc(e["keT_set"], 1)
                    pool.tensor_tensor(v["qdT"][r][:, :, :], v["in"][:, 0:HEADS, :], v["eg"][:, :, :], ALU.mult).then_inc(e["qdT_set"], 1)
                if not isinstance(a, int) or a + 1 < NT:
                    decays(a + 1, 1 - r)

            decays(0, 0)
            run(pool, step)

        @block.scalar
        def _(act):
            def step(a, c, r):
                if a is None:
                    return
                for d, v, e in lanes:
                    act.wait_ge(e["gsum"], a + 1)
                    wait_if_any(act, e["qdT_set"], a)
                    act.activation(v["eg"][:, :, :], v["A"][0][:, :, :], ACT.Exp).then_inc(e["eg_set"], 1)
                for d, v, e in lanes:
                    act.wait_ge(e["masked"], a + 1)
                    wait_if_any(act, e["qkT_set"], a)
                    act.activation(v["dec"][:, :, :], v["diff"][:, :, :], ACT.Exp).then_inc(e["dec_set"], 1)
                for d, v, e in lanes:
                    act.wait_ge(e["vturned"], a + 1)
                    if not isinstance(a, int) or a >= 2:
                        act.wait_ge(e["rv_set"], c)
                    act.activation(v["vtok"][r][:, :, :], v["A"][1][:, :, :], ACT.Copy).then_inc(e["vtok_set"], 1)
                for l in range(1, LEVELS):
                    for d, v, e in lanes:
                        if l == LEVELS - 1:
                            act.wait_ge(e["Tturned"], a + 1)
                            act.activation(v["Tm"][:, :, :], v["A"][0][:, :, :], ACT.Copy).then_inc(e["T_last_set"], 1)
                    for d, v, e in lanes:
                        act.wait_ge(e["X_ready"], a * 6 + l)
                        act.activation(v["X"][:, :, :], v["A"][1][:, :, :], ACT.Copy).then_inc(e["X_set"], 1)

            run(act, step)

        @block.tensor
        def _(pe):
            def by_heads(out, lhsT, rhs, start=True, stop=True):
                for h in range(HEADS):
                    m = pe.matmul(out[:, h], lhsT(h), rhs(h), start=start and h == 0, stop=stop, skip_group_check=True)
                return m

            def turn(out, src):
                for h in range(HEADS):
                    m = pe.transpose(out[:, h], src(h), k["ident"][:, :])
                return m

            def products(a, r, n):
                for d, v, e in lanes:
                    q, kk, vv = (lambda h, o=o: v["in"][:, o * HEADS + h, :] for o in range(3))
                    if n == 0:
                        wait_if_any(pe, e["R_set"], a * 7)
                        pe.wait_ge(e["gsum_in"], a + 1)
                        pe.matmul(v["A"][0][:, :, :], k["ones"][:, :], v["dg"][:, :, :], start=True, stop=True).then_inc(e["gsum"], 1)
                    elif n == 1:
                        pe.wait_ge(e["loaded"], a * 16 + 16)
                        turn(v["A"][1], kk).then_inc(e["kturned"], 1)
                    elif n == 2:
                        pe.wait_ge(e["eg_set"], a + 1)
                        pe.wait_ge(e["diff_set"], a + 1)
                        by_heads(v["A"][0], kk, kk).then_inc(e["kk"], 1)
                    elif n == 3:
                        pe.wait_ge(e["kdec_set"], a + 1)
                        turn(v["A"][1], vv).then_inc(e["vturned"], 1)
                    else:
                        pe.wait_ge(e["vtok_set"], a + 1)
                        by_heads(v["A"][1], kk, q).then_inc(e["qk"], 1)

            def inverse(a, r, l, n):
                for d, v, e in lanes:
                    R = lambda h: v["R"][r][:, h, :]
                    if n == 0:
                        if l == LEVELS - 1:
                            pe.wait_ge(e["R_set"], a * 7 + l)
                            turn(v["A"][0], R).then_inc(e["Tturned"], 1)
                    elif n == 1:
                        if l == LEVELS - 1:
                            pe.wait_ge(e["T_last_set"], a + 1)
                        else:
                            pe.wait_ge(e["T_set"], a * (LEVELS - 2) + l)
                        pe.wait_ge(e["M_set"], a * 7 + (l + 1))
                        if l == 1:
                            pe.wait_ge(e["qkT_set"], a + 1)
                        by_heads(v["A"][1], lambda h: v["M"][:, l, h, :], lambda h: v["Tm"][:, h, :]).then_inc(e["X_ready"], 1)
                    else:
                        pe.wait_ge(e["X_set"], a * 6 + l)
                        by_heads(v["A"][0], lambda h: v["X"][:, h, :], R).then_inc(e["dR_ready"], 1)

            def scan(c, r, n, which):
                for d, v, e in which:
                    of = lambda name: lambda h: v[name][r][:, h, :]
                    S, rv, vn = (lambda h, x=x: v[x][:, h, :] for x in ("S", "rv", "vn"))
                    if n == 0:
                        pe.wait_ge(e["S_set"], state(c))
                        pe.wait_ge(e["keT_set"], c + 1)
                        by_heads(v["B"][0], of("keT"), S).then_inc(e["kS_ready"], 1)
                    elif n == 1:
                        pe.wait_ge(e["rv_set"], c + 1)
                        pe.wait_ge(e["R_set"], c * 7 + 7)
                        by_heads(v["B"][1], of("R"), rv).then_inc(e["Tv_ready"], 1)
                    elif n == 2:
                        pe.wait_ge(e["qdT_set"], c + 1)
                        by_heads(v["B"][0], of("qdT"), S, stop=False)
                    elif n == 3:
                        pe.wait_ge(e["vn_set"], c + 1)
                        by_heads(v["B"][1], of("kdec"), vn).then_inc(e["kv_ready"], 1)
                    else:
                        by_heads(v["B"][0], of("qkT"), vn, start=False).then_inc(e["o_ready"], 1)

            def step(a, c, r):
                s = (lambda n, which=lanes: scan(c, 1 - r, n, which)) if c is not None else (lambda n, which=lanes: None)
                if a is None:
                    for n in range(5):
                        s(n)
                    return
                products(a, r, 0)
                products(a, r, 1)
                products(a, r, 2)
                s(0)
                products(a, r, 3)
                s(1)
                products(a, r, 4)
                s(2)
                for l in range(1, LEVELS):
                    inverse(a, r, l, 0)
                    inverse(a, r, l, 1)
                    inverse(a, r, l, 2)
                    if l <= 4:
                        s(3 + (l - 1) % 2, lanes[(l - 1) // 2:(l - 1) // 2 + 1])

            run(pe, step)

        @block.vector
        def _(dve):
            def take_gates(a, r):
                for d, v, e in lanes:
                    if not isinstance(a, int) or a >= 2:
                        dve.wait_ge(e["gsum_in"], a - 1)
                    dve.tensor_copy(v["gs"][r][:, :], gates[:, d, bass.ds(tile(d, a), 1), :]
                                    .rearrange("p a c -> p (a c)")).then_inc(e["gates_set"], 1)

            def residual(c, r):
                for d, v, e in lanes:
                    dve.wait_ge(e["vtok_set"], c + 1)
                    dve.wait_ge(e["kS_ready"], c + 1)
                    dve.tensor_tensor(v["rv"][:, :, :], v["vtok"][r][:, :, :], v["B"][0][:, :, :], ALU.subtract).then_inc(e["rv_set"], 1)

            def new_values(c, r):
                for d, v, e in lanes:
                    dve.wait_ge(e["Tv_ready"], c + 1)
                    dve.tensor_tensor(v["vn"][:, :, :], v["B"][1][:, :, :], bcast(v["gs"][r][:, 4:8], P, 2), ALU.mult).then_inc(e["vn_set"], 1)

            def finish(d, c, r):
                v, e = L[d], E[d]
                dve.wait_ge(e["o_ready"], c + 1)
                wait_if_any(dve, E[1 - d]["o_added"], c)
                out = O[:, bass.ds(tile(d, c), 1), :].rearrange("p a (h c) -> p (a h) c", h=HEADS)
                dve.tensor_tensor(out, v["B"][0][:, :, :], out, ALU.add).then_inc(e["o_added"], 1)
                dve.wait_ge(e["kv_ready"], c + 1)
                dve.wait_ge(e["S_set"], state(c))
                for h in range(HEADS):
                    m = dve.scalar_tensor_tensor(out=v["S"][:, h, :], in0=v["S"][:, h, :], scalar=v["gs"][r][:, 12 + h:13 + h],
                                                 in1=v["B"][1][:, h], op0=ALU.mult, op1=ALU.add)
                m.then_inc(e["S_set"], 1)

            def clear_state(c):
                for d, v, e in lanes:
                    if c:
                        dve.wait_ge(e["S_set"], c + 1)
                    dve.memset(v["S"][:, :, :], 0.0).then_inc(e["S_set"], 1)

            def step(a, c, r):
                if a is None:
                    residual(c, 1 - r)
                    new_values(c, 1 - r)
                    for d in range(2):
                        finish(d, c, 1 - r)
                    return
                if isinstance(c, int) and c == LT_TILES:
                    clear_state(c)
                for d, v, e in lanes:
                    dve.wait_ge(e["gates_set"], a + 1)
                    wait_if_any(dve, e["dec_set"], a)
                    dve.wait_ge(e["eg_set"], a + 1)
                    dve.tensor_tensor(v["diff"][:, :, :], v["A"][0][:, :, :], bcast(v["gs"][r][:, 0:4], P, 2), ALU.subtract).then_inc(e["diff_set"], 1)
                for d, v, e in lanes:
                    dve.wait_ge(e["kturned"], a + 1)
                    dve.tensor_tensor(v["kdec"][r][:, :, :], v["A"][1][:, :, :], bcast(v["gs"][r][:, 8:12], P, 2), ALU.mult).then_inc(e["kdec_set"], 1)
                if c is not None:
                    residual(c, 1 - r)
                for d, v, e in lanes:
                    dve.wait_ge(e["dec_set"], a + 1)
                    dve.wait_ge(e["kk"], a + 1)
                    wait_if_any(dve, e["M_set"], a * 7)
                    for h in range(HEADS):
                        m = dve.scalar_tensor_tensor(out=v["lt"][:, h, :], in0=v["A"][0][:, h], scalar=v["gs"][r][:, 4 + h:5 + h],
                                                     in1=v["dec"][:, h, :], op0=ALU.mult, op1=ALU.mult)
                    m.then_inc(e["lt_set"], 1)
                def turn(v, e, l):
                    dve.wait_ge(e["R_set"], a * 7 + (l + 1))
                    flat = [x.rearrange("p h c -> p (h c)") for x in (v["Tm"][:, :, :], v["R"][r][:, :, :])]
                    dve.transpose(*flat).then_inc(e["T_set"], 1)

                for d, v, e in lanes:
                    dve.wait_ge(e["M_set"], a * 7 + 1)
                    dve.tensor_tensor(v["R"][r][:, :, :], bcast(k["ident"][:, :], HEADS, 1), v["M"][:, 0], ALU.subtract).then_inc(e["R_set"], 1)
                    turn(v, e, 0)
                    dve.wait_ge(e["qk"], a + 1)
                    dve.tensor_tensor(v["qkT"][r][:, :, :], v["A"][1][:, :, :], v["dec"][:, :, :], ALU.mult).then_inc(e["qkT_set"], 1)
                if c is not None:
                    new_values(c, 1 - r)
                for l in range(1, LEVELS):
                    for d, v, e in lanes:
                        dve.wait_ge(e["R_set"], a * 7 + l)
                        dve.wait_ge(e["dR_ready"], a * 6 + l)
                        dve.tensor_tensor(v["R"][r][:, :, :], v["R"][r][:, :, :], v["A"][0][:, :, :], ALU.subtract).then_inc(e["R_set"], 1)
                        if l < LEVELS - 2:
                            turn(v, e, l)
                    if c is not None and 3 <= l <= 4:
                        finish(l - 3, c, 1 - r)
                    if l == 4 and (not isinstance(a, int) or a + 1 < NT):
                        if c is not None:
                            for d, v, e in lanes:
                                dve.wait_ge(e["S_set"], state(c) + 1)
                        take_gates(a + 1, 1 - r)

            clear_state(0)
            take_gates(0, 0)
            run(dve, step)


def software_pipeline(eng, step):
    for u in range(3):
        step(u % 2, u)
    with eng.Fori(1, (NT - 2) // 2) as j:
        step(1, j * 2 + 1)
        step(0, j * 2 + 2)
    for u in (NT - 1, NT):
        step(u % 2, u)


def parts_of(u):
    if not isinstance(u, int):
        return True, True, True
    return u < NT, u + 1 < NT, u >= 1


def wait_if_any(eng, sem, value):
    if not isinstance(value, int) or value > 0:
        eng.wait_ge(sem, value)


def output(nc, k, dram, feat, O, lg, x2_rows, xn_rows):
    with ExitStack() as ctx:
        b = Bufs(nc, ctx, "output_")
        (wo,), (wl,) = over(nc, b, ("wo",), [P, KD, D])
        wh, g2 = b.sb("wo_high", [P, KD, D], F32R), b.sb("g2", [P, D])
        rw, rb, dg = b.sb("router_w", [P, KD, NG + NE]), b.sb("router_b", [P, NG + NE]), b.sb("dn_gain", [P, 1])
        pair = lambda name, shape, dt=F32: [b.sb(f"{name}{p}", shape, dt) for p in range(2)]
        mh, ml = pair("mixT_high", [P, KD, P], F32R), pair("mixT_low", [P, KD, P], F32R)
        mixT, z, x = pair("mixT", [P, KD, P]), pair("z", [P, HEADS, P]), pair("xres", [P, D])
        on, x2, xn, xT = pair("on", [P, HEADS, P]), pair("x2", [P, D]), pair("xn", [P, D]), pair("xT", [P, KD, P])
        ss, rt, ri = pair("oss", [P, HEADS]), pair("ort", [P, HEADS]), pair("ori", [P, HEADS])
        ss2, rt2, ri2 = pair("xss", [P, 1]), pair("xrt", [P, 1]), pair("xri", [P, 1])
        junk, junk2 = b.sb("junk_o", [P, HEADS, P]), b.sb("junk_x", [P, D])
        tA, lgp = b.ps("on_turned", [P, HEADS, P]), b.ps("logits", [P, 512])
        Y = [b.ps(f"yo{n}", [P, 512]) for n in range(2)]
        tX = [b.ps(f"x_turned{n}", [P, 4, P]) for n in range(2)]
        names = ("o_squared o_rooted o_inverted on_set on_turned mix_set y_ready x2_set x_squared x_rooted x_inverted "
                 "xn_set x_turned xT_set lg_ready lg_set w_high w_split m_high m_split splits_begun").split()
        e = {n: b.sem("out_" + n) for n in names}
        const = b.sem("out_const")
        loaded = [b.sem(f"out_loaded{p}") for p in range(2)]
        x2_st = [b.sem(f"x2_stored{p}") for p in range(2)]
        xn_st = [b.sem(f"xn_stored{p}") for p in range(2)]
        block = ctx.enter_context(nc.Block())
        wo_in = [b.sem(f"wo_loaded{i}") for i in range(KD)]
        CONSTS = 4 * 16

        def through_slot(eng, sem, t, p, each):
            eng.wait_ge(sem, (t - p) * (each // 2) + each)

        @block.sync
        def _(sp):
            def load(p, t):
                cols = bass.ds(t * P, P)
                sp.dma_start(mixT[p][:, 0:4, :], feat[16:20, :, cols].rearrange("c p t -> p c t")).then_inc(loaded[p], 16)
                sp.dma_start(z[p][:, :, :], feat[12:16, :, cols].rearrange("c p t -> p c t")).then_inc(loaded[p], 16)
                sp.dma_start(x[p][:, :], dram["x"][cols, :]).then_inc(loaded[p], 16)

            def store_sum(p, t):
                sp.dma_start(x2_rows[bass.ds(t * P, P), :], x2[p][:, :]).then_inc(x2_st[p], 16)

            def store_normed(p, t):
                sp.dma_start(xn_rows[bass.ds(t * P, P), :], xn[p][:, :]).then_inc(xn_st[p], 16)

            sp.dma_start(dg[:, :], dram["dn_norm_g"]).then_inc(const, 16)
            for p in range(2):
                load(p, p)
            for dst, src in ((g2[:, :], dram["norm2_g"].partition_broadcast(P)),
                             (rw[:, :, :], dram["router_w"].rearrange("(k p) n -> p k n", p=P)),
                             (rb[:, :], dram["router_b"].partition_broadcast(P))):
                sp.dma_start(dst, src).then_inc(const, 16)
            for i in range(KD):
                sp.dma_start(wo[:, i, :], dram["w_o"][i * P:(i + 1) * P, :]).then_inc(wo_in[i], 16)
            with sp.Fori(1, NT // 2) as j:
                for p in range(2):
                    t = j * 2 + p
                    sp.wait_ge(e["x2_set"], t - 1)
                    load(p, t)
                    store_sum(p, t - 2)
                    sp.wait_ge(e["xn_set"], t - 1)
                    store_normed(p, t - 2)
            for p in range(2):
                sp.wait_ge(e["x2_set"], NT - 1 + p)
                store_sum(p, NT - 2 + p)
                sp.wait_ge(e["xn_set"], NT - 1 + p)
                store_normed(p, NT - 2 + p)
            for p in range(2):
                sp.wait_ge(x2_st[p], 8 * NT)
                sp.wait_ge(xn_st[p], 8 * NT)

        @block.scalar
        def _(act):
            def begin(p, t):
                for h in range(HEADS):
                    src = O[:, bass.ds(t, 1), h * P:(h + 1) * P].rearrange("p a c -> p (a c)")
                    m = act.activation(junk[:, h, :], src, ACT.Square, accum_out=ss[p][:, h:h + 1])
                m.then_inc(e["o_squared"], 1)
                act.wait_ge(e["o_squared"], t + 1)
                act.activation(rt[p][:, :], ss[p][:, :], ACT.Sqrt, bias=k["eps"][:, :], scale=1.0 / P).then_inc(e["o_rooted"], 1)

            def step(p, u):
                project_, begin_, end_ = parts_of(u)
                t = u - 1
                if end_:
                    act.wait_ge(e["x2_set"], t + 1)
                    act.activation(junk2[:, :], x2[1 - p][:, :], ACT.Square, accum_out=ss2[1 - p][:, :]).then_inc(e["x_squared"], 1)
                    act.wait_ge(e["x_squared"], t + 1)
                    act.activation(rt2[1 - p][:, :], ss2[1 - p][:, :], ACT.Sqrt, bias=k["eps"][:, :], scale=1.0 / D).then_inc(e["x_rooted"], 1)
                if begin_:
                    begin(1 - p, u + 1)
                if end_:
                    act.wait_ge(e["x_turned"], t + 1)
                    for n in range(2):
                        m = act.activation(xT[1 - p][:, 4 * n:4 * n + 4, :], tX[n][:, :, :], ACT.Copy)
                    m.then_inc(e["xT_set"], 1)

            begin(0, 0)
            for i in range(KD):
                act.wait_ge(wo_in[i], 16)
                act.activation(wh[:, i, :], wo[:, i, :], ACT.Copy).then_inc(e["w_high"], 1)
            software_pipeline(act, step)

        @block.tensor
        def _(pe):
            def begin(p, t):
                pe.wait_ge(e["on_set"], t + 1)
                for h in range(HEADS):
                    m = pe.transpose(tA[:, h], on[p][:, h, :], k["ident"][:, :])
                m.then_inc(e["on_turned"], 1)

            def project_half(p, u, n):
                for kt in range(KD):
                    if n == 0 and isinstance(u, int) and u == 0:
                        pe.wait_ge(e["w_split"], kt + 1)
                    high, low = (t[:, kt, n * 512:(n + 1) * 512] for t in (wh, wl))
                    for i, (x, w) in enumerate(((mh, high), (mh, low), (ml, high))):
                        m = pe.matmul(Y[n][:, :], x[p][:, kt, :], w, start=kt == 0 and i == 0, stop=kt == KD - 1 and i == 2)
                return m

            def step(p, u):
                project_, begin_, end_ = parts_of(u)
                t = u - 1
                if project_:
                    pe.wait_ge(e["m_split"], u * 2 + 2)
                    wait_if_any(pe, e["x2_set"], u)
                    project_half(p, u, 0)
                if begin_:
                    begin(1 - p, u + 1)
                if end_:
                    pe.wait_ge(e["xn_set"], t + 1)
                    wait_if_any(pe, e["xT_set"], t)
                    for c in range(KD):
                        m = pe.transpose(tX[c // 4][:, c % 4, :], xn[1 - p][:, c * P:(c + 1) * P], k["ident"][:, :])
                    m.then_inc(e["x_turned"], 1)
                if project_:
                    project_half(p, u, 1).then_inc(e["y_ready"], 1)
                if end_:
                    pe.wait_ge(e["xT_set"], t + 1)
                    wait_if_any(pe, e["lg_set"], t)
                    for kt in range(KD):
                        m = pe.matmul(lgp[:, 0:NG + NE], xT[1 - p][:, kt, :], rw[:, kt, :], start=kt == 0, stop=kt == KD - 1)
                    m.then_inc(e["lg_ready"], 1)

            begin(0, 0)
            pe.wait_ge(const, CONSTS)
            software_pipeline(pe, step)

        @block.vector
        def _(dve):
            def begin(p, t):
                dve.wait_ge(e["o_rooted"], t + 1)
                dve.reciprocal(ri[p][:, :], rt[p][:, :]).then_inc(e["o_inverted"], 1)
                dve.wait_ge(e["o_inverted"], t + 1)
                src = O[:, bass.ds(t, 1), :].rearrange("p a (h c) -> p (a h) c", h=HEADS)
                dve.tensor_tensor(on[p][:, :, :], src, bcast(ri[p][:, :], P, 2), ALU.mult).then_inc(e["on_set"], 1)

            def gate(p, t):
                dve.wait_ge(e["on_turned"], t + 1)
                through_slot(dve, loaded[p], t, p, 48)
                dve.scalar_tensor_tensor(out=mixT[p][:, 4:8, :], in0=tA[:, :, :], scalar=dg[:, :], in1=z[p][:, :, :],
                                         op0=ALU.mult, op1=ALU.mult).then_inc(e["mix_set"], 1)

            def step(p, u):
                project_, begin_, end_ = parts_of(u)
                t = u - 1
                if end_:
                    dve.wait_ge(e["x_rooted"], t + 1)
                    dve.reciprocal(ri2[1 - p][:, :], rt2[1 - p][:, :]).then_inc(e["x_inverted"], 1)
                    dve.wait_ge(e["x_inverted"], t + 1)
                    wait_if_any(dve, xn_st[1 - p], (t - (1 - p)) * 8)
                    dve.scalar_tensor_tensor(out=xn[1 - p][:, :], in0=x2[1 - p][:, :], scalar=ri2[1 - p][:, :], in1=g2[:, :],
                                             op0=ALU.mult, op1=ALU.mult).then_inc(e["xn_set"], 1)
                if begin_:
                    begin(1 - p, u + 1)
                if begin_:
                    gate(1 - p, u + 1)
                if project_:
                    dve.wait_ge(e["y_ready"], u + 1)
                    wait_if_any(dve, x2_st[p], (u - p) * 8)
                    for n in range(2):
                        m = dve.tensor_tensor(x2[p][:, n * 512:(n + 1) * 512], Y[n][:, :], x[p][:, n * 512:(n + 1) * 512], ALU.add)
                    m.then_inc(e["x2_set"], 1)
                if end_:
                    dve.wait_ge(e["lg_ready"], t + 1)
                    dst = lg[:, bass.ds(t, 1), :].rearrange("p a c -> p (a c)")
                    dve.tensor_tensor(dst, lgp[:, 0:NG + NE], rb[:, :], ALU.add).then_inc(e["lg_set"], 1)

            begin(0, 0)
            dve.wait_ge(const, CONSTS)
            gate(0, 0)
            for i in range(KD):
                dve.wait_ge(e["w_high"], i + 1)
                dve.tensor_tensor(wl[:, i, :], wo[:, i, :], wh[:, i, :].bitcast(F32), ALU.subtract).then_inc(e["w_split"], 1)
            software_pipeline(dve, step)

        @block.gpsimd
        def _(pool):
            def split(p, t):
                for half in range(2):
                    ks = slice(4 * half, 4 * half + 4)
                    if half:
                        pool.wait_ge(e["mix_set"], t + 1)
                    else:
                        through_slot(pool, loaded[p], t, p, 48)
                        if not isinstance(t, int) or t >= 2:
                            pool.wait_ge(e["y_ready"], t - 1)
                    pool.sem_inc(e["splits_begun"], 1)
                    pool.tensor_copy(mh[p][:, ks, :], mixT[p][:, ks, :]).then_inc(e["m_high"], 1)
                    pool.wait_ge(e["m_high"], t * 2 + (half + 1))
                    pool.tensor_tensor(ml[p][:, ks, :], mixT[p][:, ks, :], mh[p][:, ks, :].bitcast(F32), ALU.subtract).then_inc(e["m_split"], 1)

            for p in range(2):
                split(p, p)
            with pool.Fori(1, NT // 2) as j:
                for p in range(2):
                    split(p, j * 2 + p)


def route(nc, k, lg, gate, slot, table, idx):
    with ExitStack() as ctx:
        b = Bufs(nc, ctx, "route_")
        S4, S8 = [P, NT, NG], [P, NT, EPG]
        desc, it128, itb = b.sb("desc", [P, EPG]), b.sb("it128", [P, NT]), b.sb("itb", [P, MAXB + 2])
        tok, itr = b.sb("tok", [P, 2, NT]), b.sb("itr", [P, P])
        mg, m1, m2 = (b.sb(n, [P, NT]) for n in ("mg", "m1", "m2"))
        t4, t8 = b.sb("t4", S4), b.sb("t8", S8)
        hg, h1, h2 = b.sb("hot_group", S4), b.sb("hot1", S8), b.sb("hot2", S8)
        mx4, eg4, sg = b.sb("mx4", S4), b.sb("eg4", S4), b.sb("sg", [P, NT])
        sel, es, ms = b.sb("sel", [P, NT, NG, EPG]), b.sb("es", S8), b.sb("ms", S8)
        dm, ratio, den = (b.sb(n, [P, NT]) for n in ("dm", "ratio", "den"))
        A = [b.sb(f"A{c}", [P, NT, NG, EPG]) for c in range(2)]
        both, pos, prod = b.sb("A_both", [P, NT, NE]), b.sb("pos", [P, NT, NE]), b.sb("prod", [P, NT, NE])
        off = b.sb("off", [P, NT + 1, NE])
        cmp = b.sb("cmp", [P, MAXB * NE])
        nb, cum = b.sb("nblk", [P, NE]), [b.sb(f"cum{i}", [P, NE]) for i in range(2)]
        bx = b.sb("block_expert", [P, MAXB])
        sf = [b.sb(f"slot_f{c}", [P, NT]) for c in range(2)]
        tf = b.sb("table_f", [P, 2 * MAXB + NE + 1])
        marked = b.sb("slot_tokens_f", [P, MAXB + 2])
        row_i = b.sb("slot_row_i", [P, 2, NT], I32)
        row, blk = ([b.sb(f"slot_{n}{c}", [P, NT]) for c in range(2)] for n in ("row", "block"))
        hot_row = [b.sb(f"hot_row{c}", [P, NT, P], F32R) for c in range(2)]
        hot_block = [b.sb(f"hot_block{c}", [P, NT, MAXB + 2]) for c in range(2)]
        marks = [b.sb(f"marks{c}", [P, NT, 2, MAXB + 2], F32R) for c in range(2)]
        H = NT // 2
        rank = [b.ps(f"rank{h}", [P, H, NE]) for h in range(2)]
        tot = [b.ps(f"tot{h}", [P, H, NE]) for h in range(2)]
        idp = b.ps("slot_tokens", [P, 2, MAXB + 2])
        dv, ac, pl, pe_s = b.sem("route_vector"), b.sem("route_scalar"), b.sem("route_pool"), b.sem("route_tensor")
        both_set, rows_set, hot_set, hot_blocks_set, placed = (b.sem("route_" + n) for n in
            ("both_set", "rows_set", "hot_set", "hot_blocks_set", "placed"))
        exps_in, dm_in = b.sem("route_exps_in"), b.sem("route_dm_in")
        block = ctx.enter_context(nc.Block())

        @block.gpsimd
        def _(pool):
            pool.iota(itr[:, :], pattern=[[1, P]], base=0, channel_multiplier=0, allow_small_or_imprecise_dtypes=True).then_inc(pl, 1)
            pool.iota(desc[:, :], pattern=[[-1, EPG]], base=EPG, channel_multiplier=0, allow_small_or_imprecise_dtypes=True).then_inc(pl, 1)
            pool.iota(it128[:, :], pattern=[[P, NT]], base=0, channel_multiplier=0, allow_small_or_imprecise_dtypes=True).then_inc(pl, 1)
            pool.iota(itb[:, :], pattern=[[1, MAXB + 2]], base=0, channel_multiplier=0, allow_small_or_imprecise_dtypes=True).then_inc(pl, 1)
            pool.iota(tok[:, 0, :], pattern=[[0, NT]], base=0, channel_multiplier=1, allow_small_or_imprecise_dtypes=True).then_inc(pl, 1)
            pool.iota(tok[:, 1, :], pattern=[[1, NT]], base=0, channel_multiplier=0, allow_small_or_imprecise_dtypes=True).then_inc(pl, 1)
            pool.wait_ge(pl, 6)
            for c in range(2):
                pool.wait_ge(hot_set, 2 * c + 1)
                for i in range(2):
                    pool.tensor_tensor(marks[c][:, :, i, :], hot_block[c][:, :, :], bcast(tok[:, i, :], MAXB + 2, 2), ALU.mult).then_inc(hot_blocks_set, 1)

        @block.scalar
        def _(act):
            act.wait_ge(exps_in, 1)
            act.activation(eg4[:, :, :], mx4[:, :, :], ACT.Exp).then_inc(ac, 1)
            act.wait_ge(dm_in, 1)
            act.activation(ratio[:, :], dm[:, :], ACT.Exp).then_inc(ac, 1)

        @block.tensor
        def _(pe):
            pe.wait_ge(both_set, 1)
            for h in range(2):
                pe.matmul(rank[h][:, :, :], k["lower"][:, :], both[:, h * H:(h + 1) * H, :], start=True, stop=True)
                m = pe.matmul(tot[h][:, :, :], k["ones"][:, :], both[:, h * H:(h + 1) * H, :], start=True, stop=True)
            m.then_inc(pe_s, 1)
            for c in range(2):
                pe.wait_ge(hot_set, 2 * c + 2)
                pe.wait_ge(hot_blocks_set, 2 * c + 2)
                for t in range(NT):
                    m = pe.matmul(idp[:, :, :], hot_row[c][:, t, :], marks[c][:, t, :, :], start=c + t == 0, stop=c == 1 and t == NT - 1)
            m.then_inc(placed, 1)

        @block.vector
        def _(dve):
            n = [0]

            def link(m):
                n[0] += 1
                m.then_inc(dv, 1)
                dve.wait_ge(dv, n[0])

            def first_max(v, w, top, scores, hot):
                link(dve.tensor_reduce(top[:, :], v, AX.X, ALU.max))
                link(dve.tensor_tensor(scores[:, :, :], v, bcast(top[:, :], w, 2), ALU.is_equal))
                link(dve.tensor_tensor(scores[:, :, :], scores[:, :, :], bcast(desc[:, EPG - w:EPG], NT, 1), ALU.mult))
                link(dve.tensor_reduce(sg[:, :], scores[:, :, :], AX.X, ALU.max))
                link(dve.tensor_tensor(hot[:, :, :], scores[:, :, :], bcast(sg[:, :], w, 2), ALU.is_equal))

            dve.wait_ge(pl, 6)
            groups = lg[:, :, 0:NG]
            first_max(groups, NG, mg, t4, hg)
            dve.tensor_tensor(mx4[:, :, :], groups, bcast(mg[:, :], NG, 2), ALU.subtract).then_inc(exps_in, 1)
            experts = lg[:, :, NG:NG + NE].rearrange("p t (g e) -> p t g e", g=NG)
            link(dve.tensor_tensor(sel[:, :, :, :], experts, bcast(hg[:, :, :], EPG, 3), ALU.mult))
            link(dve.tensor_reduce(es[:, :, :], sel[:, :, :, :].rearrange("p t g e -> p t e g"), AX.X, ALU.add))
            first_max(es[:, :, :], EPG, m1, t8, h1)
            link(dve.scalar_tensor_tensor(out=ms[:, :, :], in0=h1[:, :, :], scalar=-1e30, in1=es[:, :, :], op0=ALU.mult, op1=ALU.add))
            first_max(ms[:, :, :], EPG, m2, t8, h2)
            dve.tensor_tensor(dm[:, :], m2[:, :], m1[:, :], ALU.subtract).then_inc(dm_in, 1)
            for c, h in ((0, h1), (1, h2)):
                link(dve.tensor_tensor(A[c][:, :, :, :], bcast(hg[:, :, :], EPG, 3), bcast(h[:, :, :], NG, 2), ALU.mult))
            flat = [a[:, :, :, :].rearrange("p t g e -> p t (g e)") for a in A]
            dve.tensor_tensor(both[:, :, :], flat[0], flat[1], ALU.add).then_inc(both_set, 1)
            dve.wait_ge(ac, 2)
            link(dve.tensor_reduce(sg[:, :], eg4[:, :, :], AX.X, ALU.add))
            link(dve.tensor_scalar(den[:, :], ratio[:, :], 1.0, None, ALU.add))
            link(dve.tensor_tensor(den[:, :], den[:, :], sg[:, :], ALU.mult))
            link(dve.reciprocal(gate[:, 0, :], den[:, :]))
            link(dve.tensor_tensor(gate[:, 1, :], gate[:, 0, :], ratio[:, :], ALU.mult))
            link(dve.memset(off[:, 0, :], 0.0))
            dve.wait_ge(pe_s, 1)
            for t in range(NT):
                link(dve.tensor_tensor(off[:, t + 1, :], tot[t // H][:, t % H, :], off[:, t, :], ALU.add))
            for h in range(2):
                link(dve.tensor_tensor(pos[:, h * H:(h + 1) * H, :], rank[h][:, :, :], off[:, h * H:(h + 1) * H, :], ALU.add))
            blocks = cmp[:, 0:NE * NT].rearrange("p (e t) -> p e t", t=NT)
            link(dve.tensor_tensor(blocks, bcast(off[:, NT, :], NT, 2), bcast(it128[:, :], NE, 1), ALU.is_gt))
            link(dve.tensor_reduce(nb[:, :], blocks, AX.X, ALU.add))
            link(dve.tensor_copy(cum[0][:, :], nb[:, :]))
            for i in range(5):
                s, a, c = 1 << i, cum[i % 2], cum[1 - i % 2]
                link(dve.tensor_copy(c[:, 0:s], a[:, 0:s]))
                link(dve.tensor_tensor(c[:, s:NE], a[:, s:NE], a[:, 0:NE - s], ALU.add))
            end = cum[1]
            link(dve.tensor_tensor(cum[0][:, :], end[:, :], nb[:, :], ALU.subtract))
            link(dve.scalar_tensor_tensor(out=pos[:, :, :], in0=bcast(cum[0][:, :], NT, 1), scalar=float(P), in1=pos[:, :, :],
                                          op0=ALU.mult, op1=ALU.add))
            for c in range(2):
                link(dve.tensor_tensor(prod[:, :, :], flat[c], pos[:, :, :], ALU.mult))
                link(dve.tensor_reduce(sf[c][:, :], prod[:, :, :], AX.X, ALU.add))
            for c in range(2):
                link(dve.tensor_copy(slot[:, c, :], sf[c][:, :]))
                link(dve.tensor_single_scalar(row_i[:, c, :], slot[:, c, :], P - 1, ALU.bitwise_and))
                dve.tensor_copy(row[c][:, :], row_i[:, c, :]).then_inc(rows_set, 1)
            for c in range(2):
                dve.wait_ge(rows_set, c + 1)
                link(dve.tensor_tensor(blk[c][:, :], sf[c][:, :], row[c][:, :], ALU.subtract))
                link(dve.tensor_scalar(blk[c][:, :], blk[c][:, :], 1.0 / P, None, ALU.mult))
                dve.tensor_tensor(hot_block[c][:, :, :], bcast(itb[:, :], NT, 1), bcast(blk[c][:, :], MAXB + 2, 2), ALU.is_equal).then_inc(hot_set, 1)
                dve.tensor_tensor(hot_row[c][:, :, :], bcast(itr[:, :], NT, 1), bcast(row[c][:, :], P, 2), ALU.is_equal).then_inc(hot_set, 1)
            ends = cmp[:, :].rearrange("p (b e) -> p b e", e=NE)
            link(dve.tensor_tensor(ends, bcast(itb[:, 0:MAXB], NE, 2), bcast(end[:, :], MAXB, 1), ALU.is_ge))
            link(dve.tensor_reduce(bx[:, :], ends, AX.X, ALU.add))
            link(dve.tensor_scalar(tf[:, 0:MAXB], bx[:, :], float(NE - 1), None, ALU.min))
            link(dve.tensor_copy(table[:, 0:MAXB], tf[:, 0:MAXB]))
            link(dve.tensor_single_scalar(table[:, MAXB:2 * MAXB], table[:, 0:MAXB], 1, ALU.bitwise_and))
            link(dve.tensor_scalar(tf[:, 0:NE], end[:, :], 1.0, None, ALU.add))
            link(dve.tensor_copy(table[:, 2 * MAXB:2 * MAXB + NE], tf[:, 0:NE]))
            link(dve.tensor_copy(table[:, 2 * MAXB + NE:2 * MAXB + NE + 1], end[:, NE - 1:NE]))
            dve.wait_ge(placed, 1)
            link(dve.tensor_copy(marked[:, :], idp[:, 0, :]))
            link(dve.scalar_tensor_tensor(out=marked[:, :], in0=idp[:, 1, :], scalar=float(P), in1=marked[:, :], op0=ALU.mult, op1=ALU.add))
            dve.tensor_copy(idx[:, :], marked[:, :])


def experts(nc, k, dram, table, idx, xn_rows, y_rows):
    with ExitStack() as ctx:
        b = Bufs(nc, ctx, "experts_")
        pair = lambda name, shape, dt=F32: [b.sb(f"{name}{p}", shape, dt) for p in range(2)]

        whole, lows = over(nc, b, ("w1", "w3"), [P, 2, KD, FF])
        W = {n: (b.sb(f"{n}_high", [P, 2, KD, FF], F32R), low, w) for n, low, w in zip(("w1", "w3"), lows, whole)}
        raw, xl = over(nc, b, ("xT0", "xT1"), [P, KD, P])
        (w2_whole,), (w2_low,) = over(nc, b, ("w2",), [P, 2, FF // P, D])
        w2_high = b.sb("w2_high", [P, FF // P, D], F32R)
        ix, xg = pair("ix", [P, 1], I32), b.sb("xg", [P, D])
        xh = pair("xT_high", [P, KD, P], F32R)
        s, yo = b.sb("silu", [P, FF]), b.sb("yout", [P, D])
        h3 = yo[:, FF:2 * FF]
        (gT,), (gT_low,) = over(nc, b, ("gT",), [P, FF // P, P])
        gT_high = b.sb("gT_high", [P, FF // P, P], F32R)
        tX = [b.ps(f"xg_turned{n}", [P, 4, P]) for n in range(2)]
        H1, H3, tG = b.ps("h1", [P, FF]), b.ps("h3", [P, FF]), b.ps("g_turned", [P, FF // P, P])
        Y = [b.ps(f"ye{n}", [P, 512]) for n in range(2)]
        names = ("ix_set turned raw_set high_set low_set h1_ready h3_ready silu_set h3_set gated_set g_turned gT_set gT_high_set gT_low_set "
                 "y_ready y_set done split w2_split gathers_begun all_stored w_high_set w2_high_set pairs_through").split()
        e = {n: b.sem("moe_" + n) for n in names}
        gathered, y_free = b.sem("moe_gathered"), b.sem("moe_y_free")
        PARTS = [(n, q) for n in ("w1", "w3") for q in range(2)]
        KQ = KD // 2
        w_sem = [{n: b.sem(f"moe_{n[0]}_{n[1]}_{p}") for n in PARTS} for p in range(2)]
        w2_sem = [b.sem(f"moe_w2_{p}") for p in range(2)]
        emptied = b.sem("emptied")
        block = ctx.enter_context(nc.Block())
        NB = 2 * MAXB + NE
        PAIRS = (MAXB - 1) // 2

        def n_blocks(eng):
            return eng.value_load(table[0:1, NB:NB + 1], min_val=1, max_val=MAXB)

        def through_blocks(eng, n, step, and_then=None):
            step(0, 0, 0)
            with eng.Fori(0, PAIRS) as j:
                with eng.If(j * 2 + 1 < n):
                    step(1, j * 2 + 1, j)
                    step(0, j * 2 + 2, j + 1)
                if and_then is not None:
                    and_then(j)

        @block.sync
        def _(sp):
            def end_of(x):
                return sp.value_load(table[0:1, bass.ds(x + 2 * MAXB, 1)], min_val=1, max_val=MAXB + 1)

            def load_w13(p, x, parts=PARTS):
                for n, q in parts:
                    sp.dma_start(W[n][2][:, p, q * KQ:(q + 1) * KQ],
                                 dram[n][bass.ds(x, 1), q * KQ * P:(q + 1) * KQ * P, :].rearrange("a (k p) n -> p (a k) n", p=P)).then_inc(w_sem[p][n, q], 16)

            def load_w2(p, x):
                sp.dma_start(w2_whole[:, p], dram["w2"][bass.ds(x, 1)].rearrange("a (k p) n -> p (a k) n", p=P)).then_inc(w2_sem[p], 16)

            def step(p, x, j):
                sp.wait_ge(e["h3_ready"], end_of(x - 2))
                load_w13(p, x)
                if not (isinstance(x, int) and x < 3):
                    sp.wait_ge(e["done"], end_of(x - 3))
                load_w2(1 - p, x - 1)

            load_w13(0, 0, PARTS[0:2])
            sp.wait_ge(gathered, 16)
            load_w13(0, 0, PARTS[2:])
            load_w13(1, 1)
            load_w2(0, 0)
            for p in range(2):
                step(p, 2 + p, 1)
            with sp.Fori(2, NE // 2) as j:
                for p in range(2):
                    step(p, j * 2 + p, j)
            sp.wait_ge(e["done"], end_of(NE - 3))
            load_w2(1, NE - 1)

        @block.vector
        def _(dve):
            def split_w13(p, x, j):
                for i, (n, q) in enumerate(PARTS):
                    high, low, loaded = (t[:, p, q * KQ:(q + 1) * KQ, :] for t in W[n])
                    dve.wait_ge(w_sem[p][n, q], j * 16 + 16)
                    dve.tensor_copy(high, loaded).then_inc(e["w_high_set"], 1)
                    dve.wait_ge(e["w_high_set"], x * 4 + (i + 1))
                    m = dve.tensor_tensor(low, loaded, high.bitcast(F32), ALU.subtract)
                    if q:
                        m.then_inc(e["split"], 1)

            def split_w2(p, x, j):
                dve.wait_ge(w2_sem[p], j * 16 + 16)
                if not (isinstance(x, int) and x == 0):
                    last = dve.value_load(table[0:1, bass.ds(x + (2 * MAXB - 1), 1)], min_val=1, max_val=MAXB + 1)
                    dve.wait_ge(e["done"], last)
                for i in range(2):
                    cs = slice(2 * i, 2 * i + 2)
                    dve.tensor_copy(w2_high[:, cs], w2_whole[:, p, cs]).then_inc(e["w2_high_set"], 1)
                    dve.wait_ge(e["w2_high_set"], x * 2 + (i + 1))
                    m = dve.tensor_tensor(w2_low[:, p, cs], w2_whole[:, p, cs], w2_high[:, cs].bitcast(F32), ALU.subtract)
                m.then_inc(e["w2_split"], 1)

            def pair_of(j, more=True):
                split_w13(1, j * 2 + 1, j)
                split_w2(0, j * 2, j)
                if more:
                    split_w13(0, j * 2 + 2, j + 1)
                split_w2(1, j * 2 + 1, j)

            split_w13(0, 0, 0)
            pair_of(0)
            with dve.Fori(1, NE // 2 - 1) as j:
                pair_of(j)
            pair_of(NE // 2 - 1, more=False)

        @block.gpsimd
        def _(pool):
            def gather(p, blk):
                pool.tensor_copy(ix[p][:, :], idx[:, bass.ds(blk, 1)]).then_inc(e["ix_set"], 1)
                pool.wait_ge(e["ix_set"], blk + 1)
                pool.sem_inc(e["gathers_begun"], 1)
                pool.indirect_dma_start(out=xg[:, :], out_offset=None, in_=xn_rows[:, :],
                                        in_offset=bass.IndirectOffsetOnAxis(ap=ix[p][:, 0:1], axis=0)).then_inc(gathered, 16)

            def low(p, blk):
                pool.wait_ge(e["raw_set"], blk + 1)
                pool.wait_ge(e["high_set"], blk + 1)
                pool.tensor_tensor(xl[p][:, :, :], raw[p][:, :, :], xh[p][:, :, :].bitcast(F32), ALU.subtract).then_inc(e["low_set"], 1)

            def gated_low(blk):
                pool.wait_ge(e["gT_set"], blk + 1)
                pool.wait_ge(e["gT_high_set"], blk + 1)
                pool.tensor_tensor(gT_low[:, :, :], gT[:, :, :], gT_high[:, :, :].bitcast(F32), ALU.subtract).then_inc(e["gT_low_set"], 1)

            def step(p, blk, j):
                pool.wait_ge(e["turned"], blk + 2)
                gather(p, blk + 2)
                if not (isinstance(blk, int) and blk == 0):
                    gated_low(blk - 1)
                low(1 - p, blk + 1)
                pool.wait_ge(e["silu_set"], blk + 1)
                pool.wait_ge(e["h3_set"], blk + 1)
                pool.tensor_tensor(s[:, :], h3, s[:, :], ALU.mult).then_inc(e["gated_set"], 1)

            def empty_rows(j):
                with pool.If(j * -2 + (2 * PAIRS - 1) >= n):
                    dst = y_rows[bass.ds(j * (-2 * P) + (2 * PAIRS - 1) * P, 2 * P), :]
                    pool.dma_start(dst, xn_rows[0:2 * P, :]).then_inc(emptied, 16)
                    pool.wait_ge(emptied, j * 16 + 16)
                pool.sem_inc(e["pairs_through"], 1)

            n = n_blocks(pool)
            gather(0, 0)
            pool.wait_ge(e["turned"], 1)
            gather(1, 1)
            low(0, 0)
            through_blocks(pool, n, step, empty_rows)
            gated_low(n // 2 * 2)

        @block.tensor
        def _(pe):
            def turn(p, blk):
                pe.wait_ge(gathered, blk * 16 + 16)
                wait_if_any(pe, e["high_set"], blk)
                wait_if_any(pe, e["raw_set"], blk)
                for c in range(KD):
                    m = pe.transpose(tX[c // 4][:, c % 4, :], xg[:, c * P:(c + 1) * P], k["ident"][:, :])
                m.then_inc(e["turned"], 1)

            def hidden(name, out, p, half):
                for kt in range(KD):
                    high, low = (t[:, half, kt, :].rearrange("p a n -> p (a n)") for t in W[name][0:2])
                    for i, (x, w) in enumerate(((xh, high), (xh, low), (xl, high))):
                        m = pe.matmul(out[:, :], x[p][:, kt, :], w, start=kt == 0 and i == 0, stop=kt == KD - 1 and i == 2)
                return m

            def turn_gated(blk):
                pe.wait_ge(e["gated_set"], blk + 1)
                for c in range(FF // P):
                    m = pe.transpose(tG[:, c, :], s[:, c * P:(c + 1) * P], k["ident"][:, :])
                m.then_inc(e["g_turned"], 1)

            def output(blk):
                x = pe.value_load(table[0:1, bass.ds(blk, 1)], min_val=0, max_val=NE - 1)
                half = bass.ds(pe.value_load(table[0:1, bass.ds(blk + MAXB, 1)], min_val=0, max_val=1), 1)
                pe.wait_ge(e["w2_split"], x + 1)
                pe.wait_ge(e["gT_low_set"], blk + 1)
                wait_if_any(pe, e["y_set"], blk)
                for n in range(2):
                    for c in range(FF // P):
                        cols = slice(n * 512, (n + 1) * 512)
                        high, low = w2_high[:, c, cols], w2_low[:, half, c, cols].rearrange("p a n -> p (a n)")
                        for i, (g, w) in enumerate(((gT_high, high), (gT_high, low), (gT_low, high))):
                            m = pe.matmul(Y[n][:, :], g[:, c, :], w, start=c == 0 and i == 0, stop=c == FF // P - 1 and i == 2)
                    m.then_inc(e["done" if n else "y_ready"], 1)

            def step(p, blk, j):
                x = pe.value_load(table[0:1, bass.ds(blk, 1)], min_val=0, max_val=NE - 1)
                half = bass.ds(pe.value_load(table[0:1, bass.ds(blk + MAXB, 1)], min_val=0, max_val=1), 1)
                pe.wait_ge(e["low_set"], blk + 1)
                pe.wait_ge(e["split"], x * 2 + 1)
                wait_if_any(pe, e["silu_set"], blk)
                hidden("w1", H1, p, half).then_inc(e["h1_ready"], 1)
                first = isinstance(blk, int) and blk == 0
                if not first:
                    turn_gated(blk - 1)
                turn(1 - p, blk + 1)
                pe.wait_ge(e["split"], x * 2 + 2)
                wait_if_any(pe, e["h3_set"], blk)
                hidden("w3", H3, p, half).then_inc(e["h3_ready"], 1)
                if not first:
                    output(blk - 1)

            n = n_blocks(pe)
            for name in ("h3_ready", "done"):
                pe.sem_inc(e[name], 1)
            turn(0, 0)
            through_blocks(pe, n, step)
            last = n // 2 * 2
            turn_gated(last)
            output(last)

        @block.scalar
        def _(act):
            def turned(p, blk):
                act.wait_ge(e["turned"], blk + 1)
                for n in range(2):
                    m = act.activation(raw[p][:, 4 * n:4 * n + 4, :], tX[n][:, :, :], ACT.Copy)
                m.then_inc(e["raw_set"], 1)
                for n in range(2):
                    m = act.activation(xh[p][:, 4 * n:4 * n + 4, :], tX[n][:, :, :], ACT.Copy)
                m.then_inc(e["high_set"], 1)

            def turned_gate(blk):
                act.wait_ge(e["g_turned"], blk + 1)
                act.activation(gT[:, :, :], tG[:, :, :], ACT.Copy).then_inc(e["gT_set"], 1)
                act.activation(gT_high[:, :, :], tG[:, :, :], ACT.Copy).then_inc(e["gT_high_set"], 1)

            def output(blk):
                act.wait_ge(y_free, blk * 16 + 16)
                for c in range(2):
                    act.wait_ge(e["done" if c else "y_ready"], blk + (1 + c))
                    m = act.activation(yo[:, c * 512:(c + 1) * 512], Y[c][:, :], ACT.Copy)
                m.then_inc(e["y_set"], 1)
                act.wait_ge(e["y_set"], blk + 1)
                act.dma_start(y_rows[bass.ds(blk * P, P), :], yo[:, :]).then_inc(y_free, 16)

            def step(p, blk, j):
                act.wait_ge(e["h1_ready"], blk + 1)
                wait_if_any(act, e["g_turned"], blk)
                act.activation(s[:, :], H1[:, :], ACT.Silu).then_inc(e["silu_set"], 1)
                first = isinstance(blk, int) and blk == 0
                if not first:
                    turned_gate(blk - 1)
                turned(1 - p, blk + 1)
                act.wait_ge(y_free, 16 if first else blk * 16)
                act.wait_ge(e["h3_ready"], blk + 2)
                act.activation(h3, H3[:, :], ACT.Copy).then_inc(e["h3_set"], 1)
                if not first:
                    act.wait_ge(e["gated_set"], blk + 1)
                    output(blk - 1)

            n = n_blocks(act)
            act.dma_start(yo[0:1, :], dram["final_norm_g"].rearrange("(a n) -> a n", a=1)).then_inc(y_free, 16)
            turned(0, 0)
            through_blocks(act, n, step)
            turned_gate(n // 2 * 2)
            act.wait_ge(e["gated_set"], n // 2 * 2 + 1)
            output(n // 2 * 2)
            act.wait_ge(y_free, n // 2 * 32 + 32)
            act.sem_inc(e["all_stored"], 1)


def combine(nc, k, dram, gate, slot, x2_rows, y_rows, y):
    with ExitStack() as ctx:
        b = Bufs(nc, ctx, "combine_")
        U = 3
        ring = lambda name, shape, dt=F32: [b.sb(f"{name}{p}", shape, dt) for p in range(U)]
        gf, junk = b.sb("final_gain", [P, D]), b.sb("junk_f", [P, D])
        ix, x, out = ring("cix", [P, 2], I32), ring("cx", [P, D]), ring("out", [P, D])
        r = [ring(f"crow{c}", [P, D]) for c in range(2)]
        ss, rt, ri = ring("css", [P, 1]), ring("crt", [P, 1]), ring("cri", [P, 1])
        names = "ix_set gathers_begun sum1 sum2 squared rooted inverted out_set".split()
        e = {n: b.sem("fin_" + n) for n in names}
        const = b.sem("fin_const")
        x_ld = [b.sem(f"fin_x{p}") for p in range(U)]
        r_ld = [b.sem(f"fin_rows{p}") for p in range(U)]
        stored = [b.sem(f"fin_stored{p}") for p in range(U)]
        block = ctx.enter_context(nc.Block())

        def through_tiles(eng, first, last, step):
            with eng.Fori(first, last) as j:
                for p in range(U):
                    step(p, j, j * U + p)

        @block.sync
        def _(sp):
            def store(p, t):
                sp.wait_ge(e["out_set"], t + 1)
                sp.dma_start(y[bass.ds(t * P, P), :], out[p][:, :]).then_inc(stored[p], 16)

            def step(p, j, t):
                sp.wait_ge(e["out_set"], t - (U - 1))
                sp.dma_start(x[p][:, :], x2_rows[bass.ds(t * P, P), :]).then_inc(x_ld[p], 16)
                store(p, t - U)

            for p in range(U):
                sp.dma_start(x[p][:, :], x2_rows[p * P:(p + 1) * P, :]).then_inc(x_ld[p], 16)
            sp.dma_start(gf[:, :], dram["final_norm_g"].partition_broadcast(P)).then_inc(const, 16)
            through_tiles(sp, 1, NT // U, step)
            for p in range(U):
                store(p, NT - U + p)
            for p in range(U):
                sp.wait_ge(stored[p], 16 * NT // U)

        @block.gpsimd
        def _(pool):
            def rows(p, t):
                pool.tensor_copy(ix[p][:, :], slot[:, :, bass.ds(t, 1)].rearrange("p c a -> p (c a)")).then_inc(e["ix_set"], 1)
                pool.wait_ge(e["ix_set"], t + 1)
                pool.sem_inc(e["gathers_begun"], 1)
                for c in range(2):
                    pool.indirect_dma_start(out=r[c][p][:, :], out_offset=None, in_=y_rows[:, :],
                                            in_offset=bass.IndirectOffsetOnAxis(ap=ix[p][:, c:c + 1], axis=0)).then_inc(r_ld[p], 16)

            def step(p, j, t):
                pool.wait_ge(e["sum2"], t - (U - 1))
                rows(p, t)

            for p in range(U):
                rows(p, p)
            through_tiles(pool, 1, NT // U, step)

        @block.vector
        def _(dve):
            def sums(p, j, t):
                dve.wait_ge(x_ld[p], j * 16 + 16)
                dve.wait_ge(r_ld[p], j * 32 + 32)
                g = [gate[:, c, bass.ds(t, 1)] for c in range(2)]
                dve.scalar_tensor_tensor(out=x[p][:, :], in0=r[0][p][:, :], scalar=g[0], in1=x[p][:, :],
                                         op0=ALU.mult, op1=ALU.add).then_inc(e["sum1"], 1)
                dve.wait_ge(e["sum1"], t + 1)
                dve.scalar_tensor_tensor(out=x[p][:, :], in0=r[1][p][:, :], scalar=g[1], in1=x[p][:, :],
                                         op0=ALU.mult, op1=ALU.add).then_inc(e["sum2"], 1)

            def norm(p, j, t, first=False):
                dve.wait_ge(e["rooted"], t + 1)
                dve.reciprocal(ri[p][:, :], rt[p][:, :]).then_inc(e["inverted"], 1)
                dve.wait_ge(e["inverted"], t + 1)
                if not first:
                    dve.wait_ge(stored[p], j * 16)
                dve.scalar_tensor_tensor(out=out[p][:, :], in0=x[p][:, :], scalar=ri[p][:, :], in1=gf[:, :],
                                         op0=ALU.mult, op1=ALU.mult).then_inc(e["out_set"], 1)

            def step(p, j, t):
                sums(p, j, t)
                norm((p - 1) % U, j if p else j - 1, t - 1, isinstance(t, int) and t <= U)

            dve.wait_ge(const, 16)
            sums(0, 0, 0)
            for t in range(1, U + 1):
                step(t % U, t // U, t)
            for t in range(U + 1, 2 * U):
                step(t % U, t // U, t)
            through_tiles(dve, 2, NT // U, step)
            norm(U - 1, NT // U - 1, NT - 1)

        @block.scalar
        def _(act):
            def step(p, j, t):
                act.wait_ge(e["sum2"], t + 1)
                act.activation(junk[:, :], x[p][:, :], ACT.Square, accum_out=ss[p][:, :]).then_inc(e["squared"], 1)
                act.wait_ge(e["squared"], t + 1)
                act.activation(rt[p][:, :], ss[p][:, :], ACT.Sqrt, bias=k["eps"][:, :], scale=1.0 / D).then_inc(e["rooted"], 1)

            through_tiles(act, 0, NT // U, step)


def encoder(nc, dram, y):
    with ExitStack() as ctx:
        b = Bufs(nc, ctx)
        feat = nc.dram_tensor("feat", (20, P, T), F32).ap()
        ab_rows = nc.dram_tensor("ab_rows", (16, T), F32).ap()
        x2_rows = nc.dram_tensor("x2_rows", (T, D), F32).ap()
        xn_rows = nc.dram_tensor("xn_rows", (T, D), F32).ap()
        y_rows = nc.dram_tensor("y_rows", (SLOTS, D), F32).ap()
        k = {"ident": b.sb("ident", [P, P]), "eps": b.sb("eps", [P, 1])}
        gate, slot = b.sb("gate", [P, 2, NT]), b.sb("slot", [P, 2, NT], I32)
        table, idx = b.sb("table", [P, 2 * MAXB + NE + 1], I32), b.sb("idx", [P, MAXB + 2], I32)
        until_routed = ctx.enter_context(ExitStack())
        u = Bufs(nc, until_routed)
        k["ones"], k["lower"], lg = u.sb("ones", [P, P]), u.sb("lower", [P, P]), u.sb("lg", [P, NT, NG + NE])
        with ExitStack() as mixers:
            m = Bufs(nc, mixers)
            k.update({
                "group": m.sb("group", [P, P]), "tri": m.sb("tri", [P, 2, P]), "neg": m.sb("neg", [P, 2, P]),
                "lvl": m.sb("lvl", [P, 2, LEVELS, P]),
                "cw_mix": m.sb("cw_mix", [P, CONV_TILES, 3]), "cg_mix": m.sb("cg_mix", [P, CONV_TILES]),
                "cw_qkv": m.sb("cw_qkv", [P, 3 * HEADS, 3]), "alog": m.sb("alog", [P, 2 * HEADS]),
                "dtb": m.sb("dtb", [P, 2 * HEADS]), "eps128": m.sb("eps128", [P, 1]), "one": m.sb("one", [P, 1]),
            })
            with ExitStack() as c2:
                hT = [Bufs(nc, c2).sb(f"hT_{part}", [P, KD, T], F32R) for part in ("high", "low")]
                with ExitStack() as c3:
                    k["g1"] = Bufs(nc, c3).sb("g1", [P, D])
                    constants(nc, k, dram)
                    with nc.cleanup_on_exit():
                        normalise(nc, k, dram, hT)
                with nc.cleanup_on_exit():
                    project(nc, k, dram, hT, feat, ab_rows)
            gates = m.sb("gates", [P, 2, NT, 5 * HEADS])
            with ExitStack() as c2:
                O = Bufs(nc, c2).sb("O", [P, NT, HEADS * P])
                decays(nc, k, ab_rows, gates, O)
                with nc.cleanup_on_exit():
                    delta(nc, k, gates, feat, O)
                with nc.cleanup_on_exit():
                    output(nc, k, dram, feat, O, lg, x2_rows, xn_rows)
        route(nc, k, lg, gate, slot, table, idx)
        until_routed.close()
        experts(nc, k, dram, table, idx, xn_rows, y_rows)
        combine(nc, k, dram, gate, slot, x2_rows, y_rows, y)


def lay_out(inputs):
    a = {name: np.asarray(v) for name, v in inputs.items()}
    w_in = a["w_in"][0]
    start = {"b": 0, "c": 512, "h": 1024, "q": 1536, "k": 2048, "v": 2560, "z": 3072}
    tiles = [w_in[:, start[job] + g * P:start[job] + (g + 1) * P] for g in range(HEADS) for job in JOBS]
    by_tap = lambda w: w.reshape(3, -1, P).transpose(2, 1, 0)
    return {
        "x": np.concatenate([a["x_prompt"][0], a["x_sample"][0]], 0),
        "w_tiles": np.stack(tiles).reshape(len(tiles), KD, P, P).transpose(0, 2, 1, 3),
        "w_ab": w_in[:, 3584:].reshape(KD, P, 4 * HEADS).transpose(1, 0, 2),
        "norm1_g": a["norm1_g"][0],
        "conv_a_w": by_tap(a["conv_a_w"][0]),
        "conv_a_norm_g": a["conv_a_norm_g"][0].reshape(CONV_TILES, P).T,
        "dn_conv_w": by_tap(a["dn_conv_w"][0]),
        "dn_a_log": a["dn_a_log"][0].reshape(-1),
        "dn_dt_bias": a["dn_dt_bias"][0].reshape(-1),
        "dn_norm_g": a["dn_norm_g"][0].reshape(P, 1),
        "w_o": a["w_o"][0],
        "norm2_g": a["norm2_g"][0],
        "router_w": np.concatenate([a["router_group_w"][0], a["router_expert_w"][0]], 1),
        "router_b": np.concatenate([a["router_group_b"][0], a["router_expert_b"][0]]),
        "w1": a["w1"][0], "w3": a["w3"][0], "w2": a["w2"][0],
        "final_norm_g": a["final_norm_g"],
    }


def kernel(**inputs):
    import concourse.bacc as bacc
    from concourse.bass_utils import run_bass_kernel_spmd

    nc = bacc.Bacc("TRN2", target_bir_lowering=False, num_devices=1)
    arrays, dram = {}, {}
    for name, array in lay_out(inputs).items():
        arrays[f"in_{name}_dram"] = np.ascontiguousarray(array)
        dram[name] = nc.dram_tensor(f"in_{name}_dram", array.shape, mybir.dt.from_np(array.dtype), kind="ExternalInput").ap()
    y = nc.dram_tensor("out_0_dram", (T, D), F32, kind="ExternalOutput").ap()
    encoder(nc, dram, y)
    r = run_bass_kernel_spmd(nc, [arrays], core_ids=[0])
    rows = r.results[0]["out_0_dram"]
    return rows[None, :LONG], rows[None, LONG:]
```
